# Optimizing a Trainium2 kernel written in Bass

```python
import math
import jax, jax.numpy as jnp
from jax import lax
import numpy as np

D_MODEL = 1024
BATCH = 1
SEQ = 128
DEPTH = 2
DEC_BATCH = 1
DEC_SEQ = 512
PAST_LEN = 128

GRID_W = 64
Q_BLOCK = 128
ROPE_THETA = 10000.0
DIFF_HEADS = 4
DIFF_HEAD_DIM = 64
DIFF_V_DIM = 2 * DIFF_HEAD_DIM
DIFF_QK_WIDTH = DIFF_HEADS * 2 * DIFF_HEAD_DIM
DIFF_WIDTH = DIFF_HEADS * DIFF_V_DIM
GQA_HEADS = 8
GQA_KV_HEADS = 2
GQA_HEAD_DIM = 64
GQA_GROUP = GQA_HEADS // GQA_KV_HEADS
GQA_WIDTH = GQA_HEADS * GQA_HEAD_DIM
GQA_KV_WIDTH = GQA_KV_HEADS * GQA_HEAD_DIM
FOURIER_GROUPS = 4
FOURIER_GROUP_DIM = 128
FOURIER_WIDTH = FOURIER_GROUPS * FOURIER_GROUP_DIM
N_BRANCH = 3
BRANCH_WIDTH = 512
IN_SIZES = (DIFF_QK_WIDTH, DIFF_QK_WIDTH, DIFF_WIDTH, GQA_WIDTH, GQA_KV_WIDTH, GQA_KV_WIDTH,
            FOURIER_WIDTH, N_BRANCH * D_MODEL)
IN_COLS = sum(IN_SIZES)
PEER_HEADS = 8
PEER_KEYS = 128
PEER_EXPERTS = PEER_KEYS * PEER_KEYS
PEER_QUERY_DIM = 128
PEER_HALF = PEER_QUERY_DIM // 2
PEER_TOPK = 16
PEER_CHUNK = 128
DEEPNORM_ALPHA = (2 * DEPTH) ** 0.25
DEEPNORM_BETA = (8 * DEPTH) ** -0.25
LN_EPS = 1e-6

kernel_name = 'hybrid_diffusion_prefix_trunk_step'

def layer_norm(x, g=None, b=None):
    xf = x.astype(jnp.float32)
    mu = jnp.mean(xf, -1, keepdims=True)
    xc = xf - mu
    y = xc * lax.rsqrt(jnp.mean(xc * xc, -1, keepdims=True) + LN_EPS)
    if g is not None:
        y = y * g.astype(jnp.float32) + b.astype(jnp.float32)
    return y.astype(x.dtype)

def rms_norm(x, g):
    xf = x.astype(jnp.float32)
    y = xf * lax.rsqrt(jnp.mean(xf * xf, -1, keepdims=True) + LN_EPS) * g.astype(jnp.float32)
    return y.astype(x.dtype)

def axial_rope(n_tokens, dim):
    n_rows = n_tokens // GRID_W
    row = jnp.repeat(jnp.arange(n_rows), GRID_W).astype(jnp.float32)
    col = jnp.tile(jnp.arange(GRID_W), n_rows).astype(jnp.float32)
    n_freq = dim // 4
    freqs = ROPE_THETA ** (-jnp.arange(n_freq, dtype=jnp.float32) / n_freq)
    ang = jnp.concatenate([row[:, None] * freqs, col[:, None] * freqs], -1)
    return jnp.cos(ang), jnp.sin(ang)

def apply_rope(x, cos, sin):
    xp = x.astype(jnp.float32).reshape(x.shape[:-1] + (x.shape[-1] // 2, 2))
    xe, xo = xp[..., 0], xp[..., 1]
    c, s = cos[None, :, None, :], sin[None, :, None, :]
    out = jnp.stack([xe * c - xo * s, xe * s + xo * c], -1).reshape(x.shape)
    return out.astype(x.dtype)

def sweep_query_blocks(block_fn, q):
    b, s = q.shape[0], q.shape[1]
    nb = s // Q_BLOCK
    qb = jnp.moveaxis(q.reshape((b, nb, Q_BLOCK) + q.shape[2:]), 1, 0)
    out = jnp.moveaxis(lax.map(block_fn, qb), 0, 1)
    return out.reshape((b, s) + out.shape[3:])

def diff_attention(q, k, v, lam):
    scale = DIFF_HEAD_DIM ** -0.5
    def block(qb):
        s = jnp.einsum('bqhmd,bkhmd->bhmqk', qb, k).astype(jnp.float32) * scale
        a = jax.nn.softmax(s, axis=-1)
        w = (a[:, :, 0] - lam * a[:, :, 1]).astype(v.dtype)
        return jnp.einsum('bhqk,bkhd->bqhd', w, v)
    return sweep_query_blocks(block, q)

def gqa_attention(q, k, v):
    scale = GQA_HEAD_DIM ** -0.5
    def block(qb):
        s = jnp.einsum('bqhgd,bkhd->bhgqk', qb, k).astype(jnp.float32) * scale
        a = jax.nn.softmax(s, axis=-1).astype(v.dtype)
        return jnp.einsum('bhgqk,bkhd->bqhgd', a, v)
    return sweep_query_blocks(block, q)

def fourier_mix(z):
    f = jnp.fft.fft2(z.astype(jnp.float32), axes=(1, 3), norm='ortho')
    return jnp.real(f).astype(z.dtype)

def token_mixer(h, lp, rope, ctx_kv):
    b, s, _ = h.shape
    z = h @ lp['w_in']
    splits = np.cumsum(IN_SIZES)[:-1].tolist()
    dq, dk, dv, gq, gk, gv, fz, gz = jnp.split(z, splits, axis=-1)
    dq = dq.reshape(b, s, DIFF_HEADS, 2, DIFF_HEAD_DIM)
    dk = dk.reshape(b, s, DIFF_HEADS, 2 * DIFF_HEAD_DIM)
    dv = dv.reshape(b, s, DIFF_HEADS, DIFF_V_DIM)
    gq = rms_norm(gq.reshape(b, s, GQA_KV_HEADS, GQA_GROUP, GQA_HEAD_DIM), lp['q_norm_g'])
    gk = rms_norm(gk.reshape(b, s, GQA_KV_HEADS, GQA_HEAD_DIM), lp['k_norm_g'])
    gv = gv.reshape(b, s, GQA_KV_HEADS, GQA_HEAD_DIM)
    own_kv = (dk, dv, gk, gv)

    dk_att = dk.reshape(b, s, DIFF_HEADS, 2, DIFF_HEAD_DIM)
    gk_att = gk
    if rope is not None:
        cos, sin = rope
        dq = apply_rope(dq.reshape(b, s, 2 * DIFF_HEADS, DIFF_HEAD_DIM), cos, sin).reshape(dq.shape)
        dk_att = apply_rope(dk_att.reshape(b, s, 2 * DIFF_HEADS, DIFF_HEAD_DIM), cos, sin).reshape(dk_att.shape)
        gq = apply_rope(gq.reshape(b, s, GQA_HEADS, GQA_HEAD_DIM), cos, sin).reshape(gq.shape)
        gk_att = apply_rope(gk, cos, sin)
    dv_att, gv_att = dv, gv
    if ctx_kv is not None:
        cdk, cdv, cgk, cgv = ctx_kv
        p = cdk.shape[1]
        dk_att = jnp.concatenate([dk_att, cdk.reshape(b, p, DIFF_HEADS, 2, DIFF_HEAD_DIM)], 1)
        dv_att = jnp.concatenate([dv_att, cdv], 1)
        gk_att = jnp.concatenate([gk_att, cgk], 1)
        gv_att = jnp.concatenate([gv_att, cgv], 1)

    lam_init = lp['lam_init']
    lam_vec = lp['diff_lam'].astype(jnp.float32)
    lam = (jnp.exp(jnp.sum(lam_vec[0] * lam_vec[1])) - jnp.exp(jnp.sum(lam_vec[2] * lam_vec[3]))
           + lam_init)
    d_o = diff_attention(dq, dk_att, dv_att, lam)
    d_o = (rms_norm(d_o, lp['diff_norm_g']) * (1.0 - lam_init)).reshape(b, s, DIFF_WIDTH)
    g_o = gqa_attention(gq, gk_att, gv_att).reshape(b, s, GQA_WIDTH)
    f_o = fourier_mix(fz.reshape(b, s, FOURIER_GROUPS, FOURIER_GROUP_DIM)).reshape(b, s, FOURIER_WIDTH)

    branches = jnp.stack([d_o, g_o, f_o], axis=2)
    y = jnp.einsum('bsnc,ncd->bsnd', branches, lp['w_branch'])
    gates = jax.nn.sigmoid(gz.reshape(b, s, N_BRANCH, D_MODEL))
    out = jnp.sum(gates * y, axis=2) @ lp['w_out']
    return out, own_kv

def peer_ffn(h, lp):
    b, s, d = h.shape
    t = b * s
    x = h.reshape(t, d)
    q = (x @ lp['peer_wq']).reshape(t, PEER_HEADS, 2, PEER_HALF)
    sc = jnp.einsum('thpd,hpnd->thpn', q, lp['peer_subkeys']).astype(jnp.float32)
    sv, si = lax.top_k(sc, PEER_TOPK)
    cand = (sv[:, :, 0, :, None] + sv[:, :, 1, None, :]).reshape(t, PEER_HEADS, PEER_TOPK * PEER_TOPK)
    cidx = (si[:, :, 0, :, None] * PEER_KEYS + si[:, :, 1, None, :]).reshape(t, PEER_HEADS, PEER_TOPK * PEER_TOPK)
    top_v, top_p = lax.top_k(cand, PEER_TOPK)
    experts = jnp.take_along_axis(cidx, top_p, axis=-1)
    gates = jax.nn.softmax(top_v, axis=-1).astype(h.dtype)
    u_tab, v_tab = lp['peer_u'], lp['peer_v']

    def chunk(args):
        xc, ec, gc = args
        act = jax.nn.gelu(jnp.einsum('cd,chkd->chk', xc, u_tab[ec]), approximate=False)
        return jnp.einsum('chk,chkd->cd', gc * act, v_tab[ec])

    n = t // PEER_CHUNK
    out = lax.map(chunk, (x.reshape(n, PEER_CHUNK, d),
                          experts.reshape(n, PEER_CHUNK, PEER_HEADS, PEER_TOPK),
                          gates.reshape(n, PEER_CHUNK, PEER_HEADS, PEER_TOPK)))
    return out.reshape(b, s, d)

def trunk_layer(x, mod, lp, rope, ctx_kv):
    sh1, sc1, g1, sh2, sc2, g2 = jnp.split(mod, 6, axis=-1)
    h = layer_norm(x) * (1.0 + sc1) + sh1
    mix, own_kv = token_mixer(h, lp, rope, ctx_kv)
    x = layer_norm(DEEPNORM_ALPHA * x + g1 * mix, lp['ln_g'][0], lp['ln_b'][0])
    h = layer_norm(x) * (1.0 + sc2) + sh2
    x = layer_norm(DEEPNORM_ALPHA * x + g2 * peer_ffn(h, lp), lp['ln_g'][1], lp['ln_b'][1])
    return x, own_kv

def setup_inputs(seed: int = 0) -> dict:
    key = jax.random.key(seed)
    ks = jax.random.split(key, 24)
    def nrm(k, shape, scale):
        return jax.random.normal(k, shape, jnp.float32) * scale
    d = D_MODEL
    return {
        'x_prompt': nrm(ks[0], (BATCH, SEQ, d), 1.0),
        'x_sample': nrm(ks[1], (DEC_BATCH, DEC_SEQ, d), 1.0),
        'cache_diff_k': nrm(ks[2], (DEC_BATCH, DEPTH, PAST_LEN, DIFF_HEADS, 2 * DIFF_HEAD_DIM), 1.0),
        'cache_diff_v': nrm(ks[3], (DEC_BATCH, DEPTH, PAST_LEN, DIFF_HEADS, DIFF_V_DIM), 1.0),
        'cache_gqa_k': nrm(ks[4], (DEC_BATCH, DEPTH, PAST_LEN, GQA_KV_HEADS, GQA_HEAD_DIM), 1.0),
        'cache_gqa_v': nrm(ks[5], (DEC_BATCH, DEPTH, PAST_LEN, GQA_KV_HEADS, GQA_HEAD_DIM), 1.0),
        'c': nrm(ks[6], (DEC_BATCH, d), 1.0),
        'c_ctx': nrm(ks[7], (d,), 1.0),
        'w_mod': nrm(ks[8], (DEPTH, d, 6 * d), 0.5 * d ** -0.5),
        'b_mod': nrm(ks[9], (DEPTH, 6 * d), 0.01),
        'w_in': nrm(ks[10], (DEPTH, d, IN_COLS), d ** -0.5),
        'diff_lam': nrm(ks[11], (DEPTH, 4, DIFF_HEAD_DIM), 0.1),
        'diff_norm_g': 1.0 + nrm(ks[12], (DEPTH, DIFF_V_DIM), 0.01),
        'q_norm_g': 1.0 + nrm(ks[13], (DEPTH, GQA_HEAD_DIM), 0.01),
        'k_norm_g': 1.0 + nrm(ks[14], (DEPTH, GQA_HEAD_DIM), 0.01),
        'w_branch': nrm(ks[15], (DEPTH, N_BRANCH, BRANCH_WIDTH, d), DEEPNORM_BETA * BRANCH_WIDTH ** -0.5),
        'w_out': nrm(ks[16], (DEPTH, d, d), DEEPNORM_BETA * d ** -0.5),
        'ln_g': 1.0 + nrm(ks[17], (DEPTH, 2, d), 0.01),
        'ln_b': nrm(ks[18], (DEPTH, 2, d), 0.01),
        'peer_wq': nrm(ks[19], (DEPTH, d, PEER_HEADS * PEER_QUERY_DIM), d ** -0.5),
        'peer_subkeys': nrm(ks[20], (DEPTH, PEER_HEADS, 2, PEER_KEYS, PEER_HALF), PEER_HALF ** -0.5),
        'peer_u': nrm(ks[21], (DEPTH, PEER_EXPERTS, d), d ** -0.5),
        'peer_v': nrm(ks[22], (DEPTH, PEER_EXPERTS, d), DEEPNORM_BETA),
    }

def reference(x_prompt, x_sample, cache_diff_k, cache_diff_v, cache_gqa_k, cache_gqa_v, c, c_ctx,
              w_mod, b_mod, w_in, diff_lam, diff_norm_g, q_norm_g, k_norm_g, w_branch, w_out,
              ln_g, ln_b, peer_wq, peer_subkeys, peer_u, peer_v):
    def layer_params(l):
        return {'w_in': w_in[l], 'diff_lam': diff_lam[l], 'diff_norm_g': diff_norm_g[l],
                'q_norm_g': q_norm_g[l], 'k_norm_g': k_norm_g[l], 'w_branch': w_branch[l],
                'w_out': w_out[l], 'ln_g': ln_g[l], 'ln_b': ln_b[l], 'peer_wq': peer_wq[l],
                'peer_subkeys': peer_subkeys[l], 'peer_u': peer_u[l], 'peer_v': peer_v[l],
                'lam_init': 0.8 - 0.6 * math.exp(-0.3 * l)}

    xp = x_prompt
    dk_list, dv_list, gk_list, gv_list = [], [], [], []
    for l in range(DEPTH):
        lp = layer_params(l)
        mod = (jax.nn.silu(c_ctx) @ w_mod[l] + b_mod[l])[None, None, :]
        xp, (dk, dv, gk, gv) = trunk_layer(xp, mod, lp, None, None)
        dk_list.append(dk); dv_list.append(dv); gk_list.append(gk); gv_list.append(gv)
    new_diff_k = jnp.stack(dk_list, axis=1)
    new_diff_v = jnp.stack(dv_list, axis=1)
    new_gqa_k = jnp.stack(gk_list, axis=1)
    new_gqa_v = jnp.stack(gv_list, axis=1)

    rope = axial_rope(x_sample.shape[1], DIFF_HEAD_DIM)
    xs = x_sample
    for l in range(DEPTH):
        lp = layer_params(l)
        mod = (jax.nn.silu(c) @ w_mod[l] + b_mod[l])[:, None, :]
        ctx_kv = (cache_diff_k[:, l], cache_diff_v[:, l], cache_gqa_k[:, l], cache_gqa_v[:, l])
        xs, _ = trunk_layer(xs, mod, lp, rope, ctx_kv)

    return (xp, xs, new_diff_k, new_diff_v, new_gqa_k, new_gqa_v)


_drawn_inputs = setup_inputs


def setup_inputs(seed=0):
    import zlib

    import numpy as np

    out = dict(_drawn_inputs(seed))
    spreads = {}
    factors = {'cache_diff_k': 7.599,
     'cache_diff_v': 7.265,
     'cache_gqa_k': 8.0,
     'cache_gqa_v': 8.0,
     'b_mod': 3.993,
     'diff_lam': 8.0,
     'diff_norm_g': 8.0,
     'q_norm_g': 8.0,
     'k_norm_g': 5.68}
    for name, (base, spread) in spreads.items():
        noise = np.random.default_rng([zlib.crc32(name.encode()), seed]).standard_normal(out[name].shape)
        drawn = base * np.exp(spread * noise) if base else spread * noise
        out[name] = __import__('jax').numpy.asarray(drawn.astype(out[name].dtype))
    for name, factor in factors.items():
        out[name] = (out[name] * factor).astype(out[name].dtype)
    return out
```

```python
from contextlib import ExitStack

import concourse.bass as bass
from concourse import mybir
from concourse.alu_op_type import AluOpType as ALU

F32 = mybir.dt.float32
F32R = mybir.dt.float32r
U32 = mybir.dt.uint32
ACT = mybir.ActivationFunctionType
AX = mybir.AxisListType

P = 128
D = 1024
KC = D // P
LAYERS = 2
NT = 5
T = NT * P
TH = T // 2
HEADS = 8
TOPK = 16
KEYS = 128
ALPHA = float((2 * LAYERS) ** 0.25)
EPS = 1e-6
SCALE = 64.0 ** -0.5
LOWEST = -3.0e38

RING = 4
SLOT = 2048
MOD, GQ, KV, DQ, DK, DV, FZ, DFT = 0, 24, 26, 27, 29, 31, 33, 35
MERGE, OUT, WQ, SUB, PEER = 37, 55, 59, 63, 64
NB = KEYS // 2
PER_LAYER = PEER + 2 * NB
TURNS = PER_LAYER // RING

N_STD = 6
N_MOD = 24
N_HT = 20
N_Z = 55
N_BLK = 4
N_TR = 18
N_F = 5
UNITS = 8
N_UNIT = NT * UNITS
N_BR = 10
N_MG = 24
N_OUT = 20
N_Q = 8
QUADS = P // 4
N_QUAD = NT * QUADS
N_W = 2 * NB
N_SPLIT = 2 * NB
N_V = 10 * NB
PARAM_DMAS = 5

C_ID, C_IOTA, C_COS, C_SIN, C_NSIN, C_ROPEC, C_ROPES, C_LAM = 0, 128, 256, 384, 512, 640, 768, 896
NCONST = 900


def layer_at(l, per_layer, n):
    return l * per_layer + n


def trunk(nc, weights, consts, x_in, cond, bcol, brow, rows, lnrows, cache_k, cache_v,
          y, new_dk, new_dv, new_gk, new_gv, gate_matrix):
    ctx = ExitStack()
    with ctx:
        def sem(name):
            return ctx.enter_context(nc.semaphore(name))

        slab_floats = 53200
        slab_at = -(-nc.sbuf_base // 32) * 32
        ctx.enter_context(nc.sbuf_tensor("slab", [P, slab_floats], F32))

        def at(name, shape, offset, dt=F32):
            size = 1
            for s in shape:
                size *= s
            assert offset + size <= slab_floats, (name, offset, size)
            t = nc.alloc_sbuf_tensor_at(name, [P] + list(shape), dt, offset=slab_at + 4 * offset)
            return t, offset + -(-size // 8) * 8

        o = 0
        const, o = at("const", [NCONST], o)
        row, o = at("row", [512], o)
        bc, o = at("bc", [48], o)
        modc, o = at("modc", [48, 2], o)
        cnd, o = at("cnd", [KC, 2], o)
        cnds, o = at("cnds", [KC, 2], o)
        stats, o = at("stats", [NT, 2, 6], o)
        mv, o = at("mv", [NT, 2], o)
        var, o = at("var", [64], o)
        std, o = at("std", [64], o)
        rstd, o = at("rstd", [64], o)
        lamw, o = at("lamw", [16], o)
        smx, o = at("smx", [2, 2], o)
        nbias, o = at("nbias", [2, 2], o)
        rsum, o = at("rsum", [2, 2], o)
        rinv, o = at("rinv", [2, 2], o)
        rneg, o = at("rneg", [2], o)
        ring_at = o
        ring, o = at("ring", [RING, SLOT], o)
        ht_at = o
        hT, o = at("hT", [KC, T], o)
        x, o = at("x", [NT, D], o)
        gates, o = at("gates", [2, 2, D], o)
        arena = o

        z_at = o
        z, o = at("z", [2, NT, 512], o)
        zk, o = at("zk", [NT, P], o)
        q_at = o
        qT, o = at("qT", [8, T], o)
        kT, o = at("kT", [5, 768], o)
        v_at = o
        V, o = at("V", [6, 640], o)
        fT, o = at("fT", [4, T], o)
        ck_at = o
        ckb, _ = at("ckb", [640], ck_at)
        qcur, o = at("qcur", [8, P], ck_at)
        tmp_at = o
        cb, t = at("cb", [2, KC, P], tmp_at)
        brw, t = at("brw", [2048], t)
        lamp, _ = at("lamp", [2, 64], t)
        xn, _ = at("xn", [2, D], tmp_at)
        sq, _ = at("sq", [2560], tmp_at)
        rot, _ = at("rot", [4, 1024], tmp_at)
        acs, _ = at("acs", [2, 2, 512], tmp_at)
        prob, t = at("prob", [2, 2, 640], tmp_at)
        wd, t = at("wd", [2, 640], t)
        pT, t = at("pT", [2, 10, P], t)
        o = t
        sg, t = at("sg", [2, T], tmp_at)
        mtmp, _ = at("mtmp", [T], t)
        otmp, _ = at("otmp", [2, 256], tmp_at)
        oall, _ = at("oall", [NT, D], z_at)
        mT, _ = at("mT", [KC, T], z_at)
        brT, _ = at("brT", [8, T], q_at)
        lnr, _ = at("lnr", [2, D], v_at)

        o = arena
        stg, o = at("stg", [2, NB, 2, 64], o)
        xn2, _ = at("xn2", [2, D], arena)
        qT2, o = at("qT2", [8, T], o)
        w_at = o
        work, o = at("work", [16, P], w_at)
        ohA, t = at("ohA", [8, P], w_at)
        ohB, t = at("ohB", [8, P], t)
        qcur2, _ = at("qcur2", [8, P], o)
        cand, o = at("cand", [8, 256], o)
        sv, o = at("sv", [16, TOPK], o)
        si, o = at("si", [16, TOPK], o, U32)
        sif, o = at("sif", [16, TOPK], o)
        pv, o = at("pv", [8, TOPK], o)
        pi, o = at("pi", [8, TOPK], o, U32)
        pii, o = at("pii", [2, P], o, U32)
        pif, o = at("pif", [2, P], o)
        idx, o = at("idx", [3, P], o)
        idxT, o = at("idxT", [3, P], o)
        pw, o = at("pw", [8, TOPK], o)
        pm, o = at("pm", [16], o)

        o = arena
        ring_lo = at("ring_lo", [RING, SLOT], ring_at, F32R)[0]
        hT_lo = at("hT_lo", [KC, T], ht_at, F32R)[0]
        hi_at = o
        ring_hi, o = at("ring_hi", [RING, SLOT], o, F32R)
        hT_hi, o = at("hT_hi", [KC, T], o, F32R)
        acc, o = at("acc", [NT, D], o)
        W_hi, o = at("W_hi", [2, 2, T], o, F32R)
        W_lo, o = at("W_lo", [2, 2, T], o, F32R)
        G, o = at("G", [2, 2 * NT, 2, 64], o)
        act_g, o = at("act_g", [2, T], o)
        wtmp, o = at("wtmp", [T], o)
        lnr2, _ = at("lnr2", [2, D], hi_at)

        ident = const[:, C_ID:C_ID + P]
        iota = const[:, C_IOTA:C_IOTA + P]
        ropec = const[:, C_ROPEC:C_ROPEC + P].rearrange("p (t f) -> p t f", t=4)
        ropes = const[:, C_ROPES:C_ROPES + P].rearrange("p (t f) -> p t f", t=4)

        PS = ctx.enter_context(nc.psum_tensor("PS", [P, 8 * 512], F32))

        def bank(b, a=0, e=512):
            return PS[:, b * 512 + a:b * 512 + e]

        def two_banks(b, n):
            return PS[:, b * 512:(b + 2) * 512].rearrange("p (b n) -> p b n", b=2)[:, :, 0:n]

        slot_full = [sem(f"slot_full{i}") for i in range(RING)]
        setup = sem("setup")
        layer_free = sem("layer_free")
        params = sem("params")
        ln1_rows = sem("ln1_rows")
        ln2_rows = sem("ln2_rows")
        kv_stored = sem("kv_stored")
        cond_ready = sem("cond_ready")
        cb_ready = sem("cb_ready")
        mod_full = sem("mod_full")
        mod_ready = sem("mod_ready")
        var_ready = sem("var_ready")
        std_ready = sem("std_ready")
        xn_ready = sem("xn_ready")
        xT_full = sem("xT_full")
        hT_ready = sem("hT_ready")
        z_full = sem("z_full")
        z_ready = sem("z_ready")
        blk_ready = sem("blk_ready")
        tr_full = sem("tr_full")
        tr_ready = sem("tr_ready")
        f1_full = sem("f1_full")
        f1_ready = sem("f1_ready")
        f2_full = sem("f2_full")
        f2_ready = sem("f2_ready")
        lam_sum = sem("lam_sum")
        lam_exp = sem("lam_exp")
        qcur_ready = sem("qcur_ready")
        s_full = sem("s_full")
        mx_ready = sem("mx_ready")
        p_ready = sem("p_ready")
        w_ready = sem("w_ready")
        t_full = sem("t_full")
        pT_ready = sem("pT_ready")
        o_full = sem("o_full")
        o_ready = sem("o_ready")
        dn_ready = sem("dn_ready")
        br_full = sem("br_full")
        br_ready = sem("br_ready")
        mg_full = sem("mg_full")
        sg_ready = sem("sg_ready")
        mg_done = sem("mg_done")
        out_full = sem("out_full")
        out_done = sem("out_done")
        q_full = sem("q_full")
        q_ready = sem("q_ready")
        qcur2_ready = sem("qcur2_ready")
        sc_full = sem("sc_full")
        best_ready = sem("best_ready")
        exp_ready = sem("exp_ready")
        idx_ready = sem("idx_ready")
        idxT_full = sem("idxT_full")
        idxT_ready = sem("idxT_ready")
        oh_ready = sem("oh_ready")
        quad_full = sem("quad_full")
        quad_ready = sem("quad_ready")
        g_stored = [sem(f"g_stored{i}") for i in range(2)]
        hhi_ready = sem("hhi_ready")
        hlo_ready = sem("hlo_ready")
        hi_ready = sem("hi_ready")
        split_ready = sem("split_ready")
        h_full = sem("h_full")
        gelu_ready = sem("gelu_ready")
        g_loaded = [sem(f"g_loaded{i}") for i in range(2)]
        W_ready = sem("W_ready")
        v_full = sem("v_full")
        v_done = sem("v_done")
        layer_done = sem("layer_done")
        y_stored = sem("y_stored")

        block = ctx.enter_context(nc.Block())

        def wait_slot(eng, l, n, extra=0):
            eng.wait_ge(slot_full[n % RING], 16 * (l * TURNS + n // RING + 1 + extra))

        last_use = [(mod_full, N_MOD, k + 1) for k in range(24)]
        last_use += [(z_full, N_Z, 5 * (k + 1)) for k in range(11)]
        last_use += [(f1_full, N_F, N_F)] * 2
        for n in range(3):
            for half in range(2):
                done = 8 * n + 4 * half
                last_use += [(mg_full, N_MG, done + 4), (mg_full, N_MG, done + 2), (mg_full, N_MG, done + 4)]
        last_use += [(out_full, N_OUT, 5 * (k + 1)) for k in range(4)]
        last_use += [(q_full, N_Q, 2 * (k + 1)) for k in range(4)]
        last_use += [(sc_full, NT, NT)]
        assert len(last_use) == PEER

        @block.sync
        def _(sp):
            def load(l, n):
                sp.dma_start(ring[:, n % RING, :],
                             weights[bass.ds(l * PER_LAYER + n, 1)].rearrange("o p f -> (o p) f")
                             ).then_inc(slot_full[n % RING], 16)

            with sp.Fori(0, LAYERS) as l:
                for n in range(PEER + RING):
                    if n < RING:
                        if n == 0:
                            sp.wait_ge(layer_free, l + 1)
                    else:
                        s, per, value = last_use[n - RING]
                        sp.wait_ge(s, layer_at(l, per, value))
                    load(l, n)
                sp.wait_ge(h_full, layer_at(l, 2 * NB, 2))
                load(l, PEER + RING)
                with sp.Fori(0, NB // 2 - 2) as i:
                    for u in range(4):
                        b2 = u // 2
                        if u % 2 == 0:
                            sp.wait_ge(h_full, l * (2 * NB) + i * 4 + 2 * (b2 + 2))
                        else:
                            sp.wait_ge(v_full, l * N_V + i * 20 + 10 * (b2 + 1))
                        sp.dma_start(ring[:, (RING + 1 + u) % RING, :],
                                     weights[bass.ds(l * PER_LAYER + i * 4 + (PEER + RING + 1 + u), 1)]
                                     .rearrange("o p f -> (o p) f")
                                     ).then_inc(slot_full[(RING + 1 + u) % RING], 16)
                for s in range(2 * NB - 3, 2 * NB):
                    old = s - RING
                    if old % 2:
                        sp.wait_ge(h_full, layer_at(l, 2 * NB, 2 * ((old + 1) // 2 + 1)))
                    else:
                        sp.wait_ge(v_full, layer_at(l, N_V, 10 * (old // 2)))
                    load(l, PEER + s)
            sp.wait_ge(layer_done, LAYERS)
            sp.dma_start(y.rearrange("t p d -> p t d"), x[:, :, :]).then_inc(y_stored, 16)
            sp.wait_ge(y_stored, 16)

        @block.gpsimd
        def _(pool):
            pool.dma_start(const[:, :], consts).then_inc(setup, 16)
            pool.dma_start(x[:, :, :], x_in.rearrange("t p d -> p t d")).then_inc(setup, 16)
            pool.dma_start(cnd[:, :, :], cond.rearrange("p (k s) -> p k s", s=2)).then_inc(setup, 16)
            with pool.Fori(0, LAYERS) as l:
                def one(ap):
                    return ap[bass.ds(l, 1)]
                pool.wait_ge(layer_free, l + 1)
                pool.dma_start(bc[:, :], one(bcol).rearrange("o p n -> (o p) n")).then_inc(params, 16)
                pool.dma_start(brw[:, :], one(brow).rearrange("o n -> (o n)").partition_broadcast(P)).then_inc(params, 16)
                pool.dma_start(row[:, :], one(rows).rearrange("o n -> (o n)").partition_broadcast(P)).then_inc(params, 16)
                pool.dma_start(ckb[:, :], one(cache_k).rearrange("o p n -> (o p) n")).then_inc(params, 16)
                pool.dma_start(V[:, 5, :], one(cache_v).rearrange("o p n -> (o p) n")).then_inc(params, 16)
                pool.wait_ge(blk_ready, layer_at(l, N_BLK, 2))
                pool.dma_start(one(new_gk).rearrange("o p n -> (o p) n"), zk[:, 0, :]).then_inc(kv_stored, 16)
                pool.wait_ge(z_ready, layer_at(l, N_Z, 5 * 9))
                pool.dma_start(one(new_dk).rearrange("o p n -> (o p) n"), z[:, 0, 0, :]).then_inc(kv_stored, 16)
                pool.dma_start(one(new_dv).rearrange("o p n -> (o p) n"), V[:, 0, 0:512]).then_inc(kv_stored, 16)
                pool.dma_start(one(new_gv).rearrange("o p n -> (o p) n"), V[:, 0, 512:640]).then_inc(kv_stored, 16)
                pool.wait_ge(o_ready, layer_at(l, N_UNIT, N_UNIT))
                pool.dma_start(lnr[:, :, :], lnrows[bass.ds(l * 2, 1)].rearrange("o a n -> (o a n)")
                               .partition_broadcast(P)).then_inc(ln1_rows, 16)
                pool.wait_ge(setup, 48)
                pool.wait_ge(hlo_ready, l + 1)

                def load_g(b, u):
                    pool.dma_start(G[:, u, :, :, :].rearrange("p g j t -> p (g j t)"),
                                   gate_matrix[bass.ds(b, 1)].rearrange("o p n -> (o p) n")
                                   ).then_inc(g_loaded[u], 16)
                load_g(0, 0)
                load_g(1, 1)
                with pool.Fori(0, (NB - 2) // 2) as i:
                    for u in range(2):
                        pool.wait_ge(W_ready, l * N_W + i * 4 + 2 * (u + 1))
                        load_g(i * 2 + (2 + u), u)
                pool.wait_ge(v_done, layer_at(l, N_V, N_V))
                pool.dma_start(lnr2[:, :, :], lnrows[bass.ds(l * 2 + 1, 1)].rearrange("o a n -> (o a n)")
                               .partition_broadcast(P)).then_inc(ln2_rows, 16)
            pool.wait_ge(kv_stored, 64 * LAYERS)

        @block.tensor
        def _(pe):
            mm = nc.tensor.matmul

            def group(out, pairs):
                for n, (a, b) in enumerate(pairs):
                    last = mm(out, a, b, start=(n == 0), stop=(n == len(pairs) - 1))
                return last

            def turn(out, in_):
                return nc.tensor.transpose(out, in_, ident)

            with pe.Fori(0, LAYERS) as l:
                pe.wait_ge(cb_ready, l + 1)
                for k in range(24):
                    wait_slot(pe, l, MOD + k)
                    w = ring[:, (MOD + k) % RING, :].rearrange("p (k n) -> p k n", k=KC)
                    if k // 4 in (2, 5):
                        gk = k - 8 if k < 12 else k - 16
                        b = 1 + gk % 2
                        if gk >= 2:
                            pe.wait_ge(mod_ready, layer_at(l, 9, gk - 1))
                        for s in range(2):
                            last = group(bank(b, 256 * s, 256 * s + 256),
                                         [(cb[:, s, c, :], w[:, c, :]) for c in range(KC)])
                    else:
                        for sub in range(2):
                            q = 2 * k + sub
                            last = group(bank(0, 2 * q, 2 * q + 2),
                                         [(w[:, c, sub * P:sub * P + P], cnds[:, c, :]) for c in range(KC)])
                    last.then_inc(mod_full, 1)

                def ln_turn(part, src):
                    for t in range(NT):
                        pe.wait_ge(xn_ready, layer_at(l, 10, 5 * part + t + 1))
                        for h in range(2):
                            j = 10 * part + 2 * t + h
                            if 2 * t + h >= 4:
                                pe.wait_ge(hT_ready, layer_at(l, N_HT, j - 3))
                            for c in range(4):
                                last = turn(bank(4 + j % 4, c * P, c * P + P), src[:, t % 2, (4 * h + c) * P:(4 * h + c + 1) * P])
                            last.then_inc(xT_full, 1)

                ln_turn(0, xn)

                pe.wait_ge(hT_ready, layer_at(l, N_HT, 10))

                def project(k):
                    wait_slot(pe, l, GQ + k)
                    w = ring[:, (GQ + k) % RING, :].rearrange("p (k n) -> p k n", k=KC)
                    for t in range(NT):
                        j = 5 * k + t
                        if j >= 4:
                            pe.wait_ge(z_ready, layer_at(l, N_Z, j - 3))
                        group(bank(j % 4, 0, 256), [(hT[:, c, t * P:t * P + P], w[:, c, :])
                                                    for c in range(KC)]).then_inc(z_full, 1)

                tr = [0]

                def qk_turn(ins):
                    j = tr[0]
                    if j >= 2:
                        pe.wait_ge(tr_ready, layer_at(l, N_TR, j - 1))
                    for c, a in enumerate(ins):
                        last = turn(bank(4 + j % 2, c * P, c * P + P), a)
                    last.then_inc(tr_full, 1)
                    tr[0] += 1

                for k in range(5):
                    project(k)
                pe.wait_ge(blk_ready, layer_at(l, N_BLK, 1))
                for t in range(NT):
                    qk_turn([z[:, 0, t, c * P:c * P + P] for c in range(4)])
                pe.wait_ge(blk_ready, layer_at(l, N_BLK, 2))
                pe.wait_ge(params, layer_at(l, 16 * PARAM_DMAS, 16 * PARAM_DMAS))
                qk_turn([zk[:, t, :] for t in range(4)])
                qk_turn([zk[:, 4, :], ckb[:, 512:640]])
                for k in range(5, 7):
                    project(k)
                pe.wait_ge(blk_ready, layer_at(l, N_BLK, 3))
                for t in range(NT):
                    qk_turn([z[:, 1, t, c * P:c * P + P] for c in range(4)])
                for k in range(7, 9):
                    project(k)
                pe.wait_ge(blk_ready, layer_at(l, N_BLK, 4))
                for t in range(NT):
                    qk_turn([z[:, 0, t, c * P:c * P + P] for c in range(4)])
                qk_turn([ckb[:, c * P:c * P + P] for c in range(4)])
                for k in range(9, 11):
                    project(k)

                pe.wait_ge(z_ready, layer_at(l, N_Z, N_Z))
                pe.wait_ge(tr_ready, layer_at(l, N_TR, N_TR))

                def dft_tokens(k):
                    if k >= 1:
                        pe.wait_ge(f1_ready, layer_at(l, N_F, k))
                    if k == 0:
                        for g in range(4):
                            b = 4 + g // 2
                            last = mm(bank(b, 256 * (g % 2), 256 * (g % 2) + 256), z[:, 1, 0, g * P:g * P + P],
                                      const[:, C_COS:C_COS + 256], start=True, stop=True)
                    else:
                        g = k - 1
                        for b in range(2):
                            if k == 1:
                                wait_slot(pe, l, DFT + b)
                            w = ring[:, (DFT + b) % RING, :].rearrange("p (t n) -> p t n", t=4)
                            last = group(bank(4 + b), [(z[:, 1, 1 + t, g * P:g * P + P], w[:, t, :]) for t in range(4)])
                    last.then_inc(f1_full, 1)

                def dft_channels(k):
                    pe.wait_ge(f1_ready, layer_at(l, N_F, k + 1))
                    if k >= 2:
                        pe.wait_ge(f2_ready, layer_at(l, N_F, k - 1))
                    b = 6 + k % 2
                    if k == 0:
                        a = acs[:, 0, :, :].rearrange("p a (g n) -> p (a g) n", n=256)
                        rc, rs = a[:, :, 0:P], a[:, :, P:256]
                    else:
                        rc, rs = acs[:, k % 2, 0, :], acs[:, k % 2, 1, :]
                    group(bank(b), [(const[:, C_COS:C_COS + P], rc),
                                    (const[:, C_NSIN:C_NSIN + P], rs)]).then_inc(f2_full, 1)

                dft_tokens(0)
                for k in range(1, 5):
                    dft_tokens(k)
                    dft_channels(k - 1)
                dft_channels(4)
                pe.wait_ge(f2_ready, layer_at(l, N_F, N_F))

                def attend(t, nk):
                    base = l * N_UNIT + t * UNITS
                    k0 = 0 if nk == 1 else P
                    pe.wait_ge(qcur_ready, l * NT + t + 1)

                    def scores(u):
                        if u >= 1:
                            pe.wait_ge(p_ready, base + u)
                        kc = u if u < 4 else 4
                        for m in range(2):
                            r = slice(64 * m, 64 * m + 64)
                            last = mm(PS[:, m * 1024:m * 1024 + min(nk, 4) * P], qcur[r, u, :],
                                      kT[r, kc, k0:k0 + min(nk, 4) * P], start=True, stop=True)
                            if nk == 5:
                                last = mm(PS[:, m * 1024 + 512:m * 1024 + 640], qcur[r, u, :],
                                          kT[r, kc, k0 + 512:k0 + 640], start=True, stop=True)
                        last.then_inc(s_full, 1)

                    def turn_probs(u):
                        pe.wait_ge(w_ready, base + u + 1)
                        if u >= 1:
                            pe.wait_ge(pT_ready, base + u)
                        for m in range(1 if u < 4 else 2):
                            src = wd[:, u % 2, :] if u < 4 else prob[:, u % 2, m, :]
                            for k in range(nk):
                                n = m * nk + k
                                last = turn(PS[:, 2048 + n * P:2048 + n * P + P], src[:, k * P:k * P + P])
                        last.then_inc(t_full, 1)

                    def values(u):
                        pe.wait_ge(pT_ready, base + u + 1)
                        if u >= 1 or nk == 5:
                            pe.wait_ge(o_ready, base + u)
                        kt = [0] if nk == 1 else list(range(1, 6))
                        if u < 4:
                            last = group(bank(7, 0, P), [(pT[:, u % 2, i, :], V[:, k, u * P:u * P + P])
                                                         for i, k in enumerate(kt)])
                        else:
                            for m in range(2):
                                last = group(bank(7, 64 * m, 64 * m + 64),
                                             [(pT[:, u % 2, m * nk + i, :], V[:, k, 512 + 64 * m:576 + 64 * m])
                                              for i, k in enumerate(kt)])
                        last.then_inc(o_full, 1)

                    scores(0)
                    for u in range(UNITS):
                        if u + 1 < UNITS:
                            scores(u + 1)
                        turn_probs(u)
                        values(u)

                attend(0, 1)
                with pe.Fori(1, NT) as t:
                    attend(t, 5)

                pe.wait_ge(dn_ready, l + 1)
                for t in range(NT):
                    for h in range(2):
                        j = 2 * t + h
                        if j >= 4:
                            pe.wait_ge(br_ready, layer_at(l, N_BR, j - 3))
                        for c in range(4):
                            last = turn(bank(j % 4, c * P, c * P + P), oall[:, t, (4 * h + c) * P:(4 * h + c + 1) * P])
                        last.then_inc(br_full, 1)
                pe.wait_ge(br_ready, layer_at(l, N_BR, N_BR))

                for n in range(3):
                    for half in range(2):
                        slot = MERGE + 6 * n + 3 * half
                        wb = ring[:, slot % RING, :].rearrange("p (c n) -> p c n", c=4)
                        wait_slot(pe, l, slot)
                        for dc in range(4):
                            j = 8 * n + 4 * half + dc
                            gs = slot + 1 + dc // 2
                            if dc % 2 == 0:
                                wait_slot(pe, l, gs)
                            wg = ring[:, gs % RING, :].rearrange("p (c n) -> p c n", c=KC)
                            if j >= 2:
                                pe.wait_ge(mg_done, layer_at(l, N_MG, j - 1))
                            b = 4 * (j % 2)
                            g0 = (dc % 2) * P
                            for th in range(2):
                                ts = slice(th * TH, th * TH + TH)
                                group(bank(b + 2 + th, 0, TH), [(wg[:, c, g0:g0 + P], hT[:, c, ts]) for c in range(KC)])
                            for th in range(2):
                                ts = slice(th * TH, th * TH + TH)
                                src = [fT[:, c, ts] if n == 2 else brT[:, 4 * n + c, ts] for c in range(4)]
                                last = group(bank(b + th, 0, TH),
                                             [(wb[:, c, dc * P:dc * P + P], src[c]) for c in range(4)])
                            last.then_inc(mg_full, 1)
                pe.wait_ge(mg_done, layer_at(l, N_MG, N_MG))

                for k in range(4):
                    wait_slot(pe, l, OUT + k)
                    w = ring[:, (OUT + k) % RING, :].rearrange("p (c n) -> p c n", c=KC)
                    for t in range(NT):
                        j = 5 * k + t
                        if j >= 4:
                            pe.wait_ge(out_done, layer_at(l, N_OUT, j - 3))
                        group(bank(j % 4, 0, 256), [(mT[:, c, t * P:t * P + P], w[:, c, :])
                                                    for c in range(KC)]).then_inc(out_full, 1)

                ln_turn(1, xn2)

                pe.wait_ge(hT_ready, layer_at(l, N_HT, N_HT))
                for k in range(4):
                    wait_slot(pe, l, WQ + k)
                    w = ring[:, (WQ + k) % RING, :].rearrange("p (c n) -> p c n", c=KC)
                    for hh in range(2):
                        j = 2 * k + hh
                        if j >= 2:
                            pe.wait_ge(q_ready, layer_at(l, N_Q, j - 1))
                        for th in range(2):
                            last = group(bank(2 * (j % 2) + th, 0, TH),
                                         [(w[:, c, hh * P:hh * P + P], hT[:, c, th * TH:th * TH + TH])
                                          for c in range(KC)])
                        last.then_inc(q_full, 1)

                keys = ring[:, SUB % RING, 0:1024].rearrange("p (h n) -> p h n", h=HEADS)
                with pe.Fori(0, NT) as t:
                    pe.wait_ge(qcur2_ready, l * NT + t + 1)
                    wait_slot(pe, l, SUB)
                    for h in range(HEADS):
                        for p in range(2):
                            r = slice(64 * p, 64 * p + 64)
                            last = mm(PS[:, 1024 * p + h * P:1024 * p + h * P + P], qcur2[r, h, :], keys[r, h, :],
                                      start=True, stop=True)
                    last.then_inc(sc_full, 1)
                    pe.wait_ge(idx_ready, l * NT + t + 1)
                    for n in range(3):
                        last = turn(bank(4, n * P, n * P + P), idx[:, n, :])
                    last.then_inc(idxT_full, 1)
                    with pe.Fori(0, P // 8) as i:
                        for u in range(2):
                            pe.wait_ge(oh_ready, l * N_QUAD + t * QUADS + i * 2 + (u + 1))
                            for k in range(4):
                                last = mm(bank(5 + u, k * P, k * P + P), ohA[:, 4 * u + k, :], ohB[:, 4 * u + k, :],
                                          start=True, stop=True)
                            last.then_inc(quad_full, 1)

                pe.wait_ge(quad_ready, layer_at(l, N_QUAD, N_QUAD))
                pe.wait_ge(hlo_ready, l + 1)

                def three(out, hi, lo, mhi, mlo, first, final):
                    mm(out, hi, mhi, start=first, stop=False)
                    mm(out, hi, mlo, start=False, stop=False)
                    return mm(out, lo, mhi, start=False, stop=final)

                def up(b, s, wait_gelu=True):
                    uh = ring_hi[:, s, :].rearrange("p (c j n) -> p c j n", c=KC, j=2)
                    ul = ring_lo[:, s, :].rearrange("p (c j n) -> p c j n", c=KC, j=2)
                    for j in range(2):
                        if wait_gelu:
                            pe.wait_ge(gelu_ready, l * (2 * NB) + b * 2 + (j - 1))
                        for c in range(KC):
                            for th in range(2):
                                ts = slice(th * TH, th * TH + TH)
                                last = three(bank(2 * j + th, 0, TH), uh[:, c, j, :], ul[:, c, j, :],
                                             hT_hi[:, c, ts], hT_lo[:, c, ts], c == 0, c == KC - 1)
                        last.then_inc(h_full, 1)

                def down(b, s, par, first=False):
                    vh = ring_hi[:, s, :].rearrange("p (j n) -> p j n", j=2)
                    vl = ring_lo[:, s, :].rearrange("p (j n) -> p j n", j=2)
                    pe.wait_ge(W_ready, l * N_W + b * 2 + 2)
                    for n in range(10):
                        t, dh = n // 2, n % 2
                        if not (first and n < 4):
                            pe.wait_ge(v_done, l * N_V + b * 10 + (n - 3))
                        for j in range(2):
                            last = three(bank(4 + (10 * par + n) % 4), W_hi[:, par, j, t * P:t * P + P],
                                         W_lo[:, par, j, t * P:t * P + P], vh[:, j, dh * 512:dh * 512 + 512],
                                         vl[:, j, dh * 512:dh * 512 + 512], j == 0, j == 1)
                        last.then_inc(v_full, 1)

                def split_wait(n):
                    pe.wait_ge(split_ready, l * N_SPLIT + n + 1)

                split_wait(0)
                up(0, PEER % RING, wait_gelu=False)
                split_wait(1)
                up(1, 1)
                split_wait(2)
                down(0, 2, 0, first=True)
                split_wait(3)
                up(2, 3)
                split_wait(4)
                down(1, 0, 1)
                with pe.Fori(1, NB // 2 - 1) as i:
                    split_wait(i * 4 + 1)
                    up(i * 2 + 1, 1)
                    split_wait(i * 4 + 2)
                    down(i * 2, 2, 0)
                    split_wait(i * 4 + 3)
                    up(i * 2 + 2, 3)
                    split_wait(i * 4 + 4)
                    down(i * 2 + 1, 0, 1)
                split_wait(2 * NB - 3)
                up(NB - 1, 1)
                split_wait(2 * NB - 2)
                down(NB - 2, 2, 0)
                split_wait(2 * NB - 1)
                down(NB - 1, 3, 1)

        @block.scalar
        def _(act):
            A = nc.scalar.activation
            act.wait_ge(setup, 48)
            A(cnds[:, :, :], cnd[:, :, :], ACT.Silu).then_inc(cond_ready, 1)

            with act.Fori(0, LAYERS) as l:
                def root(k, n):
                    act.wait_ge(var_ready, layer_at(l, N_STD, k + 1))
                    A(std[:, 0:n], var[:, 0:n], ACT.Sqrt).then_inc(std_ready, 1)

                def modulate(part):
                    for t in range(NT):
                        s = 0 if t == 0 else 1
                        for h in range(2):
                            j = 10 * part + 2 * t + h
                            act.wait_ge(xT_full, layer_at(l, N_HT, j + 1))
                            for c in range(4):
                                k = 4 * h + c
                                q = 24 * part + k
                                last = A(hT[:, k, t * P:t * P + P], bank(4 + j % 4, c * P, c * P + P), ACT.Identity,
                                         bias=modc[:, q, s:s + 1], scale=modc[:, q + 8, s:s + 1])
                            last.then_inc(hT_ready, 1)

                act.wait_ge(lam_sum, l + 1)
                A(lamw[:, 2:4], lamw[:, 0:2], ACT.Exp).then_inc(lam_exp, 1)

                root(0, NT)
                act.wait_ge(mod_ready, layer_at(l, 9, 9))
                modulate(0)

                def project(k):
                    for t in range(NT):
                        j = 5 * k + t
                        act.wait_ge(z_full, layer_at(l, N_Z, j + 1))
                        src = bank(j % 4, 0, 256)
                        if k < 2:
                            dst = z[:, 0, t, :].rearrange("p (c v d) -> p c v d", c=4, v=2)[:, :, k, :]
                            last = nc.scalar.copy(dst, src.rearrange("p (c d) -> p c d", c=4))
                        elif k == 2:
                            nc.scalar.copy(zk[:, t, :], src[:, 0:P])
                            last = nc.scalar.copy(V[:, t, 512:640], src[:, P:256])
                        else:
                            n = (k - 3) // 2
                            cols = slice(256 * ((k - 3) % 2), 256 * ((k - 3) % 2) + 256)
                            dst = [z[:, 1, t, cols], z[:, 0, t, cols], V[:, t, cols], z[:, 1, t, cols]][n]
                            last = nc.scalar.copy(dst, src)
                        last.then_inc(z_ready, 1)

                tr = [0]

                def qk_out(dst, n):
                    j = tr[0]
                    act.wait_ge(tr_full, layer_at(l, N_TR, j + 1))
                    src = bank(4 + j % 2, 0, n * P)
                    if dst.ndim == 3:
                        src = src.rearrange("p (c n) -> p c n", c=n)
                    nc.scalar.copy(dst, src).then_inc(tr_ready, 1)
                    tr[0] += 1

                for k in range(3):
                    project(k)
                root(1, 50)
                for k in range(3, 5):
                    project(k)
                for t in range(NT):
                    qk_out(qT[:, 4:8, t * P:t * P + P], 4)
                qk_out(kT[:, 4, 0:512], 4)
                qk_out(kT[:, 4, 512:768], 2)
                for k in range(5, 7):
                    project(k)
                for t in range(NT):
                    qk_out(qT[:, 0:4, t * P:t * P + P], 4)
                for k in range(7, 9):
                    project(k)
                for t in range(NT + 1):
                    qk_out(kT[:, 0:4, t * P:t * P + P], 4)
                for k in range(9, 11):
                    project(k)

                def dft_out1(k):
                    act.wait_ge(f1_full, layer_at(l, N_F, k + 1))
                    nc.scalar.copy(acs[:, k % 2, :, :].rearrange("p a n -> p (a n)"),
                                   PS[:, 2048:3072]).then_inc(f1_ready, 1)

                def dft_out2(k):
                    act.wait_ge(f2_full, layer_at(l, N_F, k + 1))
                    src = bank(6 + k % 2)
                    if k == 0:
                        nc.scalar.copy(fT[:, :, 0:P], src.rearrange("p (g n) -> p g n", g=4)).then_inc(f2_ready, 1)
                    else:
                        nc.scalar.copy(fT[:, k - 1, P:T], src).then_inc(f2_ready, 1)

                dft_out1(0)
                for k in range(1, 5):
                    dft_out1(k)
                    dft_out2(k - 1)
                dft_out2(4)

                def attend(t, nk):
                    base = l * N_UNIT + t * UNITS
                    w = nk * P
                    cols = slice(0, P) if nk == 1 else bass.ds(t * P, P)
                    nc.scalar.copy(qcur[:, :, :], qT[:, :, cols]).then_inc(qcur_ready, 1)

                    def exps(u):
                        act.wait_ge(mx_ready, base + u + 1)
                        if u >= 2:
                            act.wait_ge(t_full, base + u - 1)
                        for m in range(2):
                            last = A(prob[:, u % 2, m, 0:w], PS[:, m * 1024:m * 1024 + w], ACT.Exp,
                                     bias=nbias[:, u % 2, m:m + 1], scale=SCALE, accum_out=rsum[:, u % 2, m:m + 1])
                        last.then_inc(p_ready, 1)

                    def probs_out(u):
                        act.wait_ge(t_full, base + u + 1)
                        if u >= 2:
                            act.wait_ge(o_full, base + u - 1)
                        n = nk * (1 if u < 4 else 2)
                        nc.scalar.copy(pT[:, u % 2, 0:n, :].rearrange("p k n -> p (k n)"),
                                       PS[:, 2048:2048 + n * P]).then_inc(pT_ready, 1)

                    exps(0)
                    for u in range(UNITS):
                        if u + 1 < UNITS:
                            exps(u + 1)
                        probs_out(u)
                    act.wait_ge(o_full, base + UNITS)

                attend(0, 1)
                with act.Fori(1, NT) as t:
                    attend(t, 5)

                root(2, 20)
                for t in range(NT):
                    for h in range(2):
                        j = 2 * t + h
                        act.wait_ge(br_full, layer_at(l, N_BR, j + 1))
                        nc.scalar.copy(brT[:, 4 * h:4 * h + 4, t * P:t * P + P],
                                       bank(j % 4).rearrange("p (c n) -> p c n", c=4)).then_inc(br_ready, 1)

                for j in range(N_MG):
                    act.wait_ge(mg_full, layer_at(l, N_MG, j + 1))
                    if j >= 2:
                        act.wait_ge(mg_done, layer_at(l, N_MG, j - 1))
                    A(sg[:, j % 2, :].rearrange("p (h n) -> p h n", h=2), two_banks(4 * (j % 2) + 2, TH),
                      ACT.Sigmoid).then_inc(sg_ready, 1)

                root(3, NT)
                root(4, NT)
                modulate(1)

                for j in range(N_Q):
                    act.wait_ge(q_full, layer_at(l, N_Q, j + 1))
                    nc.scalar.copy(qT2[:, j, :].rearrange("p (h n) -> p h n", h=2),
                                   two_banks(2 * (j % 2), TH)).then_inc(q_ready, 1)
                act.drain()

                with act.Fori(0, NT) as t:
                    nc.scalar.copy(qcur2[:, :, :], qT2[:, :, bass.ds(t * P, P)]).then_inc(qcur2_ready, 1)
                    act.wait_ge(best_ready, l * NT + t + 1)
                    A(pw[:, :, :], pv[:, :, :], ACT.Exp).then_inc(exp_ready, 1)
                    act.wait_ge(idxT_full, l * NT + t + 1)
                    nc.scalar.copy(idxT[:, :, :].rearrange("p a n -> p (a n)"), bank(4, 0, 3 * P)).then_inc(idxT_ready, 1)
                    for half in range(2):
                        st = stg[:, half, :, :, :].rearrange("p b j t -> p (b j) t")
                        with act.Fori(0, 8) as i:
                            for u in range(2):
                                act.wait_ge(quad_full, l * N_QUAD + t * QUADS + i * 2 + (16 * half + u + 1))
                                nc.scalar.copy(st[:, :, bass.ds(i * 8 + 4 * u, 4)],
                                               bank(5 + u).rearrange("p (t j) -> p j t", t=4)).then_inc(quad_ready, 1)
                        act.wait_ge(quad_ready, l * N_QUAD + t * QUADS + 16 * (half + 1))
                        act.dma_start(
                            gate_matrix.rearrange("b p (g n) -> p b g n", g=2 * NT)[:, :, bass.ds(t * 2 + half, 1), :]
                            .rearrange("p b g n -> p b (g n)"),
                            stg[:, half, :, :, :].rearrange("p b j t -> p b (j t)")).then_inc(g_stored[half], 16)
                    for half in range(2):
                        act.wait_ge(g_stored[half], 16 * (l * NT + t + 1))

                nc.scalar.copy(hT_hi[:, :, :], hT[:, :, :]).then_inc(hhi_ready, 1)

                def split_hi(s, n):
                    act.wait_ge(slot_full[s], 16 * (l * TURNS + n + 1))
                    nc.scalar.copy(ring_hi[:, s, :], ring[:, s, :]).then_inc(hi_ready, 1)

                def gelu(b, j, buf_wait=True):
                    act.wait_ge(h_full, l * (2 * NB) + b * 2 + (j + 1))
                    if buf_wait:
                        act.wait_ge(W_ready, l * N_W + b * 2 + (j - 1))
                    A(act_g[:, j, :].rearrange("p (h n) -> p h n", h=2), two_banks(2 * j, TH),
                      ACT.Gelu).then_inc(gelu_ready, 1)

                first_turn = PEER // RING
                split_hi(0, first_turn)
                split_hi(1, first_turn)
                split_hi(2, first_turn)
                gelu(0, 0, False)
                gelu(0, 1, False)
                with act.Fori(0, NB // 2 - 1) as i:
                    for u in range(2):
                        gelu(i * 2 + (u + 1), 0)
                        s = (3 + 2 * u) % RING
                        split_hi(s, i + (first_turn + (3 + 2 * u) // RING))
                        gelu(i * 2 + (u + 1), 1)
                        s = (4 + 2 * u) % RING
                        split_hi(s, i + (first_turn + (4 + 2 * u) // RING))
                gelu(NB - 1, 0)
                split_hi(3, first_turn + NB // 2 - 1)
                gelu(NB - 1, 1)
                root(5, NT)

        @block.vector
        def _(dve):
            tt, ts_, copy = nc.vector.tensor_tensor, nc.vector.tensor_scalar, nc.vector.tensor_copy
            stt = nc.vector.scalar_tensor_tensor
            reduce = nc.vector.tensor_reduce
            dve.wait_ge(setup, 48)
            copy(lamw[:, 8:10], const[:, 0:2]).then_inc(layer_free, 1)

            with dve.Fori(0, LAYERS) as l:
                def root_wait(k):
                    dve.wait_ge(std_ready, layer_at(l, N_STD, k + 1))

                def statistics():
                    for t in range(NT):
                        for h in range(2):
                            nc.vector.bn_stats(stats[:, t, h, :], x[:, t, 512 * h:512 * h + 512])
                    dve.drain()
                    for t in range(NT):
                        nc.vector.bn_aggr(mv[:, t, :], stats[:, t, :, :].rearrange("p a b -> p (a b)"))
                    dve.drain()
                    ts_(var[:, 0:NT], mv[:, :, 1], EPS, None, ALU.add).then_inc(var_ready, 1)

                def ln_out(part, k, dst, src_ready=None):
                    statistics()
                    root_wait(k)
                    nc.vector.reciprocal(rstd[:, 0:NT], std[:, 0:NT])
                    dve.drain()
                    for t in range(NT):
                        if t >= 2:
                            dve.wait_ge(xT_full, layer_at(l, N_HT, 10 * part + 2 * (t - 1)))
                        ts_(dst[:, t % 2, :], x[:, t, :], mv[:, t, 0:1], rstd[:, t:t + 1],
                            ALU.subtract, ALU.mult).then_inc(xn_ready, 1)

                def post_norm(k, rows_sb):
                    statistics()
                    root_wait(k)
                    nc.vector.reciprocal(rstd[:, 0:NT], std[:, 0:NT])
                    dve.drain()
                    for t in range(NT):
                        ts_(x[:, t, :], x[:, t, :], mv[:, t, 0:1], rstd[:, t:t + 1], ALU.subtract, ALU.mult)
                    dve.drain()
                    g = rows_sb[:, 0, :].unsqueeze(1).broadcast_to([P, NT, D])
                    b = rows_sb[:, 1, :].unsqueeze(1).broadcast_to([P, NT, D])
                    tt(x[:, :, :], x[:, :, :], g, ALU.mult)
                    dve.drain()
                    last = tt(x[:, :, :], x[:, :, :], b, ALU.add)
                    return last

                dve.wait_ge(cond_ready, 1)
                for s in range(2):
                    last = copy(cb[:, s, :, :], cnds[:, :, s:s + 1].broadcast_to([P, KC, P]))
                last.then_inc(cb_ready, 1)
                dve.wait_ge(params, layer_at(l, 16 * PARAM_DMAS, 16 * PARAM_DMAS))

                lv = row[:, 0:256].rearrange("p (a b d) -> p a b d", a=2, b=2)
                tt(lamp[:, :, :], lv[:, :, 0, :], lv[:, :, 1, :], ALU.mult)
                dve.drain()
                reduce(lamw[:, 0:2], lamp[:, :, :], AX.X, ALU.add).then_inc(lam_sum, 1)
                dve.wait_ge(lam_exp, l + 1)
                tt(lamw[:, 4:5], lamw[:, 2:3], lamw[:, 3:4], ALU.subtract)
                copy(lamw[:, 6:7], const[:, bass.ds(l * 2 + (C_LAM + 1), 1)])
                dve.drain()
                tt(lamw[:, 4:5], lamw[:, 4:5], const[:, bass.ds(l * 2 + C_LAM, 1)], ALU.add)
                dve.drain()
                ts_(lamw[:, 5:6], lamw[:, 4:5], -1.0, None, ALU.mult)

                for gk in range(8):
                    k = 8 + gk if gk < 4 else 16 + gk
                    dve.wait_ge(mod_full, layer_at(l, N_MOD, k + 1))
                    w, c0 = gk // 4, 256 * (gk % 4)
                    bias = brw[:, w * D + c0:w * D + c0 + 256].unsqueeze(1).broadcast_to([P, 2, 256])
                    tt(gates[:, w, :, c0:c0 + 256], bank(1 + gk % 2).rearrange("p (s n) -> p s n", s=2), bias,
                       ALU.add).then_inc(mod_ready, 1)
                cols = PS[:, 0:96].rearrange("p (q s) -> p q s", s=2)
                for q in (0, 24):
                    tt(modc[:, q:q + 8, :], cols[:, q:q + 8, :],
                       bc[:, q:q + 8].unsqueeze(2).broadcast_to([P, 8, 2]), ALU.add)
                    last = stt(modc[:, q + 8:q + 16, :], cols[:, q + 8:q + 16, :], 1.0,
                               bc[:, q + 8:q + 16].unsqueeze(2).broadcast_to([P, 8, 2]), ALU.add, ALU.add)
                last.then_inc(mod_ready, 1)

                ln_out(0, 0, xn)

                def rotary(v, heads):
                    e = v.rearrange("p t h (f two) -> p t h f two", two=2)
                    xe, xo = e[:, :, :, :, 0], e[:, :, :, :, 1]
                    c = ropec.unsqueeze(2).broadcast_to([P, 4, heads, 32])
                    s = ropes.unsqueeze(2).broadcast_to([P, 4, heads, 32])
                    r = [rot[:, n, 0:4 * heads * 32].rearrange("p (t h f) -> p t h f", t=4, h=heads) for n in range(4)]
                    tt(r[0], xe, c, ALU.mult)
                    tt(r[1], xo, s, ALU.mult)
                    tt(r[2], xe, s, ALU.mult)
                    tt(r[3], xo, c, ALU.mult)
                    dve.drain()
                    tt(xe, r[0], r[1], ALU.subtract)
                    return tt(xo, r[2], r[3], ALU.add)

                gq = z[:, 0, :, :].rearrange("p t (h d) -> p (t h) d", d=64)
                gk = zk[:, :, :].rearrange("p t (h d) -> p (t h) d", d=64)
                dve.wait_ge(z_ready, layer_at(l, N_Z, 15))
                for v, n0, n in ((gq, 0, 40), (gk, 40, 10)):
                    tmp = sq[:, 0:64 * n].rearrange("p (n d) -> p n d", d=64)
                    tt(tmp, v, v, ALU.mult)
                    dve.drain()
                    reduce(var[:, n0:n0 + n], tmp, AX.X, ALU.add)
                    dve.drain()
                ts_(var[:, 0:50], var[:, 0:50], 1.0 / 64, EPS, ALU.mult, ALU.add).then_inc(var_ready, 1)
                root_wait(1)
                nc.vector.reciprocal(rstd[:, 0:50], std[:, 0:50])
                dve.drain()
                for v, n0, n, g0 in ((gq, 0, 40, 256), (gk, 40, 10, 320)):
                    tt(v, v, rstd[:, n0:n0 + n].unsqueeze(2).broadcast_to([P, n, 64]), ALU.mult)
                    dve.drain()
                    tt(v, v, row[:, g0:g0 + 64].unsqueeze(1).broadcast_to([P, n, 64]), ALU.mult)
                    dve.drain()
                rotary(z[:, 0, 1:NT, :].rearrange("p t (h d) -> p t h d", d=64), 8).then_inc(blk_ready, 1)
                dve.drain()
                rotary(zk[:, 1:NT, :].rearrange("p t (h d) -> p t h d", d=64), 2).then_inc(blk_ready, 1)
                for buf, done in ((1, 25), (0, 35)):
                    dve.drain()
                    dve.wait_ge(z_ready, layer_at(l, N_Z, done))
                    rotary(z[:, buf, 1:NT, :].rearrange("p t (h d) -> p t h d", d=64), 8).then_inc(blk_ready, 1)

                dve.wait_ge(kv_stored, 64 * (l + 1))
                dve.wait_ge(f2_full, layer_at(l, N_F, N_F))

                def attend(t, nk):
                    base = l * N_UNIT + t * UNITS
                    w = nk * P
                    tile_rows = oall[:, 0, :] if nk == 1 else oall[:, bass.ds(t, 1), :].rearrange("p o d -> p (o d)")

                    def maxima(u):
                        dve.wait_ge(s_full, base + u + 1)
                        s = PS[:, 0:2048].rearrange("p (m n) -> p m n", m=2)[:, :, 0:w]
                        reduce(smx[:, u % 2, :], s, AX.X, ALU.max)
                        dve.drain()
                        ts_(nbias[:, u % 2, :], smx[:, u % 2, :], -SCALE, None, ALU.mult).then_inc(mx_ready, 1)

                    def weights_of(u):
                        b = u % 2
                        dve.wait_ge(p_ready, base + u + 1)
                        if u >= 4:
                            nc.vector.reciprocal(rinv[:, b, :], rsum[:, b, :]).then_inc(w_ready, 1)
                            return
                        nc.vector.reciprocal(rinv[:, b, :], rsum[:, b, :])
                        dve.drain()
                        tt(rneg[:, b:b + 1], rinv[:, b, 1:2], lamw[:, 5:6], ALU.mult)
                        dve.drain()
                        ts_(prob[:, b, 1, 0:w], prob[:, b, 1, 0:w], rneg[:, b:b + 1], None, ALU.mult)
                        dve.drain()
                        if u >= 2:
                            dve.wait_ge(t_full, base + u - 1)
                        stt(wd[:, b, 0:w], prob[:, b, 0, 0:w], rinv[:, b, 0:1], prob[:, b, 1, 0:w],
                            ALU.mult, ALU.add).then_inc(w_ready, 1)

                    def outputs(u):
                        dve.wait_ge(o_full, base + u + 1)
                        if u < 4:
                            last = copy(tile_rows[:, u * P:u * P + P], bank(7, 0, P))
                        else:
                            for m in range(2):
                                c = 512 + (4 * m + u - 4) * 64
                                last = ts_(tile_rows[:, c:c + 64], bank(7, 64 * m, 64 * m + 64),
                                           rinv[:, u % 2, m:m + 1], None, ALU.mult)
                        last.then_inc(o_ready, 1)

                    maxima(0)
                    for u in range(UNITS):
                        weights_of(u)
                        if u >= 1:
                            outputs(u - 1)
                        if u + 1 < UNITS:
                            maxima(u + 1)
                    outputs(UNITS - 1)
                    dve.drain()

                attend(0, 1)
                with dve.Fori(1, NT) as t:
                    attend(t, 5)

                dv4 = oall[:, :, 0:512].rearrange("p t (h d) -> p t h d", d=P)
                s4 = sq[:, :].rearrange("p (t h d) -> p t h d", t=NT, h=4)
                tt(s4, dv4, dv4, ALU.mult)
                dve.drain()
                reduce(var[:, 0:20], sq[:, :].rearrange("p (n d) -> p n d", d=P), AX.X, ALU.add)
                dve.drain()
                ts_(var[:, 0:20], var[:, 0:20], 1.0 / P, EPS, ALU.mult, ALU.add).then_inc(var_ready, 1)
                root_wait(2)
                nc.vector.reciprocal(rstd[:, 0:20], std[:, 0:20])
                dve.drain()
                ts_(rstd[:, 0:20], rstd[:, 0:20], lamw[:, 6:7], None, ALU.mult)
                dve.drain()
                tt(dv4, dv4, rstd[:, 0:20].rearrange("p (t h) -> p t h", t=NT).unsqueeze(3).broadcast_to([P, NT, 4, P]),
                   ALU.mult)
                dve.drain()
                tt(dv4, dv4, row[:, 384:512].unsqueeze(1).unsqueeze(1).broadcast_to([P, NT, 4, P]),
                   ALU.mult).then_inc(dn_ready, 1)

                for j in range(N_MG):
                    n, dc = j // 8, j % 8
                    b = 4 * (j % 2)
                    dve.wait_ge(sg_ready, layer_at(l, N_MG, j + 1))
                    s = sg[:, j % 2, :].rearrange("p (h n) -> p h n", h=2)
                    m = mT[:, dc, :].rearrange("p (h n) -> p h n", h=2)
                    tm = mtmp[:, :].rearrange("p (h n) -> p h n", h=2)
                    if n == 0:
                        tt(m, two_banks(b, TH), s, ALU.mult).then_inc(mg_done, 1)
                    else:
                        tt(tm, two_banks(b, TH), s, ALU.mult)
                        dve.drain()
                        tt(m, m, tm, ALU.add).then_inc(mg_done, 1)
                        dve.drain()

                for j in range(N_OUT):
                    k, t = j // 5, j % 5
                    s = 0 if t == 0 else 1
                    cols = slice(256 * k, 256 * k + 256)
                    dve.wait_ge(out_full, layer_at(l, N_OUT, j + 1))
                    tt(otmp[:, j % 2, :], bank(j % 4, 0, 256), gates[:, 0, s, cols], ALU.mult)
                    dve.drain()
                    stt(x[:, t, cols], x[:, t, cols], ALPHA, otmp[:, j % 2, :], ALU.mult, ALU.add).then_inc(out_done, 1)
                dve.drain()
                dve.wait_ge(ln1_rows, 16 * (l + 1))
                post_norm(3, lnr)
                dve.drain()
                ln_out(1, 4, xn2)

                scores = PS[:, 0:2048].rearrange("p (s n) -> p s n", n=P)
                with dve.Fori(0, NT) as t:
                    dve.wait_ge(sc_full, l * NT + t + 1)
                    nc.vector.memset(pm[:, :], 0.0)
                    for s in range(16):
                        nc.vector.max(sv[:, s, 0:8], scores[:, s, :])
                    dve.drain()
                    for s in range(16):
                        nc.vector.match_replace(work[:, s, :], sv[:, s, 0:8], scores[:, s, :], LOWEST)
                        nc.vector.max_index(si[:, s, 0:8], sv[:, s, 0:8], scores[:, s, :])
                    dve.drain()
                    for s in range(16):
                        nc.vector.max(sv[:, s, 8:16], work[:, s, :])
                    dve.drain()
                    for s in range(16):
                        nc.vector.max_index(si[:, s, 8:16], sv[:, s, 8:16], work[:, s, :])
                    c4 = cand[:, :, :].rearrange("p h (i j) -> p h i j", i=TOPK)
                    tt(c4, sv[:, 0:8, :].unsqueeze(3).broadcast_to([P, 8, TOPK, TOPK]),
                       sv[:, 8:16, :].unsqueeze(2).broadcast_to([P, 8, TOPK, TOPK]), ALU.add)
                    dve.drain()
                    copy(sif[:, :, :], si[:, :, :])
                    c2 = work[:, :, :].rearrange("p s n -> p (s n)").rearrange("p (h n) -> p h n", h=8)
                    for h in range(HEADS):
                        nc.vector.max(pv[:, h, 0:8], cand[:, h, :])
                    dve.drain()
                    for h in range(HEADS):
                        nc.vector.match_replace(c2[:, h, :], pv[:, h, 0:8], cand[:, h, :], LOWEST)
                        nc.vector.max_index(pi[:, h, 0:8], pv[:, h, 0:8], cand[:, h, :])
                    dve.drain()
                    for h in range(HEADS):
                        nc.vector.max(pv[:, h, 8:16], c2[:, h, :])
                    dve.drain()
                    for h in range(HEADS):
                        nc.vector.max_index(pi[:, h, 8:16], pv[:, h, 8:16], c2[:, h, :])
                    copy(pm[:, 8:16], pv[:, :, 0])
                    dve.drain()
                    tt(pv[:, :, :], pv[:, :, :], pm[:, 8:16].unsqueeze(2).broadcast_to([P, 8, TOPK]),
                       ALU.subtract).then_inc(best_ready, 1)
                    flat = pi[:, :, :].rearrange("p h k -> p (h k)")
                    ts_(pii[:, 0, :], flat, 4, None, ALU.logical_shift_right)
                    ts_(pii[:, 1, :], flat, 15, None, ALU.bitwise_and)
                    dve.drain()
                    copy(pif[:, :, :], pii[:, :, :])
                    dve.drain()
                    eq = cand[:, :, :].rearrange("p h (k m) -> p h k m", k=TOPK)
                    for p in range(2):
                        place = pif[:, p, :].unsqueeze(2).broadcast_to([P, P, TOPK])
                        tt(cand[:, :, :].rearrange("p h (k m) -> p (h k) m", k=TOPK),
                           iota[:, 0:TOPK].unsqueeze(1).broadcast_to([P, P, TOPK]), place, ALU.is_equal)
                        dve.drain()
                        tt(eq, eq, sif[:, 8 * p:8 * p + 8, :].unsqueeze(2).broadcast_to([P, 8, TOPK, TOPK]), ALU.mult)
                        dve.drain()
                        reduce(idx[:, p, :], cand[:, :, :].rearrange("p h (k m) -> p (h k) m", k=TOPK), AX.X, ALU.add)
                        dve.drain()
                    dve.wait_ge(exp_ready, l * NT + t + 1)
                    reduce(pm[:, 0:8], pw[:, :, :], AX.X, ALU.add)
                    dve.drain()
                    nc.vector.reciprocal(pm[:, 8:16], pm[:, 0:8])
                    dve.drain()
                    tt(idx[:, 2, :].rearrange("p (h k) -> p h k", h=8), pw[:, :, :],
                       pm[:, 8:16].unsqueeze(2).broadcast_to([P, 8, TOPK]), ALU.mult).then_inc(idx_ready, 1)
                    dve.wait_ge(idxT_ready, l * NT + t + 1)

                    def onehots(tok, u):
                        for k in range(4):
                            n = 4 * u + k
                            ts_(ohA[:, n, :], iota, idxT[:, 0, bass.ds(tok + n, 1)], None, ALU.is_equal)
                            last = ts_(ohB[:, n, :], iota, idxT[:, 1, bass.ds(tok + n, 1)],
                                       idxT[:, 2, bass.ds(tok + n, 1)], ALU.is_equal, ALU.mult)
                        last.then_inc(oh_ready, 1)

                    onehots(0, 0)
                    onehots(0, 1)
                    with dve.Fori(1, P // 8) as i:
                        for u in range(2):
                            dve.wait_ge(quad_ready, l * N_QUAD + t * QUADS + i * 2 + (u - 1))
                            onehots(i * 8, u)
                    dve.wait_ge(quad_ready, l * N_QUAD + t * QUADS + QUADS)

                dve.wait_ge(hhi_ready, l + 1)
                nc.vector.memset(acc[:, :, :], 0.0)
                dve.drain()
                tt(hT_lo[:, :, :], hT[:, :, :], hT_hi[:, :, :].bitcast(F32), ALU.subtract).then_inc(hlo_ready, 1)

                def split_lo(s, n):
                    dve.wait_ge(hi_ready, l * N_SPLIT + n + 1)
                    tt(ring_lo[:, s, :], ring[:, s, :], ring_hi[:, s, :].bitcast(F32), ALU.subtract).then_inc(split_ready, 1)

                def weigh(b, j, u, gcount):
                    if j == 0:
                        dve.wait_ge(g_loaded[u], 16 * (l * (NB // 2) + gcount + 1))
                    dve.wait_ge(gelu_ready, l * (2 * NB) + b * 2 + (j + 1))
                    tt(wtmp[:, :].rearrange("p (g t) -> p g t", t=64),
                       act_g[:, j, :].rearrange("p (g t) -> p g t", t=64), G[:, u, :, j, :], ALU.mult)
                    dve.drain()
                    copy(W_hi[:, u, j, :], wtmp[:, :])
                    dve.drain()
                    tt(W_lo[:, u, j, :], wtmp[:, :], W_hi[:, u, j, :].bitcast(F32), ALU.subtract).then_inc(W_ready, 1)
                    dve.drain()

                def add_up(b, n0, n1, par):
                    for n in range(n0, n1):
                        t, dh = n // 2, n % 2
                        dve.wait_ge(v_full, l * N_V + b * 10 + (n + 1))
                        a = acc[:, t, 512 * dh:512 * dh + 512]
                        tt(a, a, bank(4 + (10 * par + n) % 4), ALU.add).then_inc(v_done, 1)

                for n in range(3):
                    split_lo(n, n)
                weigh(0, 0, 0, 0)
                weigh(0, 1, 0, 0)
                with dve.Fori(0, NB // 2 - 1) as i:
                    for u in range(2):
                        v = 1 - u
                        gc = i + u
                        weigh(i * 2 + (u + 1), 0, v, gc)
                        split_lo((3 + 2 * u) % RING, i * 4 + (3 + 2 * u))
                        weigh(i * 2 + (u + 1), 1, v, gc)
                        add_up(i * 2 + u, 0, 5, u)
                        split_lo((4 + 2 * u) % RING, i * 4 + (4 + 2 * u))
                        add_up(i * 2 + u, 5, 10, u)
                weigh(NB - 1, 0, 1, NB // 2 - 1)
                split_lo(3, 2 * NB - 1)
                weigh(NB - 1, 1, 1, NB // 2 - 1)
                add_up(NB - 2, 0, 10, 0)
                add_up(NB - 1, 0, 10, 1)
                dve.drain()

                for t in range(NT):
                    tt(acc[:, t, :], acc[:, t, :], gates[:, 1, 0 if t == 0 else 1, :], ALU.mult)
                dve.drain()
                stt(x[:, :, :].rearrange("p t d -> p (t d)"), x[:, :, :].rearrange("p t d -> p (t d)"), ALPHA,
                    acc[:, :, :].rearrange("p t d -> p (t d)"), ALU.mult, ALU.add)
                dve.drain()
                dve.wait_ge(ln2_rows, 16 * (l + 1))
                post_norm(5, lnr2).then_inc(layer_done, 1)
                dve.drain()
                copy(lamw[:, 8:10], const[:, 0:2]).then_inc(layer_free, 1)


def constants(np):
    f = np.float64
    n = np.arange(P)
    ang = 2 * np.pi * ((n[:, None] * n[None, :]) % P) / P
    cos, sin = np.cos(ang) / np.sqrt(f(P)), np.sin(ang) / np.sqrt(f(P))
    tok = np.arange(4 * P)
    freq = np.float32(10000.0) ** (-np.arange(16, dtype=np.float32) / np.float32(16))
    pos = np.concatenate([(tok // 64)[:, None] * freq, (tok % 64)[:, None] * freq], -1).astype(np.float32)
    rc = np.cos(pos.astype(f)).reshape(4, P, 32).transpose(1, 0, 2).reshape(P, P)
    rs = np.sin(pos.astype(f)).reshape(4, P, 32).transpose(1, 0, 2).reshape(P, P)
    lam = []
    for layer in range(LAYERS):
        init = 0.8 - 0.6 * np.exp(-0.3 * layer)
        lam += [init, 1.0 - init]
    parts = [np.eye(P), np.tile(n, (P, 1)), cos, sin, -sin, rc, rs, np.tile(lam, (P, 1))]
    table = np.concatenate(parts, 1).astype(np.float32)
    assert table.shape[1] == NCONST
    m = np.arange(4 * P)
    ang = 2 * np.pi * ((m[:, None] * m[None, :]) % (4 * P)) / (4 * P)
    dft = [(g(ang) / np.sqrt(f(4 * P))).astype(np.float32).reshape(4, P, 4 * P).transpose(1, 0, 2).reshape(P, SLOT)
           for g in (np.cos, np.sin)]
    return table, dft


def weight_stream(np, w_mod, w_in, w_branch, w_out, peer_wq, peer_subkeys, peer_u, peer_v, dft):
    out = np.zeros((LAYERS, PER_LAYER, P, SLOT), np.float32)

    def columns(w, c0, width=256):
        return w[:, c0:c0 + width].reshape(-1, P, width).transpose(1, 0, 2).reshape(P, -1)

    for l in range(LAYERS):
        s = out[l]
        for k in range(24):
            s[MOD + k] = columns(w_mod[l], 256 * k)
        starts = [1536, 1792, 2048, 0, 256, 512, 768, 1024, 1280, 2304, 2560]
        for k, c0 in enumerate(starts):
            s[GQ + k] = columns(w_in[l], c0)
        s[DFT], s[DFT + 1] = dft
        for n in range(3):
            for half in range(2):
                slot = MERGE + 6 * n + 3 * half
                s[slot] = columns(w_branch[l, n], 512 * half, 512)
                for g in range(2):
                    s[slot + 1 + g] = columns(w_in[l], 2816 + n * D + 512 * half + 256 * g)
        for k in range(4):
            s[OUT + k] = columns(w_out[l], 256 * k)
            s[WQ + k] = columns(peer_wq[l], 256 * k)
        s[SUB, :, 0:1024] = peer_subkeys[l].transpose(1, 3, 0, 2).reshape(P, 1024)
        u = peer_u[l].reshape(P, NB, 2, KC, P).transpose(1, 4, 3, 2, 0).reshape(NB, P, SLOT)
        v = peer_v[l].reshape(P, NB, 2, D).transpose(1, 0, 2, 3).reshape(NB, P, SLOT)
        s[PEER] = u[0]
        s[PEER + 1:PER_LAYER - 1:2] = u[1:]
        s[PEER + 2:PER_LAYER:2] = v[:-1]
        s[PER_LAYER - 1] = v[-1]
    return out.reshape(LAYERS * PER_LAYER, P, SLOT)


def build(nc):
    def dram(name, shape, kind):
        return nc.dram_tensor(name, shape, F32, kind=kind).ap()

    ins = {n: dram(n, s, "ExternalInput") for n, s in (
        ("weights", (LAYERS * PER_LAYER, P, SLOT)), ("consts", (P, NCONST)), ("x_in", (NT, P, D)),
        ("cond", (P, 2 * KC)), ("bcol", (LAYERS, P, 48)), ("brow", (LAYERS, 2048)), ("rows", (LAYERS, 512)),
        ("lnrows", (LAYERS * 2, 2, D)), ("cache_k", (LAYERS, P, 640)), ("cache_v", (LAYERS, P, 640)))}
    outs = {n: dram(n, s, "ExternalOutput") for n, s in (
        ("y", (NT, P, D)), ("new_dk", (LAYERS, P, 512)), ("new_dv", (LAYERS, P, 512)),
        ("new_gk", (LAYERS, P, P)), ("new_gv", (LAYERS, P, P)))}
    gate_matrix = dram("gate_matrix", (NB, P, 2 * T), "Internal")
    trunk(nc, **ins, **outs, gate_matrix=gate_matrix)


def layouts(np, i):
    c = np.ascontiguousarray
    table, dft = constants(np)
    rows = np.concatenate([i["diff_lam"].reshape(LAYERS, 256), i["q_norm_g"], i["k_norm_g"], i["diff_norm_g"]], 1)
    b = i["b_mod"]
    return {
        "weights": weight_stream(np, i["w_mod"], i["w_in"], i["w_branch"], i["w_out"], i["peer_wq"],
                                 i["peer_subkeys"], i["peer_u"], i["peer_v"], dft),
        "consts": table,
        "x_in": np.concatenate([i["x_prompt"].reshape(1, P, D), i["x_sample"].reshape(4, P, D)], 0),
        "cond": c(np.stack([i["c_ctx"], i["c"][0]], -1).reshape(KC, P, 2).transpose(1, 0, 2).reshape(P, 2 * KC)),
        "bcol": c(b.reshape(LAYERS, 48, P).transpose(0, 2, 1)),
        "brow": np.concatenate([b[:, 2048:3072], b[:, 5120:6144]], 1),
        "rows": rows,
        "lnrows": c(np.stack([i["ln_g"], i["ln_b"]], 2).reshape(LAYERS * 2, 2, D)),
        "cache_k": np.concatenate([i["cache_diff_k"][0].reshape(LAYERS, P, 512),
                                   i["cache_gqa_k"][0].reshape(LAYERS, P, P)], -1),
        "cache_v": np.concatenate([i["cache_diff_v"][0].reshape(LAYERS, P, 512),
                                   i["cache_gqa_v"][0].reshape(LAYERS, P, P)], -1),
    }


def kernel(**inputs):
    import numpy as np
    import concourse.bacc as bacc
    from concourse.bass_utils import run_bass_kernel_spmd

    arrays = layouts(np, {k: np.asarray(v) for k, v in inputs.items()})
    nc = bacc.Bacc("TRN2", target_bir_lowering=False, num_devices=1)
    build(nc)
    r = run_bass_kernel_spmd(nc, [arrays], core_ids=[0]).results[0]
    y = r["y"]
    return (y[0:1], y[1:].reshape(1, 512, D),
            r["new_dk"].reshape(1, LAYERS, P, 4, P), r["new_dv"].reshape(1, LAYERS, P, 4, P),
            r["new_gk"].reshape(1, LAYERS, P, 2, 64), r["new_gv"].reshape(1, LAYERS, P, 2, 64))
```

```python
from contextlib import ExitStack

import concourse.bass as bass
from concourse import mybir
from concourse.alu_op_type import AluOpType as ALU

F32 = mybir.dt.float32
F32R = mybir.dt.float32r
U32 = mybir.dt.uint32
ACT = mybir.ActivationFunctionType
AX = mybir.AxisListType

P = 128
D = 1024
KC = D // P
LAYERS = 2
NT = 5
T = NT * P
TH = T // 2
HEADS = 8
TOPK = 16
KEYS = 128
ALPHA = float((2 * LAYERS) ** 0.25)
EPS = 1e-6
SCALE = 64.0 ** -0.5
LOWEST = -3.0e38

RING = 4
SLOT = 2048
MOD1, GQ, KV, DQ, DK, DV, FZ, DFT, MOD2 = 0, 8, 10, 11, 13, 15, 17, 19, 21
MERGE, OUT, WQ, SUB, PEER = 37, 55, 59, 63, 64
NB = KEYS // 2
PER_LAYER = PEER + 2 * NB
TURNS = PER_LAYER // RING

N_STD = 6
N_MOD = 24
N_HT = 20
N_Z = 55
N_BLK = 4
N_TR = 18
N_F = 5
UNITS = 8
N_UNIT = NT * UNITS
TURN_GROUPS = 12
N_T = NT * TURN_GROUPS
N_BR = 10
N_MG = 24
N_OUT = 20
N_Q = 8
QUADS = P // 4
N_QUAD = NT * QUADS
N_W = 2 * NB
N_SPLIT = 2 * NB
N_V = 10 * NB
PARAM_DMAS = 4

C_ID, C_IOTA, C_COS, C_SIN, C_NSIN, C_ROPEC, C_ROPES, C_ONE, C_LAM = 0, 128, 256, 384, 512, 640, 768, 896, 1024
NCONST = 1028


def layer_at(l, per_layer, n):
    return l * per_layer + n


def trunk(nc, weights, consts, x_in, cond, bcol, rows, lnrows, cache_k, cache_v,
          y, new_dk, new_dv, new_gk, new_gv, gate_matrix):
    ctx = ExitStack()
    with ctx:
        def sem(name):
            return ctx.enter_context(nc.semaphore(name))

        slab_floats = 53200
        slab_at = -(-nc.sbuf_base // 32) * 32
        ctx.enter_context(nc.sbuf_tensor("slab", [P, slab_floats], F32))

        def at(name, shape, offset, dt=F32):
            size = 1
            for s in shape:
                size *= s
            assert offset + size <= slab_floats, (name, offset, size)
            t = nc.alloc_sbuf_tensor_at(name, [P] + list(shape), dt, offset=slab_at + 4 * offset)
            return t, offset + -(-size // 8) * 8

        o = 0
        const, o = at("const", [NCONST], o)
        row, o = at("row", [512], o)
        bc, o = at("bc", [48], o)
        modc, o = at("modc", [48, 2], o)
        cnd, o = at("cnd", [KC, 2], o)
        cnds, o = at("cnds", [KC, 2], o)
        stats, o = at("stats", [NT, 2, 6], o)
        mv, o = at("mv", [NT, 2], o)
        var, o = at("var", [64], o)
        std, o = at("std", [64], o)
        rstd, o = at("rstd", [64], o)
        lamw, o = at("lamw", [16], o)
        smx, o = at("smx", [2, 2], o)
        nbias, o = at("nbias", [2, 2], o)
        rsum, o = at("rsum", [2, 2], o)
        rinv, o = at("rinv", [2, 2], o)
        rneg, o = at("rneg", [2], o)
        ring_at = o
        ring, o = at("ring", [RING, SLOT], o)
        ht_at = o
        hT, o = at("hT", [KC, T], o)
        x, o = at("x", [NT, D], o)
        gate2, o = at("gate2", [2, D], o)
        arena = o

        z_at = o
        z, o = at("z", [2, NT, 512], o)
        zk, o = at("zk", [NT, P], o)
        q_at = o
        qT, o = at("qT", [8, T], o)
        k_at = o
        kT, o = at("kT", [5, 768], o)
        V, o = at("V", [6, 640], o)
        fT, o = at("fT", [4, T], o)
        ck_at = o
        ckb, _ = at("ckb", [640], ck_at)
        qcur, o = at("qcur", [8, P], ck_at)
        tmp_at = o
        lamp, _ = at("lamp", [2, 64], tmp_at + 4096)
        xn, _ = at("xn", [2, D], tmp_at)
        sq, _ = at("sq", [2560], tmp_at)
        rot, _ = at("rot", [4, 1024], tmp_at)
        acs, _ = at("acs", [2, 2, 512], tmp_at)
        prob, t = at("prob", [2, 2, 640], tmp_at)
        wd, t = at("wd", [2, 640], t)
        pT, t = at("pT", [2, 2, 5, P], t)
        o = t
        sg, t = at("sg", [2, T], tmp_at)
        mtmp, _ = at("mtmp", [T], t)
        otmp, _ = at("otmp", [2, 256], tmp_at)
        oall, _ = at("oall", [NT, D], z_at)
        mT, _ = at("mT", [KC, T], z_at)
        brT, _ = at("brT", [8, T], q_at)
        diag, t = at("diag", [2, 2, KC, P], k_at)
        lnr, _ = at("lnr", [2, D], t)
        gate1, _ = at("gate1", [2, D], tmp_at + 3840)

        o = arena
        stg, o = at("stg", [2, NB, 2, 64], o)
        xn2, _ = at("xn2", [2, D], arena)
        qT2, o = at("qT2", [8, T], o)
        ohA, _ = at("ohA", [4, 4, P], o)
        work, o = at("work", [16, P], o)
        ohE, _ = at("ohE", [4, 4, P], o)
        cand, o = at("cand", [8, 256], o)
        ohB, _ = at("ohB", [4, 4, P], o)
        score, o = at("score", [16, P], o)
        qcur2, _ = at("qcur2", [8, P], ring_at + (SUB % RING) * SLOT + 1024)
        sv, o = at("sv", [16, TOPK], o)
        si, o = at("si", [16, TOPK], o, U32)
        sif, o = at("sif", [16, TOPK], o)
        pv, o = at("pv", [8, TOPK], o)
        pi, o = at("pi", [8, TOPK], o, U32)
        pii, o = at("pii", [2, P], o, U32)
        pif, o = at("pif", [2, P], o)
        idx, o = at("idx", [3, P], o)
        idxT, o = at("idxT", [3, P], o)
        pw, o = at("pw", [8, TOPK], o)
        pm, o = at("pm", [16], o)

        o = arena
        ring_lo = at("ring_lo", [RING, SLOT], ring_at, F32R)[0]
        hT_lo = at("hT_lo", [KC, T], ht_at, F32R)[0]
        hi_at = o
        ring_hi, o = at("ring_hi", [RING, SLOT], o, F32R)
        hT_hi, o = at("hT_hi", [KC, T], o, F32R)
        acc, o = at("acc", [NT, D], o)
        W_hi, o = at("W_hi", [2, 2, T], o, F32R)
        W_lo, o = at("W_lo", [2, 2, T], o, F32R)
        G, o = at("G", [2, 2 * NT, 2, 64], o)
        act_g, o = at("act_g", [2, T], o)
        wtmp, o = at("wtmp", [T], o)
        lnr2, _ = at("lnr2", [2, D], hi_at)

        ident = const[:, C_ID:C_ID + P]
        iota = const[:, C_IOTA:C_IOTA + P]
        ropec = const[:, C_ROPEC:C_ROPEC + P].rearrange("p (t f) -> p t f", t=4)
        ropes = const[:, C_ROPES:C_ROPES + P].rearrange("p (t f) -> p t f", t=4)

        PS = ctx.enter_context(nc.psum_tensor("PS", [P, 8 * 512], F32))

        def bank(b, a=0, e=512):
            return PS[:, b * 512 + a:b * 512 + e]

        def two_banks(b, n):
            return PS[:, b * 512:(b + 2) * 512].rearrange("p (b n) -> p b n", b=2)[:, :, 0:n]

        slot_full = [sem(f"slot_full{i}") for i in range(RING)]
        setup = sem("setup")
        layer_free = sem("layer_free")
        params = sem("params")
        ln1_rows = sem("ln1_rows")
        ln2_rows = sem("ln2_rows")
        kv_stored = sem("kv_stored")
        cond_ready = sem("cond_ready")
        mod_full = sem("mod_full")
        mod_ready = sem("mod_ready")
        diag_ready = sem("diag_ready")
        row_full = sem("row_full")
        row_ready = sem("row_ready")
        var_ready = sem("var_ready")
        std_ready = sem("std_ready")
        xn_ready = sem("xn_ready")
        xT_full = sem("xT_full")
        hT_ready = sem("hT_ready")
        z_full = sem("z_full")
        z_ready = sem("z_ready")
        blk_ready = sem("blk_ready")
        tr_full = sem("tr_full")
        tr_ready = sem("tr_ready")
        f1_full = sem("f1_full")
        f1_ready = sem("f1_ready")
        f2_full = sem("f2_full")
        f2_ready = sem("f2_ready")
        lam_sum = sem("lam_sum")
        lam_exp = sem("lam_exp")
        qcur_ready = sem("qcur_ready")
        s_full = sem("s_full")
        tail_full = sem("tail_full")
        mx_ready = sem("mx_ready")
        p_ready = sem("p_ready")
        w_ready = sem("w_ready")
        t_full = sem("t_full")
        pT_ready = sem("pT_ready")
        o_full = sem("o_full")
        o_ready = sem("o_ready")
        dn_ready = sem("dn_ready")
        br_full = sem("br_full")
        br_ready = sem("br_ready")
        mg_full = sem("mg_full")
        sg_ready = sem("sg_ready")
        mg_done = sem("mg_done")
        out_full = sem("out_full")
        out_done = sem("out_done")
        q_full = sem("q_full")
        q_ready = sem("q_ready")
        qcur2_ready = sem("qcur2_ready")
        sc_full = sem("sc_full")
        score_ready = sem("score_ready")
        best_ready = sem("best_ready")
        exp_ready = sem("exp_ready")
        idx_ready = sem("idx_ready")
        idxT_full = sem("idxT_full")
        idxT_ready = sem("idxT_ready")
        eq_ready = sem("eq_ready")
        oh_ready = sem("oh_ready")
        quad_full = sem("quad_full")
        quad_ready = sem("quad_ready")
        g_stored = [sem(f"g_stored{i}") for i in range(2)]
        hhi_ready = sem("hhi_ready")
        hlo_ready = sem("hlo_ready")
        hi_ready = sem("hi_ready")
        split_ready = sem("split_ready")
        h_full = sem("h_full")
        gelu_ready = sem("gelu_ready")
        g_loaded = [sem(f"g_loaded{i}") for i in range(2)]
        W_ready = sem("W_ready")
        v_full = sem("v_full")
        v_done = sem("v_done")
        layer_done = sem("layer_done")
        y_stored = sem("y_stored")

        block = ctx.enter_context(nc.Block())

        def wait_slot(eng, l, n, extra=0):
            eng.wait_ge(slot_full[n % RING], 16 * (l * TURNS + n // RING + 1 + extra))

        last_use = [(mod_full, N_MOD, k + 1) for k in range(8)]
        last_use += [(z_full, N_Z, 5 * (k + 1)) for k in range(11)]
        last_use += [(f1_full, N_F, N_F)] * 2
        last_use += [(mod_full, N_MOD, k + 1) for k in range(8, 24)]
        for n in range(3):
            for half in range(2):
                done = 8 * n + 4 * half
                last_use += [(mg_full, N_MG, done + 4), (mg_full, N_MG, done + 2), (mg_full, N_MG, done + 4)]
        last_use += [(out_full, N_OUT, 5 * (k + 1)) for k in range(4)]
        last_use += [(q_full, N_Q, 2 * (k + 1)) for k in range(4)]
        last_use += [(sc_full, NT, NT)]
        assert len(last_use) == PEER

        def turn_group(u, m):
            return u if u < 4 else 4 + 2 * (u - 4) + m

        @block.sync
        def _(sp):
            def load(l, n):
                sp.dma_start(ring[:, n % RING, :],
                             weights[bass.ds(l * PER_LAYER + n, 1)].rearrange("o p f -> (o p) f")
                             ).then_inc(slot_full[n % RING], 16)

            with sp.Fori(0, LAYERS) as l:
                for n in range(PEER + RING):
                    if n < RING:
                        if n == 0:
                            sp.wait_ge(layer_free, l + 1)
                    else:
                        s, per, value = last_use[n - RING]
                        sp.wait_ge(s, layer_at(l, per, value))
                    load(l, n)
                sp.wait_ge(h_full, layer_at(l, 2 * NB, 2))
                load(l, PEER + RING)
                with sp.Fori(0, NB // 2 - 2) as i:
                    for u in range(4):
                        b2 = u // 2
                        if u % 2 == 0:
                            sp.wait_ge(h_full, l * (2 * NB) + i * 4 + 2 * (b2 + 2))
                        else:
                            sp.wait_ge(v_full, l * N_V + i * 20 + 10 * (b2 + 1))
                        sp.dma_start(ring[:, (RING + 1 + u) % RING, :],
                                     weights[bass.ds(l * PER_LAYER + i * 4 + (PEER + RING + 1 + u), 1)]
                                     .rearrange("o p f -> (o p) f")
                                     ).then_inc(slot_full[(RING + 1 + u) % RING], 16)
                for s in range(2 * NB - 3, 2 * NB):
                    old = s - RING
                    if old % 2:
                        sp.wait_ge(h_full, layer_at(l, 2 * NB, 2 * ((old + 1) // 2 + 1)))
                    else:
                        sp.wait_ge(v_full, layer_at(l, N_V, 10 * (old // 2)))
                    load(l, PEER + s)
            sp.wait_ge(layer_done, LAYERS)
            sp.dma_start(y.rearrange("t p d -> p t d"), x[:, :, :]).then_inc(y_stored, 16)
            sp.wait_ge(y_stored, 16)

        @block.gpsimd
        def _(pool):
            pool.dma_start(const[:, :], consts).then_inc(setup, 16)
            pool.dma_start(x[:, :, :], x_in.rearrange("t p d -> p t d")).then_inc(setup, 16)
            pool.dma_start(cnd[:, :, :], cond.rearrange("p (k s) -> p k s", s=2)).then_inc(setup, 16)
            with pool.Fori(0, LAYERS) as l:
                def one(ap):
                    return ap[bass.ds(l, 1)]
                pool.wait_ge(layer_free, l + 1)
                pool.dma_start(bc[:, :], one(bcol).rearrange("o p n -> (o p) n")).then_inc(params, 16)
                pool.dma_start(row[:, :], one(rows).rearrange("o n -> (o n)").partition_broadcast(P)).then_inc(params, 16)
                pool.dma_start(ckb[:, :], one(cache_k).rearrange("o p n -> (o p) n")).then_inc(params, 16)
                pool.dma_start(V[:, 5, :], one(cache_v).rearrange("o p n -> (o p) n")).then_inc(params, 16)
                pool.wait_ge(blk_ready, layer_at(l, N_BLK, 2))
                pool.dma_start(one(new_gk).rearrange("o p n -> (o p) n"), zk[:, 0, :]).then_inc(kv_stored, 16)
                pool.wait_ge(z_ready, layer_at(l, N_Z, 5 * 9))
                pool.dma_start(one(new_dk).rearrange("o p n -> (o p) n"), z[:, 0, 0, :]).then_inc(kv_stored, 16)
                pool.dma_start(one(new_dv).rearrange("o p n -> (o p) n"), V[:, 0, 0:512]).then_inc(kv_stored, 16)
                pool.dma_start(one(new_gv).rearrange("o p n -> (o p) n"), V[:, 0, 512:640]).then_inc(kv_stored, 16)
                pool.wait_ge(o_ready, layer_at(l, N_UNIT, N_UNIT))
                pool.dma_start(lnr[:, :, :], lnrows[bass.ds(l * 2, 1)].rearrange("o a n -> (o a n)")
                               .partition_broadcast(P)).then_inc(ln1_rows, 16)
                with pool.Fori(0, NT) as t:
                    with pool.Fori(0, P // 16) as i:
                        for u in range(4):
                            pool.wait_ge(eq_ready, l * N_QUAD + t * QUADS + i * 4 + (u + 1))
                            g = idxT[:, 2, bass.ds(i * 16 + 4 * u, 4)].unsqueeze(2).broadcast_to([P, 4, P])
                            nc.gpsimd.tensor_tensor(ohB[:, u, :, :], ohE[:, u, :, :], g, ALU.mult).then_inc(oh_ready, 1)
                pool.wait_ge(setup, 48)
                pool.wait_ge(hlo_ready, l + 1)

                def load_g(b, u):
                    pool.dma_start(G[:, u, :, :, :].rearrange("p g j t -> p (g j t)"),
                                   gate_matrix[bass.ds(b, 1)].rearrange("o p n -> (o p) n")
                                   ).then_inc(g_loaded[u], 16)
                load_g(0, 0)
                load_g(1, 1)
                with pool.Fori(0, (NB - 2) // 2) as i:
                    for u in range(2):
                        pool.wait_ge(W_ready, l * N_W + i * 4 + 2 * (u + 1))
                        load_g(i * 2 + (2 + u), u)
                pool.wait_ge(v_done, layer_at(l, N_V, N_V))
                pool.dma_start(lnr2[:, :, :], lnrows[bass.ds(l * 2 + 1, 1)].rearrange("o a n -> (o a n)")
                               .partition_broadcast(P)).then_inc(ln2_rows, 16)
            pool.wait_ge(kv_stored, 64 * LAYERS)

        @block.tensor
        def _(pe):
            mm = nc.tensor.matmul

            def group(out, pairs):
                for n, (a, b) in enumerate(pairs):
                    last = mm(out, a, b, start=(n == 0), stop=(n == len(pairs) - 1))
                return last

            def turn(out, in_):
                return nc.tensor.transpose(out, in_, ident)

            with pe.Fori(0, LAYERS) as l:
                def modulation(slot, out, extra=0):
                    wait_slot(pe, l, slot, extra)
                    w = ring[:, slot % RING, :].rearrange("p (k n) -> p k n", k=KC)
                    for sub in range(2):
                        last = group(out[:, 2 * sub:2 * sub + 2],
                                     [(w[:, c, sub * P:sub * P + P], cnds[:, c, :]) for c in range(KC)])
                    last.then_inc(mod_full, 1)

                pe.wait_ge(cond_ready, 1)
                for k in range(8):
                    modulation(MOD1 + k, bank(0, 4 * k, 4 * k + 4))

                def ln_turn(part, src):
                    for t in range(NT):
                        pe.wait_ge(xn_ready, layer_at(l, 10, 5 * part + t + 1))
                        for h in range(2):
                            j = 10 * part + 2 * t + h
                            if 2 * t + h >= 4:
                                pe.wait_ge(hT_ready, layer_at(l, N_HT, j - 3))
                            for c in range(4):
                                last = turn(bank(4 + j % 4, c * P, c * P + P), src[:, t % 2, (4 * h + c) * P:(4 * h + c + 1) * P])
                            last.then_inc(xT_full, 1)

                ln_turn(0, xn)

                pe.wait_ge(hT_ready, layer_at(l, N_HT, 10))

                def project(k):
                    wait_slot(pe, l, GQ + k)
                    w = ring[:, (GQ + k) % RING, :].rearrange("p (k n) -> p k n", k=KC)
                    for t in range(NT):
                        j = 5 * k + t
                        if j >= 4:
                            pe.wait_ge(z_ready, layer_at(l, N_Z, j - 3))
                        group(bank(j % 4, 0, 256), [(hT[:, c, t * P:t * P + P], w[:, c, :])
                                                    for c in range(KC)]).then_inc(z_full, 1)

                tr = [0]

                def qk_turn(ins):
                    j = tr[0]
                    if j >= 2:
                        pe.wait_ge(tr_ready, layer_at(l, N_TR, j - 1))
                    for c, a in enumerate(ins):
                        last = turn(bank(4 + j % 2, c * P, c * P + P), a)
                    last.then_inc(tr_full, 1)
                    tr[0] += 1

                for k in range(5):
                    project(k)
                pe.wait_ge(blk_ready, layer_at(l, N_BLK, 1))
                for t in range(NT):
                    qk_turn([z[:, 0, t, c * P:c * P + P] for c in range(4)])
                pe.wait_ge(blk_ready, layer_at(l, N_BLK, 2))
                pe.wait_ge(params, layer_at(l, 16 * PARAM_DMAS, 16 * PARAM_DMAS))
                qk_turn([zk[:, t, :] for t in range(4)])
                qk_turn([zk[:, 4, :], ckb[:, 512:640]])
                for k in range(5, 7):
                    project(k)
                pe.wait_ge(blk_ready, layer_at(l, N_BLK, 3))
                for t in range(NT):
                    qk_turn([z[:, 1, t, c * P:c * P + P] for c in range(4)])
                for k in range(7, 9):
                    project(k)
                pe.wait_ge(blk_ready, layer_at(l, N_BLK, 4))
                for t in range(NT):
                    qk_turn([z[:, 0, t, c * P:c * P + P] for c in range(4)])
                qk_turn([ckb[:, c * P:c * P + P] for c in range(4)])
                for k in range(9, 11):
                    project(k)

                pe.wait_ge(z_ready, layer_at(l, N_Z, N_Z))
                pe.wait_ge(tr_ready, layer_at(l, N_TR, N_TR))

                def dft_tokens(k):
                    if k >= 1:
                        pe.wait_ge(f1_ready, layer_at(l, N_F, k))
                    if k == 0:
                        for g in range(4):
                            b = 4 + g // 2
                            last = mm(bank(b, 256 * (g % 2), 256 * (g % 2) + 256), z[:, 1, 0, g * P:g * P + P],
                                      const[:, C_COS:C_COS + 256], start=True, stop=True)
                    else:
                        g = k - 1
                        for b in range(2):
                            if k == 1:
                                wait_slot(pe, l, DFT + b)
                            w = ring[:, (DFT + b) % RING, :].rearrange("p (t n) -> p t n", t=4)
                            last = group(bank(4 + b), [(z[:, 1, 1 + t, g * P:g * P + P], w[:, t, :]) for t in range(4)])
                    last.then_inc(f1_full, 1)

                def dft_channels(k):
                    pe.wait_ge(f1_ready, layer_at(l, N_F, k + 1))
                    if k >= 2:
                        pe.wait_ge(f2_ready, layer_at(l, N_F, k - 1))
                    b = 6 + k % 2
                    if k == 0:
                        a = acs[:, 0, :, :].rearrange("p a (g n) -> p (a g) n", n=256)
                        rc, rs = a[:, :, 0:P], a[:, :, P:256]
                    else:
                        rc, rs = acs[:, k % 2, 0, :], acs[:, k % 2, 1, :]
                    group(bank(b), [(const[:, C_COS:C_COS + P], rc),
                                    (const[:, C_NSIN:C_NSIN + P], rs)]).then_inc(f2_full, 1)

                dft_tokens(0)
                for k in range(1, 5):
                    dft_tokens(k)
                    dft_channels(k - 1)
                dft_channels(4)
                pe.wait_ge(f2_ready, layer_at(l, N_F, N_F))

                def attend(t, nk):
                    base = l * N_UNIT + t * UNITS
                    base_t = l * N_T + t * TURN_GROUPS
                    k0 = 0 if nk == 1 else P
                    pe.wait_ge(qcur_ready, l * NT + t + 1)

                    def scores(u):
                        if u >= 2:
                            pe.wait_ge(p_ready, base + u - 1)
                        kc = u if u < 4 else 4
                        s0 = 1536 * (u % 2)
                        pieces = [(0, 0, P), (1, 0, P)]
                        if nk == 5:
                            pieces = [(0, 512, 640), (0, 0, 512), (1, 384, 640), (1, 0, 384)]
                        for m, a, e in pieces:
                            r = slice(64 * m, 64 * m + 64)
                            if nk == 5 and (m, a) == (1, 0):
                                pe.wait_ge(tail_full, (l * (NT - 1) + t - 1) * UNITS + u + 1)
                            last = mm(PS[:, s0 + 640 * m + a:s0 + 640 * m + e], qcur[r, u, :],
                                      kT[r, kc, k0 + a:k0 + e], start=True, stop=True)
                            if nk == 5 and (m, a) == (0, 512):
                                last.then_inc(tail_full, 1)
                        last.then_inc(s_full, 1)

                    def turn_probs(u, m):
                        g = turn_group(u, m)
                        if m == 0:
                            pe.wait_ge(w_ready, base + u + 1)
                            if u >= 1 or nk == 5:
                                pe.wait_ge(o_ready, base + u)
                        if g >= 1:
                            pe.wait_ge(pT_ready, base_t + g)
                        src = wd[:, u % 2, :] if u < 4 else prob[:, u % 2, m, :]
                        for k in range(nk):
                            last = turn(PS[:, 3072 + k * P:3072 + k * P + P], src[:, k * P:k * P + P])
                        last.then_inc(t_full, 1)

                    def values(u):
                        maps = range(1 if u < 4 else 2)
                        pe.wait_ge(pT_ready, base_t + turn_group(u, maps[-1]) + 1)
                        kt = [0] if nk == 1 else list(range(1, 6))
                        for m in maps:
                            c = slice(u * P, u * P + P) if u < 4 else slice(512 + 64 * m, 576 + 64 * m)
                            n = c.stop - c.start
                            last = group(bank(7, P + n * m, P + n * m + n),
                                         [(pT[:, u % 2, m, i, :], V[:, k, c]) for i, k in enumerate(kt)])
                        last.then_inc(o_full, 1)

                    scores(0)
                    if nk == 5:
                        for k in range(4):
                            modulation(MOD2 + k, bank(6, 4 * k, 4 * k + 4), t - 1)
                    for u in range(UNITS):
                        if u + 1 < UNITS:
                            scores(u + 1)
                        for m in range(1 if u < 4 else 2):
                            turn_probs(u, m)
                        values(u)

                attend(0, 1)
                with pe.Fori(1, NT) as t:
                    attend(t, 5)

                for w in range(2):
                    pe.wait_ge(diag_ready, layer_at(l, 2, w + 1))
                    for s in range(2):
                        for h in range(2):
                            last = mm(bank(4 * w + 2 * s + h), const[:, C_ONE:C_ONE + P], diag[:, w, s, 4 * h:4 * h + 4, :],
                                      start=True, stop=True)
                    last.then_inc(row_full, 1)
                pe.wait_ge(row_ready, layer_at(l, 2, 2))

                pe.wait_ge(dn_ready, l + 1)
                for t in range(NT):
                    for h in range(2):
                        j = 2 * t + h
                        if j >= 4:
                            pe.wait_ge(br_ready, layer_at(l, N_BR, j - 3))
                        for c in range(4):
                            last = turn(bank(j % 4, c * P, c * P + P), oall[:, t, (4 * h + c) * P:(4 * h + c + 1) * P])
                        last.then_inc(br_full, 1)
                pe.wait_ge(br_ready, layer_at(l, N_BR, N_BR))

                for n in range(3):
                    for half in range(2):
                        slot = MERGE + 6 * n + 3 * half
                        wb = ring[:, slot % RING, :].rearrange("p (c n) -> p c n", c=4)
                        wait_slot(pe, l, slot)
                        for dc in range(4):
                            j = 8 * n + 4 * half + dc
                            gs = slot + 1 + dc // 2
                            if dc % 2 == 0:
                                wait_slot(pe, l, gs)
                            wg = ring[:, gs % RING, :].rearrange("p (c n) -> p c n", c=KC)
                            if j >= 2:
                                pe.wait_ge(mg_done, layer_at(l, N_MG, j - 1))
                            b = 4 * (j % 2)
                            g0 = (dc % 2) * P
                            for th in range(2):
                                ts = slice(th * TH, th * TH + TH)
                                group(bank(b + 2 + th, 0, TH), [(wg[:, c, g0:g0 + P], hT[:, c, ts]) for c in range(KC)])
                            for th in range(2):
                                ts = slice(th * TH, th * TH + TH)
                                src = [fT[:, c, ts] if n == 2 else brT[:, 4 * n + c, ts] for c in range(4)]
                                last = group(bank(b + th, 0, TH),
                                             [(wb[:, c, dc * P:dc * P + P], src[c]) for c in range(4)])
                            last.then_inc(mg_full, 1)
                pe.wait_ge(mg_done, layer_at(l, N_MG, N_MG))

                for k in range(4):
                    wait_slot(pe, l, OUT + k)
                    w = ring[:, (OUT + k) % RING, :].rearrange("p (c n) -> p c n", c=KC)
                    for t in range(NT):
                        j = 5 * k + t
                        if j >= 4:
                            pe.wait_ge(out_done, layer_at(l, N_OUT, j - 3))
                        group(bank(j % 4, 0, 256), [(mT[:, c, t * P:t * P + P], w[:, c, :])
                                                    for c in range(KC)]).then_inc(out_full, 1)

                ln_turn(1, xn2)

                pe.wait_ge(hT_ready, layer_at(l, N_HT, N_HT))
                for k in range(4):
                    wait_slot(pe, l, WQ + k)
                    w = ring[:, (WQ + k) % RING, :].rearrange("p (c n) -> p c n", c=KC)
                    for hh in range(2):
                        j = 2 * k + hh
                        if j >= 2:
                            pe.wait_ge(q_ready, layer_at(l, N_Q, j - 1))
                        for th in range(2):
                            last = group(bank(2 * (j % 2) + th, 0, TH),
                                         [(w[:, c, hh * P:hh * P + P], hT[:, c, th * TH:th * TH + TH])
                                          for c in range(KC)])
                        last.then_inc(q_full, 1)

                keys = ring[:, SUB % RING, 0:1024].rearrange("p (h n) -> p h n", h=HEADS)

                def score_tile(t):
                    pe.wait_ge(qcur2_ready, l * NT + t + 1)
                    for h in range(HEADS):
                        for p in range(2):
                            r = slice(64 * p, 64 * p + 64)
                            last = mm(PS[:, 1024 * p + h * P:1024 * p + h * P + P], qcur2[r, h, :], keys[r, h, :],
                                      start=True, stop=True)
                    last.then_inc(sc_full, 1)

                def expand_tile(t, final=False):
                    pe.wait_ge(idx_ready, l * NT + t + 1)
                    for n in range(3):
                        last = turn(bank(4, n * P, n * P + P), idx[:, n, :])
                    last.then_inc(idxT_full, 1)
                    if not final:
                        score_tile(t + 1)
                    with pe.Fori(0, P // 16) as i:
                        for u in range(4):
                            pe.wait_ge(oh_ready, l * N_QUAD + t * QUADS + i * 4 + (u + 1))
                            for k in range(4):
                                last = mm(bank(4 + u, k * P, k * P + P), ohA[:, u, k, :], ohB[:, u, k, :],
                                          start=True, stop=True)
                            last.then_inc(quad_full, 1)

                wait_slot(pe, l, SUB)
                score_tile(0)
                with pe.Fori(0, NT - 1) as t:
                    expand_tile(t)
                expand_tile(NT - 1, final=True)

                pe.wait_ge(quad_ready, layer_at(l, N_QUAD, N_QUAD))
                pe.wait_ge(hlo_ready, l + 1)

                def three(out, hi, lo, mhi, mlo, first, final):
                    mm(out, hi, mhi, start=first, stop=False)
                    mm(out, hi, mlo, start=False, stop=False)
                    return mm(out, lo, mhi, start=False, stop=final)

                def up(b, s, wait_gelu=True):
                    uh = ring_hi[:, s, :].rearrange("p (c j n) -> p c j n", c=KC, j=2)
                    ul = ring_lo[:, s, :].rearrange("p (c j n) -> p c j n", c=KC, j=2)
                    for j in range(2):
                        if wait_gelu:
                            pe.wait_ge(gelu_ready, l * (2 * NB) + b * 2 + (j - 1))
                        for c in range(KC):
                            for th in range(2):
                                ts = slice(th * TH, th * TH + TH)
                                last = three(bank(2 * j + th, 0, TH), uh[:, c, j, :], ul[:, c, j, :],
                                             hT_hi[:, c, ts], hT_lo[:, c, ts], c == 0, c == KC - 1)
                        last.then_inc(h_full, 1)

                def down(b, s, par, first=False):
                    vh = ring_hi[:, s, :].rearrange("p (j n) -> p j n", j=2)
                    vl = ring_lo[:, s, :].rearrange("p (j n) -> p j n", j=2)
                    pe.wait_ge(W_ready, l * N_W + b * 2 + 2)
                    for n in range(10):
                        t, dh = n // 2, n % 2
                        if not (first and n < 4):
                            pe.wait_ge(v_done, l * N_V + b * 10 + (n - 3))
                        for j in range(2):
                            last = three(bank(4 + (10 * par + n) % 4), W_hi[:, par, j, t * P:t * P + P],
                                         W_lo[:, par, j, t * P:t * P + P], vh[:, j, dh * 512:dh * 512 + 512],
                                         vl[:, j, dh * 512:dh * 512 + 512], j == 0, j == 1)
                        last.then_inc(v_full, 1)

                def split_wait(n):
                    pe.wait_ge(split_ready, l * N_SPLIT + n + 1)

                split_wait(0)
                up(0, PEER % RING, wait_gelu=False)
                split_wait(1)
                up(1, 1)
                split_wait(2)
                down(0, 2, 0, first=True)
                split_wait(3)
                up(2, 3)
                split_wait(4)
                down(1, 0, 1)
                with pe.Fori(1, NB // 2 - 1) as i:
                    split_wait(i * 4 + 1)
                    up(i * 2 + 1, 1)
                    split_wait(i * 4 + 2)
                    down(i * 2, 2, 0)
                    split_wait(i * 4 + 3)
                    up(i * 2 + 2, 3)
                    split_wait(i * 4 + 4)
                    down(i * 2 + 1, 0, 1)
                split_wait(2 * NB - 3)
                up(NB - 1, 1)
                split_wait(2 * NB - 2)
                down(NB - 2, 2, 0)
                split_wait(2 * NB - 1)
                down(NB - 1, 3, 1)

        @block.scalar
        def _(act):
            A = nc.scalar.activation
            act.wait_ge(setup, 48)
            A(cnds[:, :, :], cnd[:, :, :], ACT.Silu).then_inc(cond_ready, 1)

            with act.Fori(0, LAYERS) as l:
                def root(k, n):
                    act.wait_ge(var_ready, layer_at(l, N_STD, k + 1))
                    A(std[:, 0:n], var[:, 0:n], ACT.Sqrt).then_inc(std_ready, 1)

                def modulate(part):
                    for t in range(NT):
                        s = 0 if t == 0 else 1
                        for h in range(2):
                            j = 10 * part + 2 * t + h
                            act.wait_ge(xT_full, layer_at(l, N_HT, j + 1))
                            for c in range(4):
                                k = 4 * h + c
                                q = 24 * part + k
                                last = A(hT[:, k, t * P:t * P + P], bank(4 + j % 4, c * P, c * P + P), ACT.Identity,
                                         bias=modc[:, q, s:s + 1], scale=modc[:, q + 8, s:s + 1])
                            last.then_inc(hT_ready, 1)

                act.wait_ge(lam_sum, l + 1)
                A(lamw[:, 2:4], lamw[:, 0:2], ACT.Exp).then_inc(lam_exp, 1)

                root(0, NT)
                act.wait_ge(mod_ready, layer_at(l, 2, 1))
                modulate(0)

                def project(k):
                    for t in range(NT):
                        j = 5 * k + t
                        act.wait_ge(z_full, layer_at(l, N_Z, j + 1))
                        src = bank(j % 4, 0, 256)
                        if k < 2:
                            dst = z[:, 0, t, :].rearrange("p (c v d) -> p c v d", c=4, v=2)[:, :, k, :]
                            last = nc.scalar.copy(dst, src.rearrange("p (c d) -> p c d", c=4))
                        elif k == 2:
                            nc.scalar.copy(zk[:, t, :], src[:, 0:P])
                            last = nc.scalar.copy(V[:, t, 512:640], src[:, P:256])
                        else:
                            n = (k - 3) // 2
                            cols = slice(256 * ((k - 3) % 2), 256 * ((k - 3) % 2) + 256)
                            dst = [z[:, 1, t, cols], z[:, 0, t, cols], V[:, t, cols], z[:, 1, t, cols]][n]
                            last = nc.scalar.copy(dst, src)
                        last.then_inc(z_ready, 1)

                tr = [0]

                def qk_out(dst, n):
                    j = tr[0]
                    act.wait_ge(tr_full, layer_at(l, N_TR, j + 1))
                    src = bank(4 + j % 2, 0, n * P)
                    if dst.ndim == 3:
                        src = src.rearrange("p (c n) -> p c n", c=n)
                    nc.scalar.copy(dst, src).then_inc(tr_ready, 1)
                    tr[0] += 1

                for k in range(3):
                    project(k)
                root(1, 50)
                for k in range(3, 5):
                    project(k)
                for t in range(NT):
                    qk_out(qT[:, 4:8, t * P:t * P + P], 4)
                qk_out(kT[:, 4, 0:512], 4)
                qk_out(kT[:, 4, 512:768], 2)
                for k in range(5, 7):
                    project(k)
                for t in range(NT):
                    qk_out(qT[:, 0:4, t * P:t * P + P], 4)
                for k in range(7, 9):
                    project(k)
                for t in range(NT + 1):
                    qk_out(kT[:, 0:4, t * P:t * P + P], 4)
                for k in range(9, 11):
                    project(k)

                def dft_out1(k):
                    act.wait_ge(f1_full, layer_at(l, N_F, k + 1))
                    nc.scalar.copy(acs[:, k % 2, :, :].rearrange("p a n -> p (a n)"),
                                   PS[:, 2048:3072]).then_inc(f1_ready, 1)

                def dft_out2(k):
                    act.wait_ge(f2_full, layer_at(l, N_F, k + 1))
                    src = bank(6 + k % 2)
                    if k == 0:
                        nc.scalar.copy(fT[:, :, 0:P], src.rearrange("p (g n) -> p g n", g=4)).then_inc(f2_ready, 1)
                    else:
                        nc.scalar.copy(fT[:, k - 1, P:T], src).then_inc(f2_ready, 1)

                dft_out1(0)
                for k in range(1, 5):
                    dft_out1(k)
                    dft_out2(k - 1)
                dft_out2(4)

                def attend(t, nk):
                    base = l * N_UNIT + t * UNITS
                    base_t = l * N_T + t * TURN_GROUPS
                    w = nk * P
                    cols = slice(0, P) if nk == 1 else bass.ds(t * P, P)
                    nc.scalar.copy(qcur[:, :, :], qT[:, :, cols]).then_inc(qcur_ready, 1)

                    def exps(u):
                        act.wait_ge(mx_ready, base + u + 1)
                        if u >= 2:
                            act.wait_ge(t_full, base_t + turn_group(u - 2, 0 if u < 6 else 1) + 1)
                        s0 = 1536 * (u % 2)
                        for m in range(2):
                            last = A(prob[:, u % 2, m, 0:w], PS[:, s0 + m * 640:s0 + m * 640 + w], ACT.Exp,
                                     bias=nbias[:, u % 2, m:m + 1], scale=SCALE, accum_out=rsum[:, u % 2, m:m + 1])
                        last.then_inc(p_ready, 1)

                    def probs_out(u, m):
                        act.wait_ge(t_full, base_t + turn_group(u, m) + 1)
                        if u >= 2 and m == 0:
                            act.wait_ge(o_full, base + u - 1)
                        nc.scalar.copy(pT[:, u % 2, m, 0:nk, :].rearrange("p k n -> p (k n)"),
                                       PS[:, 3072:3072 + w]).then_inc(pT_ready, 1)

                    exps(0)
                    for u in range(UNITS):
                        for m in range(1 if u < 4 else 2):
                            probs_out(u, m)
                        if u + 1 < UNITS:
                            exps(u + 1)
                    act.wait_ge(o_full, base + UNITS)

                attend(0, 1)
                with act.Fori(1, NT) as t:
                    attend(t, 5)

                for w, dst in enumerate((gate1, gate2)):
                    act.wait_ge(row_full, layer_at(l, 2, w + 1))
                    nc.scalar.copy(dst[:, :, :].rearrange("p s n -> p (s n)"),
                                   PS[:, 2048 * w:2048 * w + 2048]).then_inc(row_ready, 1)
                root(2, 20)
                for t in range(NT):
                    for h in range(2):
                        j = 2 * t + h
                        act.wait_ge(br_full, layer_at(l, N_BR, j + 1))
                        nc.scalar.copy(brT[:, 4 * h:4 * h + 4, t * P:t * P + P],
                                       bank(j % 4).rearrange("p (c n) -> p c n", c=4)).then_inc(br_ready, 1)

                for j in range(N_MG):
                    act.wait_ge(mg_full, layer_at(l, N_MG, j + 1))
                    if j >= 2:
                        act.wait_ge(mg_done, layer_at(l, N_MG, j - 1))
                    A(sg[:, j % 2, :].rearrange("p (h n) -> p h n", h=2), two_banks(4 * (j % 2) + 2, TH),
                      ACT.Sigmoid).then_inc(sg_ready, 1)

                root(3, NT)
                root(4, NT)
                act.wait_ge(mod_ready, layer_at(l, 2, 2))
                modulate(1)

                for j in range(N_Q):
                    act.wait_ge(q_full, layer_at(l, N_Q, j + 1))
                    nc.scalar.copy(qT2[:, j, :].rearrange("p (h n) -> p h n", h=2),
                                   two_banks(2 * (j % 2), TH)).then_inc(q_ready, 1)
                act.drain()

                def query_tile(t):
                    cols = slice(0, P) if isinstance(t, int) else bass.ds(t * P, P)
                    nc.scalar.copy(qcur2[:, :, :], qT2[:, :, cols]).then_inc(qcur2_ready, 1)

                def expand_tile(t, final=False):
                    act.wait_ge(sc_full, l * NT + t + 1)
                    nc.scalar.copy(score[:, :, :].rearrange("p s n -> p (s n)"), PS[:, 0:2048]).then_inc(score_ready, 1)
                    if not final:
                        query_tile(t + 1)
                    act.wait_ge(best_ready, l * NT + t + 1)
                    A(pw[:, :, :], pv[:, :, :], ACT.Exp).then_inc(exp_ready, 1)
                    act.wait_ge(idxT_full, l * NT + t + 1)
                    nc.scalar.copy(idxT[:, :, :].rearrange("p a n -> p (a n)"), bank(4, 0, 3 * P)).then_inc(idxT_ready, 1)
                    for half in range(2):
                        st = stg[:, half, :, :, :].rearrange("p b j t -> p (b j) t")
                        with act.Fori(0, 4) as i:
                            for u in range(4):
                                act.wait_ge(quad_full, l * N_QUAD + t * QUADS + i * 4 + (16 * half + u + 1))
                                nc.scalar.copy(st[:, :, bass.ds(i * 16 + 4 * u, 4)],
                                               bank(4 + u).rearrange("p (t j) -> p j t", t=4)).then_inc(quad_ready, 1)
                        act.wait_ge(quad_ready, l * N_QUAD + t * QUADS + 16 * (half + 1))
                        act.dma_start(
                            gate_matrix.rearrange("b p (g n) -> p b g n", g=2 * NT)[:, :, bass.ds(t * 2 + half, 1), :]
                            .rearrange("p b g n -> p b (g n)"),
                            stg[:, half, :, :, :].rearrange("p b j t -> p b (j t)")).then_inc(g_stored[half], 16)
                    for half in range(2):
                        act.wait_ge(g_stored[half], 16 * (l * NT + t + 1))

                wait_slot(act, l, SUB)
                query_tile(0)
                with act.Fori(0, NT - 1) as t:
                    expand_tile(t)
                expand_tile(NT - 1, final=True)

                nc.scalar.copy(hT_hi[:, :, :], hT[:, :, :]).then_inc(hhi_ready, 1)

                def split_hi(s, n):
                    act.wait_ge(slot_full[s], 16 * (l * TURNS + n + 1))
                    nc.scalar.copy(ring_hi[:, s, :], ring[:, s, :]).then_inc(hi_ready, 1)

                def gelu(b, j, buf_wait=True):
                    act.wait_ge(h_full, l * (2 * NB) + b * 2 + (j + 1))
                    if buf_wait:
                        act.wait_ge(W_ready, l * N_W + b * 2 + (j - 1))
                    A(act_g[:, j, :].rearrange("p (h n) -> p h n", h=2), two_banks(2 * j, TH),
                      ACT.Gelu).then_inc(gelu_ready, 1)

                first_turn = PEER // RING
                split_hi(0, first_turn)
                split_hi(1, first_turn)
                split_hi(2, first_turn)
                gelu(0, 0, False)
                gelu(0, 1, False)
                with act.Fori(0, NB // 2 - 1) as i:
                    for u in range(2):
                        gelu(i * 2 + (u + 1), 0)
                        s = (3 + 2 * u) % RING
                        split_hi(s, i + (first_turn + (3 + 2 * u) // RING))
                        gelu(i * 2 + (u + 1), 1)
                        s = (4 + 2 * u) % RING
                        split_hi(s, i + (first_turn + (4 + 2 * u) // RING))
                gelu(NB - 1, 0)
                split_hi(3, first_turn + NB // 2 - 1)
                gelu(NB - 1, 1)
                root(5, NT)

        @block.vector
        def _(dve):
            tt, ts_, copy = nc.vector.tensor_tensor, nc.vector.tensor_scalar, nc.vector.tensor_copy
            stt = nc.vector.scalar_tensor_tensor
            reduce = nc.vector.tensor_reduce
            dve.wait_ge(setup, 48)
            copy(lamw[:, 8:10], const[:, 0:2]).then_inc(layer_free, 1)

            with dve.Fori(0, LAYERS) as l:
                def root_wait(k):
                    dve.wait_ge(std_ready, layer_at(l, N_STD, k + 1))

                def statistics():
                    for t in range(NT):
                        for h in range(2):
                            nc.vector.bn_stats(stats[:, t, h, :], x[:, t, 512 * h:512 * h + 512])
                    dve.drain()
                    for t in range(NT):
                        nc.vector.bn_aggr(mv[:, t, :], stats[:, t, :, :].rearrange("p a b -> p (a b)"))
                    dve.drain()
                    ts_(var[:, 0:NT], mv[:, :, 1], EPS, None, ALU.add).then_inc(var_ready, 1)

                def ln_out(part, k, dst, src_ready=None):
                    statistics()
                    root_wait(k)
                    nc.vector.reciprocal(rstd[:, 0:NT], std[:, 0:NT])
                    dve.drain()
                    for t in range(NT):
                        if t >= 2:
                            dve.wait_ge(xT_full, layer_at(l, N_HT, 10 * part + 2 * (t - 1)))
                        ts_(dst[:, t % 2, :], x[:, t, :], mv[:, t, 0:1], rstd[:, t:t + 1],
                            ALU.subtract, ALU.mult).then_inc(xn_ready, 1)

                def post_norm(k, rows_sb):
                    statistics()
                    root_wait(k)
                    nc.vector.reciprocal(rstd[:, 0:NT], std[:, 0:NT])
                    dve.drain()
                    for t in range(NT):
                        ts_(x[:, t, :], x[:, t, :], mv[:, t, 0:1], rstd[:, t:t + 1], ALU.subtract, ALU.mult)
                    dve.drain()
                    g = rows_sb[:, 0, :].unsqueeze(1).broadcast_to([P, NT, D])
                    b = rows_sb[:, 1, :].unsqueeze(1).broadcast_to([P, NT, D])
                    tt(x[:, :, :], x[:, :, :], g, ALU.mult)
                    dve.drain()
                    last = tt(x[:, :, :], x[:, :, :], b, ALU.add)
                    return last

                dve.wait_ge(params, layer_at(l, 16 * PARAM_DMAS, 16 * PARAM_DMAS))

                lv = row[:, 0:256].rearrange("p (a b d) -> p a b d", a=2, b=2)
                tt(lamp[:, :, :], lv[:, :, 0, :], lv[:, :, 1, :], ALU.mult)
                dve.drain()
                reduce(lamw[:, 0:2], lamp[:, :, :], AX.X, ALU.add).then_inc(lam_sum, 1)
                dve.wait_ge(lam_exp, l + 1)
                tt(lamw[:, 4:5], lamw[:, 2:3], lamw[:, 3:4], ALU.subtract)
                copy(lamw[:, 6:7], const[:, bass.ds(l * 2 + (C_LAM + 1), 1)])
                dve.drain()
                tt(lamw[:, 4:5], lamw[:, 4:5], const[:, bass.ds(l * 2 + C_LAM, 1)], ALU.add)
                dve.drain()
                ts_(lamw[:, 5:6], lamw[:, 4:5], -1.0, None, ALU.mult)

                dve.wait_ge(mod_full, layer_at(l, N_MOD, 8))
                cols = PS[:, 0:64].rearrange("p (q s) -> p q s", s=2)
                tt(modc[:, 0:8, :], cols[:, 0:8, :], bc[:, 0:8].unsqueeze(2).broadcast_to([P, 8, 2]), ALU.add)
                stt(modc[:, 8:16, :], cols[:, 8:16, :], 1.0, bc[:, 8:16].unsqueeze(2).broadcast_to([P, 8, 2]),
                    ALU.add, ALU.add).then_inc(mod_ready, 1)

                ln_out(0, 0, xn)

                def rotary(v, heads):
                    e = v.rearrange("p t h (f two) -> p t h f two", two=2)
                    xe, xo = e[:, :, :, :, 0], e[:, :, :, :, 1]
                    c = ropec.unsqueeze(2).broadcast_to([P, 4, heads, 32])
                    s = ropes.unsqueeze(2).broadcast_to([P, 4, heads, 32])
                    r = [rot[:, n, 0:4 * heads * 32].rearrange("p (t h f) -> p t h f", t=4, h=heads) for n in range(4)]
                    tt(r[0], xe, c, ALU.mult)
                    tt(r[1], xo, s, ALU.mult)
                    tt(r[2], xe, s, ALU.mult)
                    tt(r[3], xo, c, ALU.mult)
                    dve.drain()
                    tt(xe, r[0], r[1], ALU.subtract)
                    return tt(xo, r[2], r[3], ALU.add)

                gq = z[:, 0, :, :].rearrange("p t (h d) -> p (t h) d", d=64)
                gk = zk[:, :, :].rearrange("p t (h d) -> p (t h) d", d=64)
                dve.wait_ge(z_ready, layer_at(l, N_Z, 15))
                for v, n0, n in ((gq, 0, 40), (gk, 40, 10)):
                    tmp = sq[:, 0:64 * n].rearrange("p (n d) -> p n d", d=64)
                    tt(tmp, v, v, ALU.mult)
                    dve.drain()
                    reduce(var[:, n0:n0 + n], tmp, AX.X, ALU.add)
                    dve.drain()
                ts_(var[:, 0:50], var[:, 0:50], 1.0 / 64, EPS, ALU.mult, ALU.add).then_inc(var_ready, 1)
                root_wait(1)
                nc.vector.reciprocal(rstd[:, 0:50], std[:, 0:50])
                dve.drain()
                for v, n0, n, g0 in ((gq, 0, 40, 256), (gk, 40, 10, 320)):
                    tt(v, v, rstd[:, n0:n0 + n].unsqueeze(2).broadcast_to([P, n, 64]), ALU.mult)
                    dve.drain()
                    tt(v, v, row[:, g0:g0 + 64].unsqueeze(1).broadcast_to([P, n, 64]), ALU.mult)
                    dve.drain()
                rotary(z[:, 0, 1:NT, :].rearrange("p t (h d) -> p t h d", d=64), 8).then_inc(blk_ready, 1)
                dve.drain()
                rotary(zk[:, 1:NT, :].rearrange("p t (h d) -> p t h d", d=64), 2).then_inc(blk_ready, 1)
                for buf, done in ((1, 25), (0, 35)):
                    dve.drain()
                    dve.wait_ge(z_ready, layer_at(l, N_Z, done))
                    rotary(z[:, buf, 1:NT, :].rearrange("p t (h d) -> p t h d", d=64), 8).then_inc(blk_ready, 1)

                dve.wait_ge(kv_stored, 64 * (l + 1))
                dve.wait_ge(f2_full, layer_at(l, N_F, N_F))

                def attend(t, nk):
                    base = l * N_UNIT + t * UNITS
                    base_t = l * N_T + t * TURN_GROUPS
                    w = nk * P
                    tile_rows = oall[:, 0, :] if nk == 1 else oall[:, bass.ds(t, 1), :].rearrange("p o d -> p (o d)")

                    def maxima(u):
                        dve.wait_ge(s_full, base + u + 1)
                        s0 = 1536 * (u % 2)
                        s = PS[:, s0:s0 + 1280].rearrange("p (m n) -> p m n", m=2)[:, :, 0:w]
                        reduce(smx[:, u % 2, :], s, AX.X, ALU.max)
                        dve.drain()
                        ts_(nbias[:, u % 2, :], smx[:, u % 2, :], -SCALE, None, ALU.mult).then_inc(mx_ready, 1)

                    def weights_of(u):
                        b = u % 2
                        dve.wait_ge(p_ready, base + u + 1)
                        if u >= 4:
                            nc.vector.reciprocal(rinv[:, b, :], rsum[:, b, :]).then_inc(w_ready, 1)
                            return
                        nc.vector.reciprocal(rinv[:, b, :], rsum[:, b, :])
                        dve.drain()
                        tt(rneg[:, b:b + 1], rinv[:, b, 1:2], lamw[:, 5:6], ALU.mult)
                        dve.drain()
                        ts_(prob[:, b, 1, 0:w], prob[:, b, 1, 0:w], rneg[:, b:b + 1], None, ALU.mult)
                        dve.drain()
                        if u >= 2:
                            dve.wait_ge(t_full, base_t + u - 1)
                        stt(wd[:, b, 0:w], prob[:, b, 0, 0:w], rinv[:, b, 0:1], prob[:, b, 1, 0:w],
                            ALU.mult, ALU.add).then_inc(w_ready, 1)

                    def outputs(u):
                        dve.wait_ge(o_full, base + u + 1)
                        if u < 4:
                            last = copy(tile_rows[:, u * P:u * P + P], bank(7, P, 2 * P))
                        else:
                            for m in range(2):
                                c = 512 + (4 * m + u - 4) * 64
                                last = ts_(tile_rows[:, c:c + 64], bank(7, P + 64 * m, P + 64 * m + 64),
                                           rinv[:, u % 2, m:m + 1], None, ALU.mult)
                        last.then_inc(o_ready, 1)

                    maxima(0)
                    if nk == 5:
                        dve.wait_ge(mod_full, l * N_MOD + 8 + t * 4)
                        tt(modc[:, bass.ds(t * 8 + 8, 8), :], bank(6, 0, 16).rearrange("p (q s) -> p q s", s=2),
                           bc[:, bass.ds(t * 8 + 8, 8)].unsqueeze(2).broadcast_to([P, 8, 2]), ALU.add)
                    for u in range(UNITS):
                        weights_of(u)
                        if u + 1 < UNITS:
                            maxima(u + 1)
                        outputs(u)
                    dve.drain()

                attend(0, 1)
                with dve.Fori(1, NT) as t:
                    attend(t, 5)

                for w, q in ((0, 16), (1, 40)):
                    for s in range(2):
                        last = tt(diag[:, w, s, :, :], ident.unsqueeze(1).broadcast_to([P, KC, P]),
                                  modc[:, q:q + 8, s:s + 1].broadcast_to([P, KC, P]), ALU.mult)
                    last.then_inc(diag_ready, 1)
                ts_(modc[:, 32:40, :], modc[:, 32:40, :], 1.0, None, ALU.add).then_inc(mod_ready, 1)

                dv4 = oall[:, :, 0:512].rearrange("p t (h d) -> p t h d", d=P)
                s4 = sq[:, :].rearrange("p (t h d) -> p t h d", t=NT, h=4)
                tt(s4, dv4, dv4, ALU.mult)
                dve.drain()
                reduce(var[:, 0:20], sq[:, :].rearrange("p (n d) -> p n d", d=P), AX.X, ALU.add)
                dve.drain()
                ts_(var[:, 0:20], var[:, 0:20], 1.0 / P, EPS, ALU.mult, ALU.add).then_inc(var_ready, 1)
                root_wait(2)
                nc.vector.reciprocal(rstd[:, 0:20], std[:, 0:20])
                dve.drain()
                ts_(rstd[:, 0:20], rstd[:, 0:20], lamw[:, 6:7], None, ALU.mult)
                dve.drain()
                tt(dv4, dv4, rstd[:, 0:20].rearrange("p (t h) -> p t h", t=NT).unsqueeze(3).broadcast_to([P, NT, 4, P]),
                   ALU.mult)
                dve.drain()
                tt(dv4, dv4, row[:, 384:512].unsqueeze(1).unsqueeze(1).broadcast_to([P, NT, 4, P]),
                   ALU.mult).then_inc(dn_ready, 1)

                for j in range(N_MG):
                    n, dc = j // 8, j % 8
                    b = 4 * (j % 2)
                    dve.wait_ge(sg_ready, layer_at(l, N_MG, j + 1))
                    s = sg[:, j % 2, :].rearrange("p (h n) -> p h n", h=2)
                    m = mT[:, dc, :].rearrange("p (h n) -> p h n", h=2)
                    tm = mtmp[:, :].rearrange("p (h n) -> p h n", h=2)
                    if n == 0:
                        tt(m, two_banks(b, TH), s, ALU.mult).then_inc(mg_done, 1)
                    else:
                        tt(tm, two_banks(b, TH), s, ALU.mult)
                        dve.drain()
                        tt(m, m, tm, ALU.add).then_inc(mg_done, 1)
                        dve.drain()

                for j in range(N_OUT):
                    k, t = j // 5, j % 5
                    s = 0 if t == 0 else 1
                    cols = slice(256 * k, 256 * k + 256)
                    dve.wait_ge(out_full, layer_at(l, N_OUT, j + 1))
                    tt(otmp[:, j % 2, :], bank(j % 4, 0, 256), gate1[:, s, cols], ALU.mult)
                    dve.drain()
                    stt(x[:, t, cols], x[:, t, cols], ALPHA, otmp[:, j % 2, :], ALU.mult, ALU.add).then_inc(out_done, 1)
                dve.drain()
                dve.wait_ge(ln1_rows, 16 * (l + 1))
                post_norm(3, lnr)
                dve.drain()
                ln_out(1, 4, xn2)

                scores = score
                with dve.Fori(0, NT) as t:
                    dve.wait_ge(score_ready, l * NT + t + 1)
                    nc.vector.memset(pm[:, :], 0.0)
                    for s in range(16):
                        nc.vector.max(sv[:, s, 0:8], scores[:, s, :])
                    dve.drain()
                    for s in range(16):
                        nc.vector.match_replace(work[:, s, :], sv[:, s, 0:8], scores[:, s, :], LOWEST)
                        nc.vector.max_index(si[:, s, 0:8], sv[:, s, 0:8], scores[:, s, :])
                    dve.drain()
                    for s in range(16):
                        nc.vector.max(sv[:, s, 8:16], work[:, s, :])
                    dve.drain()
                    for s in range(16):
                        nc.vector.max_index(si[:, s, 8:16], sv[:, s, 8:16], work[:, s, :])
                    c4 = cand[:, :, :].rearrange("p h (i j) -> p h i j", i=TOPK)
                    tt(c4, sv[:, 0:8, :].unsqueeze(3).broadcast_to([P, 8, TOPK, TOPK]),
                       sv[:, 8:16, :].unsqueeze(2).broadcast_to([P, 8, TOPK, TOPK]), ALU.add)
                    dve.drain()
                    copy(sif[:, :, :], si[:, :, :])
                    c2 = work[:, :, :].rearrange("p s n -> p (s n)").rearrange("p (h n) -> p h n", h=8)
                    for h in range(HEADS):
                        nc.vector.max(pv[:, h, 0:8], cand[:, h, :])
                    dve.drain()
                    for h in range(HEADS):
                        nc.vector.match_replace(c2[:, h, :], pv[:, h, 0:8], cand[:, h, :], LOWEST)
                        nc.vector.max_index(pi[:, h, 0:8], pv[:, h, 0:8], cand[:, h, :])
                    dve.drain()
                    for h in range(HEADS):
                        nc.vector.max(pv[:, h, 8:16], c2[:, h, :])
                    dve.drain()
                    for h in range(HEADS):
                        nc.vector.max_index(pi[:, h, 8:16], pv[:, h, 8:16], c2[:, h, :])
                    copy(pm[:, 8:16], pv[:, :, 0])
                    dve.drain()
                    tt(pv[:, :, :], pv[:, :, :], pm[:, 8:16].unsqueeze(2).broadcast_to([P, 8, TOPK]),
                       ALU.subtract).then_inc(best_ready, 1)
                    flat = pi[:, :, :].rearrange("p h k -> p (h k)")
                    ts_(pii[:, 0, :], flat, 4, None, ALU.logical_shift_right)
                    ts_(pii[:, 1, :], flat, 15, None, ALU.bitwise_and)
                    dve.drain()
                    copy(pif[:, :, :], pii[:, :, :])
                    dve.drain()
                    eq = cand[:, :, :].rearrange("p h (k m) -> p h k m", k=TOPK)
                    for p in range(2):
                        place = pif[:, p, :].unsqueeze(2).broadcast_to([P, P, TOPK])
                        tt(cand[:, :, :].rearrange("p h (k m) -> p (h k) m", k=TOPK),
                           iota[:, 0:TOPK].unsqueeze(1).broadcast_to([P, P, TOPK]), place, ALU.is_equal)
                        dve.drain()
                        tt(eq, eq, sif[:, 8 * p:8 * p + 8, :].unsqueeze(2).broadcast_to([P, 8, TOPK, TOPK]), ALU.mult)
                        dve.drain()
                        reduce(idx[:, p, :], cand[:, :, :].rearrange("p h (k m) -> p (h k) m", k=TOPK), AX.X, ALU.add)
                        dve.drain()
                    dve.wait_ge(exp_ready, l * NT + t + 1)
                    reduce(pm[:, 0:8], pw[:, :, :], AX.X, ALU.add)
                    dve.drain()
                    nc.vector.reciprocal(pm[:, 8:16], pm[:, 0:8])
                    dve.drain()
                    tt(idx[:, 2, :].rearrange("p (h k) -> p h k", h=8), pw[:, :, :],
                       pm[:, 8:16].unsqueeze(2).broadcast_to([P, 8, TOPK]), ALU.mult).then_inc(idx_ready, 1)
                    dve.wait_ge(idxT_ready, l * NT + t + 1)

                    def onehots(i, u):
                        for n, oh in enumerate((ohA, ohE)):
                            key = idxT[:, n, bass.ds(i * 16 + 4 * u, 4)].unsqueeze(2).broadcast_to([P, 4, P])
                            last = tt(oh[:, u, :, :], iota.unsqueeze(1).broadcast_to([P, 4, P]), key, ALU.is_equal)
                        last.then_inc(eq_ready, 1)

                    for u in range(4):
                        onehots(0, u)
                    with dve.Fori(1, P // 16) as i:
                        for u in range(4):
                            dve.wait_ge(quad_ready, l * N_QUAD + t * QUADS + i * 4 + (u - 3))
                            onehots(i, u)
                    dve.wait_ge(quad_ready, l * N_QUAD + t * QUADS + QUADS)

                dve.wait_ge(hhi_ready, l + 1)
                nc.vector.memset(acc[:, :, :], 0.0)
                dve.drain()
                tt(hT_lo[:, :, :], hT[:, :, :], hT_hi[:, :, :].bitcast(F32), ALU.subtract).then_inc(hlo_ready, 1)

                def split_lo(s, n):
                    dve.wait_ge(hi_ready, l * N_SPLIT + n + 1)
                    tt(ring_lo[:, s, :], ring[:, s, :], ring_hi[:, s, :].bitcast(F32), ALU.subtract).then_inc(split_ready, 1)

                def weigh(b, j, u, gcount):
                    if j == 0:
                        dve.wait_ge(g_loaded[u], 16 * (l * (NB // 2) + gcount + 1))
                    dve.wait_ge(gelu_ready, l * (2 * NB) + b * 2 + (j + 1))
                    tt(wtmp[:, :].rearrange("p (g t) -> p g t", t=64),
                       act_g[:, j, :].rearrange("p (g t) -> p g t", t=64), G[:, u, :, j, :], ALU.mult)
                    dve.drain()
                    copy(W_hi[:, u, j, :], wtmp[:, :])
                    dve.drain()
                    tt(W_lo[:, u, j, :], wtmp[:, :], W_hi[:, u, j, :].bitcast(F32), ALU.subtract).then_inc(W_ready, 1)
                    dve.drain()

                def add_up(b, n0, n1, par):
                    for n in range(n0, n1):
                        t, dh = n // 2, n % 2
                        dve.wait_ge(v_full, l * N_V + b * 10 + (n + 1))
                        a = acc[:, t, 512 * dh:512 * dh + 512]
                        tt(a, a, bank(4 + (10 * par + n) % 4), ALU.add).then_inc(v_done, 1)

                for n in range(3):
                    split_lo(n, n)
                weigh(0, 0, 0, 0)
                weigh(0, 1, 0, 0)
                with dve.Fori(0, NB // 2 - 1) as i:
                    for u in range(2):
                        v = 1 - u
                        gc = i + u
                        weigh(i * 2 + (u + 1), 0, v, gc)
                        split_lo((3 + 2 * u) % RING, i * 4 + (3 + 2 * u))
                        weigh(i * 2 + (u + 1), 1, v, gc)
                        add_up(i * 2 + u, 0, 5, u)
                        split_lo((4 + 2 * u) % RING, i * 4 + (4 + 2 * u))
                        add_up(i * 2 + u, 5, 10, u)
                weigh(NB - 1, 0, 1, NB // 2 - 1)
                split_lo(3, 2 * NB - 1)
                weigh(NB - 1, 1, 1, NB // 2 - 1)
                add_up(NB - 2, 0, 10, 0)
                add_up(NB - 1, 0, 10, 1)
                dve.drain()

                for t in range(NT):
                    tt(acc[:, t, :], acc[:, t, :], gate2[:, 0 if t == 0 else 1, :], ALU.mult)
                dve.drain()
                stt(x[:, :, :].rearrange("p t d -> p (t d)"), x[:, :, :].rearrange("p t d -> p (t d)"), ALPHA,
                    acc[:, :, :].rearrange("p t d -> p (t d)"), ALU.mult, ALU.add)
                dve.drain()
                dve.wait_ge(ln2_rows, 16 * (l + 1))
                post_norm(5, lnr2).then_inc(layer_done, 1)
                dve.drain()
                copy(lamw[:, 8:10], const[:, 0:2]).then_inc(layer_free, 1)


def constants(np):
    f = np.float64
    n = np.arange(P)
    ang = 2 * np.pi * ((n[:, None] * n[None, :]) % P) / P
    cos, sin = np.cos(ang) / np.sqrt(f(P)), np.sin(ang) / np.sqrt(f(P))
    tok = np.arange(4 * P)
    freq = np.float32(10000.0) ** (-np.arange(16, dtype=np.float32) / np.float32(16))
    pos = np.concatenate([(tok // 64)[:, None] * freq, (tok % 64)[:, None] * freq], -1).astype(np.float32)
    rc = np.cos(pos.astype(f)).reshape(4, P, 32).transpose(1, 0, 2).reshape(P, P)
    rs = np.sin(pos.astype(f)).reshape(4, P, 32).transpose(1, 0, 2).reshape(P, P)
    lam = []
    for layer in range(LAYERS):
        init = 0.8 - 0.6 * np.exp(-0.3 * layer)
        lam += [init, 1.0 - init]
    parts = [np.eye(P), np.tile(n, (P, 1)), cos, sin, -sin, rc, rs, np.ones((P, P)), np.tile(lam, (P, 1))]
    table = np.concatenate(parts, 1).astype(np.float32)
    assert table.shape[1] == NCONST
    m = np.arange(4 * P)
    ang = 2 * np.pi * ((m[:, None] * m[None, :]) % (4 * P)) / (4 * P)
    dft = [(g(ang) / np.sqrt(f(4 * P))).astype(np.float32).reshape(4, P, 4 * P).transpose(1, 0, 2).reshape(P, SLOT)
           for g in (np.cos, np.sin)]
    return table, dft


def weight_stream(np, w_mod, w_in, w_branch, w_out, peer_wq, peer_subkeys, peer_u, peer_v, dft):
    out = np.zeros((LAYERS, PER_LAYER, P, SLOT), np.float32)

    def columns(w, c0, width=256):
        return w[:, c0:c0 + width].reshape(-1, P, width).transpose(1, 0, 2).reshape(P, -1)

    for l in range(LAYERS):
        s = out[l]
        for k in range(24):
            s[MOD1 + k if k < 8 else MOD2 + k - 8] = columns(w_mod[l], 256 * k)
        starts = [1536, 1792, 2048, 0, 256, 512, 768, 1024, 1280, 2304, 2560]
        for k, c0 in enumerate(starts):
            s[GQ + k] = columns(w_in[l], c0)
        s[DFT], s[DFT + 1] = dft
        for n in range(3):
            for half in range(2):
                slot = MERGE + 6 * n + 3 * half
                s[slot] = columns(w_branch[l, n], 512 * half, 512)
                for g in range(2):
                    s[slot + 1 + g] = columns(w_in[l], 2816 + n * D + 512 * half + 256 * g)
        for k in range(4):
            s[OUT + k] = columns(w_out[l], 256 * k)
            s[WQ + k] = columns(peer_wq[l], 256 * k)
        s[SUB, :, 0:1024] = peer_subkeys[l].transpose(1, 3, 0, 2).reshape(P, 1024)
        u = peer_u[l].reshape(P, NB, 2, KC, P).transpose(1, 4, 3, 2, 0).reshape(NB, P, SLOT)
        v = peer_v[l].reshape(P, NB, 2, D).transpose(1, 0, 2, 3).reshape(NB, P, SLOT)
        s[PEER] = u[0]
        s[PEER + 1:PER_LAYER - 1:2] = u[1:]
        s[PEER + 2:PER_LAYER:2] = v[:-1]
        s[PER_LAYER - 1] = v[-1]
    return out.reshape(LAYERS * PER_LAYER, P, SLOT)


def build(nc):
    def dram(name, shape, kind):
        return nc.dram_tensor(name, shape, F32, kind=kind).ap()

    ins = {n: dram(n, s, "ExternalInput") for n, s in (
        ("weights", (LAYERS * PER_LAYER, P, SLOT)), ("consts", (P, NCONST)), ("x_in", (NT, P, D)),
        ("cond", (P, 2 * KC)), ("bcol", (LAYERS, P, 48)), ("rows", (LAYERS, 512)),
        ("lnrows", (LAYERS * 2, 2, D)), ("cache_k", (LAYERS, P, 640)), ("cache_v", (LAYERS, P, 640)))}
    outs = {n: dram(n, s, "ExternalOutput") for n, s in (
        ("y", (NT, P, D)), ("new_dk", (LAYERS, P, 512)), ("new_dv", (LAYERS, P, 512)),
        ("new_gk", (LAYERS, P, P)), ("new_gv", (LAYERS, P, P)))}
    gate_matrix = dram("gate_matrix", (NB, P, 2 * T), "Internal")
    trunk(nc, **ins, **outs, gate_matrix=gate_matrix)


def layouts(np, i):
    c = np.ascontiguousarray
    table, dft = constants(np)
    rows = np.concatenate([i["diff_lam"].reshape(LAYERS, 256), i["q_norm_g"], i["k_norm_g"], i["diff_norm_g"]], 1)
    b = i["b_mod"]
    return {
        "weights": weight_stream(np, i["w_mod"], i["w_in"], i["w_branch"], i["w_out"], i["peer_wq"],
                                 i["peer_subkeys"], i["peer_u"], i["peer_v"], dft),
        "consts": table,
        "x_in": np.concatenate([i["x_prompt"].reshape(1, P, D), i["x_sample"].reshape(4, P, D)], 0),
        "cond": c(np.stack([i["c_ctx"], i["c"][0]], -1).reshape(KC, P, 2).transpose(1, 0, 2).reshape(P, 2 * KC)),
        "bcol": c(b.reshape(LAYERS, 48, P).transpose(0, 2, 1)),
        "rows": rows,
        "lnrows": c(np.stack([i["ln_g"], i["ln_b"]], 2).reshape(LAYERS * 2, 2, D)),
        "cache_k": np.concatenate([i["cache_diff_k"][0].reshape(LAYERS, P, 512),
                                   i["cache_gqa_k"][0].reshape(LAYERS, P, P)], -1),
        "cache_v": np.concatenate([i["cache_diff_v"][0].reshape(LAYERS, P, 512),
                                   i["cache_gqa_v"][0].reshape(LAYERS, P, P)], -1),
    }


def kernel(**inputs):
    import numpy as np
    import concourse.bacc as bacc
    from concourse.bass_utils import run_bass_kernel_spmd

    arrays = layouts(np, {k: np.asarray(v) for k, v in inputs.items()})
    nc = bacc.Bacc("TRN2", target_bir_lowering=False, num_devices=1)
    build(nc)
    r = run_bass_kernel_spmd(nc, [arrays], core_ids=[0]).results[0]
    y = r["y"]
    return (y[0:1], y[1:].reshape(1, 512, D),
            r["new_dk"].reshape(1, LAYERS, P, 4, P), r["new_dv"].reshape(1, LAYERS, P, 4, P),
            r["new_gk"].reshape(1, LAYERS, P, 2, 64), r["new_gv"].reshape(1, LAYERS, P, 2, 64))
```

```python
from contextlib import ExitStack

import concourse.bass as bass
from concourse import mybir
from concourse.alu_op_type import AluOpType as ALU

F32 = mybir.dt.float32
F32R = mybir.dt.float32r
U32 = mybir.dt.uint32
ACT = mybir.ActivationFunctionType
AX = mybir.AxisListType

P = 128
D = 1024
KC = D // P
LAYERS = 2
NT = 5
T = NT * P
TH = T // 2
HEADS = 8
TOPK = 16
KEYS = 128
ALPHA = float((2 * LAYERS) ** 0.25)
EPS = 1e-6
SCALE = 64.0 ** -0.5
LOWEST = -3.0e38

RING = 4
SLOT = 2048
MOD1, GQ, KV, DQ, DK, DV, FZ, DFT, MOD2 = 0, 8, 10, 11, 13, 15, 17, 19, 21
MERGE, OUT, SUB, WQA, WQB, PEER = 37, 55, 59, 60, 64, 68
NB = KEYS // 2
PER_LAYER = PEER + 2 * NB
POSITION = [n % RING for n in range(WQA)] + [(n - WQA) % 3 for n in range(WQA, PEER)] \
    + [n % RING for n in range(PEER, PER_LAYER)]
FILLS = [POSITION.count(p) for p in range(RING)]

N_STD = 7
N_MOD = 24
N_COL = 6
N_HT = 20
N_IN = 11
N_Z = 5 * N_IN
N_BLK = 4
N_TR = 18
N_F = 5
UNITS = 8
N_UNIT = NT * UNITS
TURN_GROUPS = 12
N_T = NT * TURN_GROUPS
N_BR = 10
N_MG = 24
N_OUT = 20
N_MSPLIT = 16
N_Q = 12
QUADS = P // 4
N_QUAD = NT * QUADS
N_W = 2 * NB
N_SPLIT = 2 * NB
N_V = 10 * NB
PARAM_DMAS = 4

C_ID, C_IOTA, C_COS, C_SIN, C_NSIN, C_ROPEC, C_ROPES, C_ONE, C_LAM = 0, 128, 256, 384, 512, 640, 768, 896, 1024
NCONST = 1028


def layer_at(l, per_layer, n):
    return l * per_layer + n


def trunk(nc, weights, consts, x_in, cond, bcol, rows, lnrows, cache_k, cache_v, x_wait,
          y, new_dk, new_dv, new_gk, new_gv, gate_matrix):
    ctx = ExitStack()
    with ctx:
        def sem(name):
            return ctx.enter_context(nc.semaphore(name))

        slab_floats = 53200
        slab_at = -(-nc.sbuf_base // 32) * 32
        ctx.enter_context(nc.sbuf_tensor("slab", [P, slab_floats], F32))

        def at(name, shape, offset, dt=F32):
            size = 1
            for s in shape:
                size *= s
            assert offset + size <= slab_floats, (name, offset, size)
            t = nc.alloc_sbuf_tensor_at(name, [P] + list(shape), dt, offset=slab_at + 4 * offset)
            return t, offset + -(-size // 8) * 8

        o = 0
        const, o = at("const", [NCONST], o)
        row, o = at("row", [512], o)
        bc, o = at("bc", [48], o)
        modc, o = at("modc", [48, 2], o)
        cnd, o = at("cnd", [KC, 2], o)
        cnds, o = at("cnds", [KC, 2], o)
        stats, o = at("stats", [NT, 2, 6], o)
        mv, o = at("mv", [NT, 2], o)
        var, o = at("var", [64], o)
        std, o = at("std", [64], o)
        rstd, o = at("rstd", [64], o)
        lamw, o = at("lamw", [16], o)
        smx, o = at("smx", [2, 2], o)
        nbias, o = at("nbias", [2, 2], o)
        rsum, o = at("rsum", [2, 2], o)
        rinv, o = at("rinv", [4, 2], o)
        rneg, o = at("rneg", [2], o)
        ring_at = o
        ring, o = at("ring", [RING, SLOT], o)
        ht_at = o
        hT, o = at("hT", [KC, T], o)
        x_at = o
        x, o = at("x", [NT, D], o)
        gate2, o = at("gate2", [2, D], o)
        arena = o

        ring_lo, _ = at("ring_lo", [RING, SLOT], ring_at, F32R)
        hT_lo, _ = at("hT_lo", [KC, T], ht_at, F32R)
        h_hi, _ = at("h_hi", [KC, T], x_at, F32R)

        z_at = o
        z, o = at("z", [2, NT, 512], o)
        zk, o = at("zk", [NT, P], o)
        q_at = o
        qT, o = at("qT", [8, T], o)
        k_at = o
        kT, o = at("kT", [5, 768], o)
        V, o = at("V", [6, 640], o)
        f_at = o
        fT, o = at("fT", [4, T], o)
        ck_at = o
        ckb, _ = at("ckb", [640], ck_at)
        qcur, o = at("qcur", [8, P], ck_at)
        tmp_at = o
        lamp, _ = at("lamp", [2, 64], tmp_at + 4096)
        xn, _ = at("xn", [2, D], tmp_at)
        sq, _ = at("sq", [2560], tmp_at)
        rot, _ = at("rot", [4, 1024], tmp_at)
        in_hi = [at("in_hi0", [SLOT], f_at, F32R)[0],
                 at("in_hi1", [SLOT], tmp_at + 4224, F32R)[0]]
        acs, _ = at("acs", [2, 2, 512], tmp_at)
        prob, t = at("prob", [2, 2, 640], tmp_at)
        wd, t = at("wd", [2, 640], t)
        pT, t = at("pT", [2, 2, 5, P], t)
        o = t
        mhi, t = at("mhi", [2, SLOT], ck_at, F32R)
        assert t <= tmp_at + 3840
        sg, t = at("sg", [2, T], tmp_at + 3840 + 2 * D)
        mtmp, t = at("mtmp", [T], t)
        otmp, t = at("otmp", [2, 256], t)
        oall, _ = at("oall", [NT, D], z_at)
        mT, _ = at("mT", [KC, T], z_at)
        brT, _ = at("brT", [8, T], q_at)
        diag, t = at("diag", [2, 2, KC, P], k_at)
        x_mix, t = at("x_mix", [NT, D], k_at)
        lnr, t = at("lnr", [2, D], t)
        assert t <= f_at
        mT_lo, _ = at("mT_lo", [KC, T], z_at, F32R)
        mT_hi, _ = at("mT_hi", [KC, T], q_at, F32R)
        gate1, _ = at("gate1", [2, D], tmp_at + 3840)

        mrow, _ = at("mrow", [1024], slab_floats - 1024)

        o = arena
        stg, o = at("stg", [2, NB, 2, 64], o)
        xn2, _ = at("xn2", [NT, D], arena)
        qT2, o = at("qT2", [8, T], o)
        ohA, _ = at("ohA", [4, 4, P], o)
        work, o = at("work", [16, P], o)
        ohE, _ = at("ohE", [2, 4, P], o)
        ohB, _ = at("ohB", [2, 4, P], o + 1024)
        cand, o = at("cand", [8, 256], o)
        score, o = at("score", [16, P], o)
        qcur2, _ = at("qcur2", [8, P], ring_at + POSITION[SUB] * SLOT + 1024)
        sv, o = at("sv", [16, TOPK], o)
        si, o = at("si", [16, TOPK], o, U32)
        sif, o = at("sif", [16, TOPK], o)
        pv, o = at("pv", [8, TOPK], o)
        pi, o = at("pi", [8, TOPK], o, U32)
        pii, o = at("pii", [2, P], o, U32)
        pif, o = at("pif", [2, P], o)
        idx, o = at("idx", [3, P], o)
        idxT, o = at("idxT", [3, P], o)
        pw, o = at("pw", [8, TOPK], o)
        pm, o = at("pm", [16], o)

        o = arena
        hi_at = o
        ring_hi, o = at("ring_hi", [RING, SLOT], o, F32R)
        hT_hi, o = at("hT_hi", [KC, T], o, F32R)
        acc, o = at("acc", [NT, D], o)
        W_hi, o = at("W_hi", [2, 2, T], o, F32R)
        W_lo, o = at("W_lo", [2, 2, T], o, F32R)
        G, o = at("G", [2, 2 * NT, 2, 64], o)
        act_g, o = at("act_g", [2, T], o)
        wtmp, o = at("wtmp", [T], o)
        lnr2, _ = at("lnr2", [2, D], hi_at)

        ident = const[:, C_ID:C_ID + P]
        iota = const[:, C_IOTA:C_IOTA + P]
        ropec = const[:, C_ROPEC:C_ROPEC + P].rearrange("p (t f) -> p t f", t=4)
        ropes = const[:, C_ROPES:C_ROPES + P].rearrange("p (t f) -> p t f", t=4)

        PS = ctx.enter_context(nc.psum_tensor("PS", [P, 8 * 512], F32))

        def bank(b, a=0, e=512):
            return PS[:, b * 512 + a:b * 512 + e]

        def two_banks(b, n):
            return PS[:, b * 512:(b + 2) * 512].rearrange("p (b n) -> p b n", b=2)[:, :, 0:n]

        slot_full = [sem(f"slot_full{i}") for i in range(RING)]
        setup = sem("setup")
        ring_free = sem("ring_free")
        layer_free = sem("layer_free")
        params = sem("params")
        ln1_rows = sem("ln1_rows")
        ln2_rows = sem("ln2_rows")
        kv_stored = sem("kv_stored")
        cond_ready = sem("cond_ready")
        mod_full = sem("mod_full")
        mrow_ready = sem("mrow_ready")
        col_full = sem("col_full")
        mod_ready = sem("mod_ready")
        diag_ready = sem("diag_ready")
        row_full = sem("row_full")
        row_ready = sem("row_ready")
        var_ready = sem("var_ready")
        std_ready = sem("std_ready")
        xn_ready = sem("xn_ready")
        xT_full = sem("xT_full")
        hT_ready = sem("hT_ready")
        z_full = sem("z_full")
        z_ready = sem("z_ready")
        blk_ready = sem("blk_ready")
        tr_full = sem("tr_full")
        tr_ready = sem("tr_ready")
        f1_full = sem("f1_full")
        f1_ready = sem("f1_ready")
        f2_full = sem("f2_full")
        f2_ready = sem("f2_ready")
        lam_sum = sem("lam_sum")
        lam_exp = sem("lam_exp")
        qcur_ready = sem("qcur_ready")
        s_full = sem("s_full")
        tail_full = sem("tail_full")
        mx_ready = sem("mx_ready")
        p_ready = sem("p_ready")
        w_ready = sem("w_ready")
        t_full = sem("t_full")
        pT_ready = sem("pT_ready")
        o_full = sem("o_full")
        o_ready = sem("o_ready")
        dn_ready = sem("dn_ready")
        br_full = sem("br_full")
        br_ready = sem("br_ready")
        x_away = sem("x_away")
        x_back = sem("x_back")
        h_hi_ready = sem("h_hi_ready")
        h_lo_ready = sem("h_lo_ready")
        in_hi_ready = sem("in_hi_ready")
        in_lo_ready = sem("in_lo_ready")
        mhi_ready = sem("mhi_ready")
        mlo_ready = sem("mlo_ready")
        mT_hi_ready = sem("mT_hi_ready")
        mT_lo_ready = sem("mT_lo_ready")
        mg_full = sem("mg_full")
        sg_ready = sem("sg_ready")
        mg_done = sem("mg_done")
        out_full = sem("out_full")
        out_done = sem("out_done")
        q_full = sem("q_full")
        q_ready = sem("q_ready")
        qcur2_ready = sem("qcur2_ready")
        sc_full = sem("sc_full")
        score_ready = sem("score_ready")
        best_ready = sem("best_ready")
        exp_ready = sem("exp_ready")
        idx_ready = sem("idx_ready")
        idxT_full = sem("idxT_full")
        idxT_ready = sem("idxT_ready")
        eq_ready = sem("eq_ready")
        oh_ready = sem("oh_ready")
        quad_full = sem("quad_full")
        quad_ready = sem("quad_ready")
        tile_expanded = sem("tile_expanded")
        g_stored = [sem(f"g_stored{i}") for i in range(2)]
        hhi_ready = sem("hhi_ready")
        hlo_ready = sem("hlo_ready")
        hi_ready = sem("hi_ready")
        split_ready = sem("split_ready")
        h_full = sem("h_full")
        gelu_ready = sem("gelu_ready")
        g_loaded = [sem(f"g_loaded{i}") for i in range(2)]
        W_ready = sem("W_ready")
        v_full = sem("v_full")
        v_done = sem("v_done")
        layer_done = sem("layer_done")
        y_stored = sem("y_stored")

        block = ctx.enter_context(nc.Block())

        def wait_slot(eng, l, n, extra=0):
            p = POSITION[n]
            eng.wait_ge(slot_full[p], 16 * (l * FILLS[p] + POSITION[:n].count(p) + 1 + extra))

        last_use = [(mod_full, N_MOD, k + 1) for k in range(8)]
        last_use += [(z_full, N_Z, 5 * (k + 1)) for k in range(11)]
        last_use += [(f1_full, N_F, N_F)] * 2
        last_use += [(mod_full, N_MOD, k + 1) for k in range(8, 24)]
        for n in range(3):
            for half in range(2):
                done = 8 * n + 4 * half
                last_use += [(mg_full, N_MG, done + 2), (mg_full, N_MG, done + 4), (mg_full, N_MG, done + 4)]
        last_use += [(out_full, N_OUT, 5 * (k + 1)) for k in range(4)]
        last_use += [(sc_full, NT, NT)]
        last_use += [(q_full, N_Q, k + 1) for k in range(4)]
        last_use += [(q_full, N_Q, 4 + 2 * (k + 1)) for k in range(4)]
        assert len(last_use) == PEER

        def turn_group(u, m):
            return u if u < 4 else 4 + 2 * (u - 4) + m

        def split_slot(g):
            return OUT + g - 12 if g >= 12 else MERGE + 3 * (g // 2) + 2 * (g % 2)

        def turned(u, m):
            b = 3 * (u % 2)
            return (bank(6), bank(b, 0, P)) if m == 0 else (bank(b + 2), bank(b + 1, 0, P))

        @block.sync
        def _(sp):
            def load(l, n):
                sp.dma_start(ring[:, POSITION[n], :],
                             weights[bass.ds(l * PER_LAYER + n, 1)].rearrange("o p f -> (o p) f")
                             ).then_inc(slot_full[POSITION[n]], 16)

            with sp.Fori(0, LAYERS) as l:
                for n in range(PEER + RING):
                    if n < RING:
                        if n in (0, RING - 1):
                            sp.wait_ge(ring_free, l * 2 + (1 if n == 0 else 2))
                    else:
                        before = max(k for k in range(n) if POSITION[k] == POSITION[n])
                        s, per, value = last_use[before]
                        sp.wait_ge(s, layer_at(l, per, value))
                    load(l, n)
                sp.wait_ge(h_full, layer_at(l, 2 * NB, 2))
                load(l, PEER + RING)
                with sp.Fori(0, NB // 2 - 2) as i:
                    for u in range(4):
                        b2 = u // 2
                        if u % 2 == 0:
                            sp.wait_ge(h_full, l * (2 * NB) + i * 4 + 2 * (b2 + 2))
                        else:
                            sp.wait_ge(v_full, l * N_V + i * 20 + 10 * (b2 + 1))
                        sp.dma_start(ring[:, (RING + 1 + u) % RING, :],
                                     weights[bass.ds(l * PER_LAYER + i * 4 + (PEER + RING + 1 + u), 1)]
                                     .rearrange("o p f -> (o p) f")
                                     ).then_inc(slot_full[(RING + 1 + u) % RING], 16)
                for s in range(2 * NB - 3, 2 * NB):
                    old = s - RING
                    if old % 2:
                        sp.wait_ge(h_full, layer_at(l, 2 * NB, 2 * ((old + 1) // 2 + 1)))
                    else:
                        sp.wait_ge(v_full, layer_at(l, N_V, 10 * (old // 2)))
                    load(l, PEER + s)
            sp.wait_ge(layer_done, LAYERS)
            sp.dma_start(y.rearrange("t p d -> p t d"), x[:, :, :]).then_inc(y_stored, 16)
            sp.wait_ge(y_stored, 16)

        @block.gpsimd
        def _(pool):
            pool.dma_start(const[:, :], consts).then_inc(setup, 16)
            pool.dma_start(x[:, :, :], x_in.rearrange("t p d -> p t d")).then_inc(setup, 16)
            pool.dma_start(cnd[:, :, :], cond.rearrange("p (k s) -> p k s", s=2)).then_inc(setup, 16)
            with pool.Fori(0, LAYERS) as l:
                def one(ap):
                    return ap[bass.ds(l, 1)]
                pool.wait_ge(layer_free, l + 1)
                pool.dma_start(bc[:, :], one(bcol).rearrange("o p n -> (o p) n")).then_inc(params, 16)
                pool.dma_start(row[:, :], one(rows).rearrange("o n -> (o n)").partition_broadcast(P)).then_inc(params, 16)
                pool.dma_start(ckb[:, :], one(cache_k).rearrange("o p n -> (o p) n")).then_inc(params, 16)
                pool.dma_start(V[:, 5, :], one(cache_v).rearrange("o p n -> (o p) n")).then_inc(params, 16)
                pool.dma_start(one(x_wait).rearrange("o t p d -> p (o t) d"), x[:, :, :]).then_inc(x_away, 16)
                for k in range(N_IN):
                    p = POSITION[GQ + k]
                    pool.wait_ge(in_hi_ready, layer_at(l, N_IN, k + 1))
                    nc.gpsimd.tensor_tensor(ring_lo[:, p, :], ring[:, p, :], in_hi[k % 2][:, :].bitcast(F32),
                                            ALU.subtract).then_inc(in_lo_ready, 1)
                pool.wait_ge(blk_ready, layer_at(l, N_BLK, 2))
                pool.dma_start(one(new_gk).rearrange("o p n -> (o p) n"), zk[:, 0, :]).then_inc(kv_stored, 16)
                pool.wait_ge(z_ready, layer_at(l, N_Z, 5 * 9))
                pool.dma_start(one(new_dk).rearrange("o p n -> (o p) n"), z[:, 0, 0, :]).then_inc(kv_stored, 16)
                pool.dma_start(one(new_dv).rearrange("o p n -> (o p) n"), V[:, 0, 0:512]).then_inc(kv_stored, 16)
                pool.dma_start(one(new_gv).rearrange("o p n -> (o p) n"), V[:, 0, 512:640]).then_inc(kv_stored, 16)
                pool.wait_ge(o_ready, layer_at(l, N_UNIT, N_UNIT))
                pool.dma_start(lnr[:, :, :], lnrows[bass.ds(l * 2, 1)].rearrange("o a n -> (o a n)")
                               .partition_broadcast(P)).then_inc(ln1_rows, 16)
                with pool.Fori(0, NT) as t:
                    def gate_quad(i, u):
                        pool.wait_ge(eq_ready, l * N_QUAD + t * QUADS + i * 4 + (u + 1))
                        g = idxT[:, 2, bass.ds(i * 16 + 4 * u, 4)].unsqueeze(2).broadcast_to([P, 4, P])
                        nc.gpsimd.tensor_tensor(ohB[:, u % 2, :, :], ohE[:, u % 2, :, :], g, ALU.mult).then_inc(oh_ready, 1)

                    for u in range(4):
                        if u >= 2:
                            pool.wait_ge(quad_full, l * N_QUAD + t * QUADS + (u - 1))
                        gate_quad(0, u)
                    with pool.Fori(1, P // 16) as i:
                        for u in range(4):
                            pool.wait_ge(quad_full, l * N_QUAD + t * QUADS + i * 4 + (u - 1))
                            gate_quad(i, u)
                pool.wait_ge(setup, 48)
                pool.wait_ge(hlo_ready, l + 1)

                def load_g(b, u):
                    pool.dma_start(G[:, u, :, :, :].rearrange("p g j t -> p (g j t)"),
                                   gate_matrix[bass.ds(b, 1)].rearrange("o p n -> (o p) n")
                                   ).then_inc(g_loaded[u], 16)
                load_g(0, 0)
                load_g(1, 1)
                with pool.Fori(0, (NB - 2) // 2) as i:
                    for u in range(2):
                        pool.wait_ge(W_ready, l * N_W + i * 4 + 2 * (u + 1))
                        load_g(i * 2 + (2 + u), u)
                pool.wait_ge(v_done, layer_at(l, N_V, N_V))
                pool.dma_start(lnr2[:, :, :], lnrows[bass.ds(l * 2 + 1, 1)].rearrange("o a n -> (o a n)")
                               .partition_broadcast(P)).then_inc(ln2_rows, 16)
            pool.wait_ge(kv_stored, 64 * LAYERS)

        @block.tensor
        def _(pe):
            mm = nc.tensor.matmul

            def group(out, pairs):
                for n, (a, b) in enumerate(pairs):
                    last = mm(out, a, b, start=(n == 0), stop=(n == len(pairs) - 1))
                return last

            def turn(out, in_):
                return nc.tensor.transpose(out, in_, ident)

            with pe.Fori(0, LAYERS) as l:
                def three(out, a_hi, a_lo, b_hi, b_lo, first, final):
                    mm(out, a_hi, b_hi, start=first, stop=False)
                    mm(out, a_hi, b_lo, start=False, stop=False)
                    return mm(out, a_lo, b_hi, start=False, stop=final)

                def modulation(slot, out, extra=0):
                    wait_slot(pe, l, slot, extra)
                    w = ring[:, slot % RING, :].rearrange("p (k n) -> p k n", k=KC)
                    group(out, [(cnds[:, c, :], w[:, c, :]) for c in range(KC)]).then_inc(mod_full, 1)

                def mod_columns(n, out):
                    pe.wait_ge(mrow_ready, n)
                    for k in range(8):
                        last = mm(out[:, 2 * k:2 * k + 2], mrow[0:2, k * P:k * P + P], ident[0:2, 0:2],
                                  start=True, stop=True)
                    last.then_inc(col_full, 1)

                pe.wait_ge(cond_ready, 1)
                for k in range(8):
                    modulation(MOD1 + k, PS[0:2, 256 * k:256 * k + 256])
                for n in range(2):
                    mod_columns(layer_at(l, N_COL, n + 1), bank(0, 16 * n, 16 * n + 16))

                def ln_turn(part, src, tiles):
                    depth = 2 if part == 0 else NT
                    for t in tiles:
                        pe.wait_ge(xn_ready, layer_at(l, 10, 5 * part + t + 1))
                        for h in range(2):
                            j = 10 * part + 2 * t + h
                            if 2 * t + h >= 4:
                                pe.wait_ge(hT_ready, layer_at(l, N_HT, j - 3))
                            for c in range(4):
                                last = turn(bank(4 + j % 4, c * P, c * P + P), src[:, t % depth, (4 * h + c) * P:(4 * h + c + 1) * P])
                            last.then_inc(xT_full, 1)

                ln_turn(0, xn, range(NT))

                pe.wait_ge(hT_ready, layer_at(l, N_HT, 10))

                def project(k):
                    pe.wait_ge(in_lo_ready, layer_at(l, N_IN, k + 1))
                    w_hi = in_hi[k % 2][:, :].rearrange("p (k n) -> p k n", k=KC)
                    w_lo = ring_lo[:, POSITION[GQ + k], :].rearrange("p (k n) -> p k n", k=KC)
                    for t in range(NT):
                        j = 5 * k + t
                        if k == 0:
                            pe.wait_ge(h_lo_ready, layer_at(l, NT, t + 1))
                        if j >= 4:
                            pe.wait_ge(z_ready, layer_at(l, N_Z, j - 3))
                        for c in range(KC):
                            last = three(bank(j % 4, 0, 256), h_hi[:, c, t * P:t * P + P], hT_lo[:, c, t * P:t * P + P],
                                         w_hi[:, c, :], w_lo[:, c, :], c == 0, c == KC - 1)
                        last.then_inc(z_full, 1)

                tr = [0]

                def qk_turn(ins):
                    j = tr[0]
                    if j >= 2:
                        pe.wait_ge(tr_ready, layer_at(l, N_TR, j - 1))
                    for c, a in enumerate(ins):
                        last = turn(bank(4 + j % 2, c * P, c * P + P), a)
                    last.then_inc(tr_full, 1)
                    tr[0] += 1

                for k in range(5):
                    project(k)
                pe.wait_ge(blk_ready, layer_at(l, N_BLK, 1))
                for t in range(NT):
                    qk_turn([z[:, 0, t, c * P:c * P + P] for c in range(4)])
                pe.wait_ge(blk_ready, layer_at(l, N_BLK, 2))
                pe.wait_ge(params, layer_at(l, 16 * PARAM_DMAS, 16 * PARAM_DMAS))
                qk_turn([zk[:, t, :] for t in range(4)])
                qk_turn([zk[:, 4, :], ckb[:, 512:640]])
                for k in range(5, 7):
                    project(k)
                pe.wait_ge(blk_ready, layer_at(l, N_BLK, 3))
                for t in range(NT):
                    qk_turn([z[:, 1, t, c * P:c * P + P] for c in range(4)])
                for k in range(7, 9):
                    project(k)
                pe.wait_ge(blk_ready, layer_at(l, N_BLK, 4))
                for t in range(NT):
                    qk_turn([z[:, 0, t, c * P:c * P + P] for c in range(4)])
                qk_turn([ckb[:, c * P:c * P + P] for c in range(4)])
                for k in range(9, 11):
                    project(k)

                pe.wait_ge(z_ready, layer_at(l, N_Z, N_Z))
                pe.wait_ge(tr_ready, layer_at(l, N_TR, N_TR))

                def dft_tokens(k):
                    if k >= 1:
                        pe.wait_ge(f1_ready, layer_at(l, N_F, k))
                    if k == 0:
                        for g in range(4):
                            b = 4 + g // 2
                            last = mm(bank(b, 256 * (g % 2), 256 * (g % 2) + 256), z[:, 1, 0, g * P:g * P + P],
                                      const[:, C_COS:C_COS + 256], start=True, stop=True)
                    else:
                        g = k - 1
                        for b in range(2):
                            if k == 1:
                                wait_slot(pe, l, DFT + b)
                            w = ring[:, (DFT + b) % RING, :].rearrange("p (t n) -> p t n", t=4)
                            last = group(bank(4 + b), [(z[:, 1, 1 + t, g * P:g * P + P], w[:, t, :]) for t in range(4)])
                    last.then_inc(f1_full, 1)

                def dft_channels(k):
                    pe.wait_ge(f1_ready, layer_at(l, N_F, k + 1))
                    if k >= 2:
                        pe.wait_ge(f2_ready, layer_at(l, N_F, k - 1))
                    b = 6 + k % 2
                    if k == 0:
                        a = acs[:, 0, :, :].rearrange("p a (g n) -> p (a g) n", n=256)
                        rc, rs = a[:, :, 0:P], a[:, :, P:256]
                    else:
                        rc, rs = acs[:, k % 2, 0, :], acs[:, k % 2, 1, :]
                    group(bank(b), [(const[:, C_COS:C_COS + P], rc),
                                    (const[:, C_NSIN:C_NSIN + P], rs)]).then_inc(f2_full, 1)

                dft_tokens(0)
                for k in range(1, 5):
                    dft_tokens(k)
                    dft_channels(k - 1)
                dft_channels(4)
                pe.wait_ge(f2_ready, layer_at(l, N_F, N_F))

                def attend(t, nk):
                    base = l * N_UNIT + t * UNITS
                    base_t = l * N_T + t * TURN_GROUPS
                    k0 = 0 if nk == 1 else P
                    pe.wait_ge(qcur_ready, l * NT + t + 1)

                    def scores(u):
                        if u >= 2:
                            pe.wait_ge(p_ready, base + u - 1)
                            pe.wait_ge(pT_ready, base_t + turn_group(u - 2, 0 if u < 6 else 1) + 1)
                        kc = u if u < 4 else 4
                        s0 = 1536 * (u % 2)
                        pieces = [(0, 0, P), (1, 0, P)]
                        if nk == 5:
                            pieces = [(0, 512, 640), (0, 0, 512), (1, 384, 640), (1, 0, 384)]
                        for m, a, e in pieces:
                            r = slice(64 * m, 64 * m + 64)
                            if nk == 5 and (m, a) == (1, 0):
                                pe.wait_ge(tail_full, (l * (NT - 1) + t - 1) * UNITS + u + 1)
                            last = mm(PS[:, s0 + 640 * m + a:s0 + 640 * m + e], qcur[r, u, :],
                                      kT[r, kc, k0 + a:k0 + e], start=True, stop=True)
                            if nk == 5 and (m, a) == (0, 512):
                                last.then_inc(tail_full, 1)
                        last.then_inc(s_full, 1)

                    def turn_probs(u, m):
                        if m == 0:
                            pe.wait_ge(w_ready, base + u + 1)
                            if u >= 1:
                                pe.wait_ge(pT_ready, base_t + turn_group(u, 0))
                        src = wd[:, u % 2, :] if u < 4 else prob[:, u % 2, m, :]
                        four, fifth = turned(u, m)
                        for k in range(nk):
                            last = turn(four[:, k * P:k * P + P] if k < 4 else fifth, src[:, k * P:k * P + P])
                        last.then_inc(t_full, 1)

                    def values(u):
                        maps = range(1 if u < 4 else 2)
                        pe.wait_ge(pT_ready, base_t + turn_group(u, maps[-1]) + 1)
                        if u >= 1 or nk == 5:
                            pe.wait_ge(o_ready, base + u)
                        kt = [0] if nk == 1 else list(range(1, 6))
                        for m in maps:
                            c = slice(u * P, u * P + P) if u < 4 else slice(512 + 64 * m, 576 + 64 * m)
                            n = c.stop - c.start
                            last = group(bank(7, P + n * m, P + n * m + n),
                                         [(pT[:, u % 2, m, i, :], V[:, k, c]) for i, k in enumerate(kt)])
                        last.then_inc(o_full, 1)

                    scores(0)
                    if nk == 5:
                        for k in range(4):
                            modulation(MOD2 + k, PS[0:2, 1536 + 256 * k:1792 + 256 * k], t - 1)
                        mod_columns(l * N_COL + t + 2, bank(6, 0, 16))
                    for u in range(UNITS):
                        if u + 1 < UNITS:
                            scores(u + 1)
                        for m in range(1 if u < 4 else 2):
                            turn_probs(u, m)
                        if u >= 1:
                            values(u - 1)
                    values(UNITS - 1)

                attend(0, 1)
                with pe.Fori(1, NT) as t:
                    attend(t, 5)

                for w in range(2):
                    pe.wait_ge(diag_ready, layer_at(l, 2, w + 1))
                    for s in range(2):
                        for h in range(2):
                            last = mm(bank(4 * w + 2 * s + h), const[:, C_ONE:C_ONE + P], diag[:, w, s, 4 * h:4 * h + 4, :],
                                      start=True, stop=True)
                    last.then_inc(row_full, 1)
                pe.wait_ge(row_ready, layer_at(l, 2, 2))

                pe.wait_ge(dn_ready, l + 1)
                for t in range(NT):
                    for h in range(2):
                        j = 2 * t + h
                        if j >= 4:
                            pe.wait_ge(br_ready, layer_at(l, N_BR, j - 3))
                        for c in range(4):
                            last = turn(bank(j % 4, c * P, c * P + P), oall[:, t, (4 * h + c) * P:(4 * h + c + 1) * P])
                        last.then_inc(br_full, 1)
                pe.wait_ge(br_ready, layer_at(l, N_BR, N_BR))

                for n in range(3):
                    for half in range(2):
                        slot = MERGE + 6 * n + 3 * half
                        wb = ring[:, (slot + 1) % RING, :].rearrange("p (c n) -> p c n", c=4)
                        for dc in range(4):
                            j = 8 * n + 4 * half + dc
                            g = j // 2
                            if dc % 2 == 0:
                                pe.wait_ge(mlo_ready, layer_at(l, N_MSPLIT, g + 1))
                            wg_hi = mhi[:, g % 2, :].rearrange("p (c n) -> p c n", c=KC)
                            wg_lo = ring_lo[:, split_slot(g) % RING, :].rearrange("p (c n) -> p c n", c=KC)
                            if j >= 2:
                                pe.wait_ge(mg_done, layer_at(l, N_MG, j - 1))
                            b = 4 * (j % 2)
                            g0 = (dc % 2) * P
                            for th in range(2):
                                ts = slice(th * TH, th * TH + TH)
                                for c in range(KC):
                                    three(bank(b + 2 + th, 0, TH), wg_hi[:, c, g0:g0 + P], wg_lo[:, c, g0:g0 + P],
                                          h_hi[:, c, ts], hT_lo[:, c, ts], c == 0, c == KC - 1)
                            if dc == 0:
                                wait_slot(pe, l, slot + 1)
                            for th in range(2):
                                ts = slice(th * TH, th * TH + TH)
                                src = [fT[:, c, ts] if n == 2 else brT[:, 4 * n + c, ts] for c in range(4)]
                                last = group(bank(b + th, 0, TH),
                                             [(wb[:, c, dc * P:dc * P + P], src[c]) for c in range(4)])
                            last.then_inc(mg_full, 1)
                pe.wait_ge(mg_done, layer_at(l, N_MG, N_MG - 1))

                for k in range(4):
                    pe.wait_ge(mlo_ready, layer_at(l, N_MSPLIT, 12 + k + 1))
                    w_hi = mhi[:, k % 2, :].rearrange("p (c n) -> p c n", c=KC)
                    w_lo = ring_lo[:, (OUT + k) % RING, :].rearrange("p (c n) -> p c n", c=KC)
                    for t in range(NT):
                        j = 5 * k + t
                        if j >= 4:
                            pe.wait_ge(out_done, layer_at(l, N_OUT, j - 3))
                        for c in range(KC):
                            if j == 0:
                                pe.wait_ge(mT_lo_ready, layer_at(l, KC, c + 1))
                            last = three(bank(j % 4, 0, 256), mT_hi[:, c, t * P:t * P + P], mT_lo[:, c, t * P:t * P + P],
                                         w_hi[:, c, :], w_lo[:, c, :], c == 0, c == KC - 1)
                        last.then_inc(out_full, 1)

                ln_turn(1, xn2, [0])

                pe.wait_ge(hT_ready, layer_at(l, N_HT, 12))
                keys = ring[:, POSITION[SUB], 0:1024].rearrange("p (h n) -> p h n", h=HEADS)

                def score_tile(t):
                    pe.wait_ge(qcur2_ready, l * NT + t + 1)
                    for h in range(HEADS):
                        for p in range(2):
                            r = slice(64 * p, 64 * p + 64)
                            last = mm(PS[:, 1024 * p + h * P:1024 * p + h * P + P], qcur2[r, h, :], keys[r, h, :],
                                      start=True, stop=True)
                    last.then_inc(sc_full, 1)

                def query(j, cols, w, toks):
                    if j >= 4:
                        pe.wait_ge(q_ready, layer_at(l, N_Q, j - 3))
                    for n, c0 in enumerate(cols):
                        size = toks.stop - toks.start
                        last = group(bank(4 + j % 4, n * size, n * size + size),
                                     [(w[:, c, c0:c0 + P], hT[:, c, toks]) for c in range(KC)])
                    last.then_inc(q_full, 1)

                for k in range(4):
                    wait_slot(pe, l, WQA + k)
                    w = ring[:, POSITION[WQA + k], :].rearrange("p (c n) -> p c n", c=KC)
                    query(k, (0, P), w, slice(0, P))
                wait_slot(pe, l, SUB)
                score_tile(0)
                pe.wait_ge(q_ready, layer_at(l, N_Q, 4))
                ln_turn(1, xn2, range(1, NT))
                pe.wait_ge(hT_ready, layer_at(l, N_HT, N_HT))
                for k in range(4):
                    wait_slot(pe, l, WQB + k)
                    w = ring[:, POSITION[WQB + k], :].rearrange("p (c n) -> p c n", c=KC)
                    for hh in range(2):
                        query(4 + 2 * k + hh, (hh * P,), w, slice(P, T))

                def expand_tile(t, final=False):
                    pe.wait_ge(idx_ready, l * NT + t + 1)
                    for n in range(3):
                        last = turn(bank(4, n * P, n * P + P), idx[:, n, :])
                    last.then_inc(idxT_full, 1)
                    if not final:
                        score_tile(t + 1)
                    with pe.Fori(0, P // 16) as i:
                        for u in range(4):
                            pe.wait_ge(oh_ready, l * N_QUAD + t * QUADS + i * 4 + (u + 1))
                            for k in range(4):
                                last = mm(bank(4 + u, k * P, k * P + P), ohA[:, u, k, :], ohB[:, u % 2, k, :],
                                          start=True, stop=True)
                            last.then_inc(quad_full, 1)

                with pe.Fori(0, NT - 1) as t:
                    expand_tile(t)
                expand_tile(NT - 1, final=True)

                pe.wait_ge(quad_ready, layer_at(l, N_QUAD, N_QUAD))
                pe.wait_ge(hlo_ready, l + 1)

                def up(b, s, wait_gelu=True):
                    uh = ring_hi[:, s, :].rearrange("p (c j n) -> p c j n", c=KC, j=2)
                    ul = ring_lo[:, s, :].rearrange("p (c j n) -> p c j n", c=KC, j=2)
                    for j in range(2):
                        if wait_gelu:
                            pe.wait_ge(gelu_ready, l * (2 * NB) + b * 2 + (j - 1))
                        for c in range(KC):
                            for th in range(2):
                                ts = slice(th * TH, th * TH + TH)
                                last = three(bank(2 * j + th, 0, TH), uh[:, c, j, :], ul[:, c, j, :],
                                             hT_hi[:, c, ts], hT_lo[:, c, ts], c == 0, c == KC - 1)
                        last.then_inc(h_full, 1)

                def down(b, s, par, first=False):
                    vh = ring_hi[:, s, :].rearrange("p (j n) -> p j n", j=2)
                    vl = ring_lo[:, s, :].rearrange("p (j n) -> p j n", j=2)
                    pe.wait_ge(W_ready, l * N_W + b * 2 + 2)
                    for n in range(10):
                        t, dh = n // 2, n % 2
                        if not (first and n < 4):
                            pe.wait_ge(v_done, l * N_V + b * 10 + (n - 3))
                        for j in range(2):
                            last = three(bank(4 + (10 * par + n) % 4), W_hi[:, par, j, t * P:t * P + P],
                                         W_lo[:, par, j, t * P:t * P + P], vh[:, j, dh * 512:dh * 512 + 512],
                                         vl[:, j, dh * 512:dh * 512 + 512], j == 0, j == 1)
                        last.then_inc(v_full, 1)

                def split_wait(n):
                    pe.wait_ge(split_ready, l * N_SPLIT + n + 1)

                split_wait(0)
                up(0, PEER % RING, wait_gelu=False)
                split_wait(1)
                up(1, 1)
                split_wait(2)
                down(0, 2, 0, first=True)
                split_wait(3)
                up(2, 3)
                split_wait(4)
                down(1, 0, 1)
                with pe.Fori(1, NB // 2 - 1) as i:
                    split_wait(i * 4 + 1)
                    up(i * 2 + 1, 1)
                    split_wait(i * 4 + 2)
                    down(i * 2, 2, 0)
                    split_wait(i * 4 + 3)
                    up(i * 2 + 2, 3)
                    split_wait(i * 4 + 4)
                    down(i * 2 + 1, 0, 1)
                split_wait(2 * NB - 3)
                up(NB - 1, 1)
                split_wait(2 * NB - 2)
                down(NB - 2, 2, 0)
                split_wait(2 * NB - 1)
                down(NB - 1, 3, 1)

        @block.scalar
        def _(act):
            A = nc.scalar.activation
            act.wait_ge(setup, 48)
            A(cnds[:, :, :], cnd[:, :, :], ACT.Silu).then_inc(cond_ready, 1)
            used = lamw[:, 11:12]
            nc.scalar.copy(used, const[:, 0:1]).then_inc(tile_expanded, 1)

            with act.Fori(0, LAYERS) as l:
                def root(k, n, n0=0):
                    act.wait_ge(var_ready, layer_at(l, N_STD, k + 1))
                    A(std[:, n0:n], var[:, n0:n], ACT.Sqrt).then_inc(std_ready, 1)

                def modulate(part, tiles):
                    for t in tiles:
                        s = 0 if t == 0 else 1
                        for h in range(2):
                            j = 10 * part + 2 * t + h
                            act.wait_ge(xT_full, layer_at(l, N_HT, j + 1))
                            for c in range(4):
                                k = 4 * h + c
                                q = 24 * part + k
                                last = A(hT[:, k, t * P:t * P + P], bank(4 + j % 4, c * P, c * P + P), ACT.Identity,
                                         bias=modc[:, q, s:s + 1], scale=modc[:, q + 8, s:s + 1])
                            last.then_inc(hT_ready, 1)

                def mod_rows(slots, n, src):
                    act.wait_ge(mod_full, slots)
                    if n is not None:
                        act.wait_ge(col_full, n)
                    nc.scalar.copy(mrow[0:2, :], src).then_inc(mrow_ready, 1)

                for n in range(2):
                    mod_rows(layer_at(l, N_MOD, 4 * n + 4), layer_at(l, N_COL, n) if n else None, PS[0:2, 1024 * n:1024 * n + 1024])

                root(0, NT)
                act.wait_ge(lam_sum, l + 1)
                A(lamw[:, 2:4], lamw[:, 0:2], ACT.Exp).then_inc(lam_exp, 1)

                def in_slot_hi(k):
                    if k < N_IN:
                        wait_slot(act, l, GQ + k)
                        nc.scalar.copy(in_hi[k % 2][:, :], ring[:, POSITION[GQ + k], :]).then_inc(in_hi_ready, 1)

                in_slot_hi(0)
                in_slot_hi(1)
                act.wait_ge(mod_ready, layer_at(l, 2, 1))
                modulate(0, range(NT))
                act.drain()
                act.wait_ge(x_away, 16 * (l + 1))
                for t in range(NT):
                    nc.scalar.copy(h_hi[:, :, t * P:t * P + P], hT[:, :, t * P:t * P + P]).then_inc(h_hi_ready, 1)

                def project(k):
                    for t in range(NT):
                        j = 5 * k + t
                        act.wait_ge(z_full, layer_at(l, N_Z, j + 1))
                        src = bank(j % 4, 0, 256)
                        if k < 2:
                            dst = z[:, 0, t, :].rearrange("p (c v d) -> p c v d", c=4, v=2)[:, :, k, :]
                            last = nc.scalar.copy(dst, src.rearrange("p (c d) -> p c d", c=4))
                        elif k == 2:
                            nc.scalar.copy(zk[:, t, :], src[:, 0:P])
                            last = nc.scalar.copy(V[:, t, 512:640], src[:, P:256])
                        else:
                            n = (k - 3) // 2
                            cols = slice(256 * ((k - 3) % 2), 256 * ((k - 3) % 2) + 256)
                            dst = [z[:, 1, t, cols], z[:, 0, t, cols], V[:, t, cols], z[:, 1, t, cols]][n]
                            last = nc.scalar.copy(dst, src)
                        last.then_inc(z_ready, 1)
                    in_slot_hi(k + 2)

                tr = [0]

                def qk_out(dst, n):
                    j = tr[0]
                    act.wait_ge(tr_full, layer_at(l, N_TR, j + 1))
                    src = bank(4 + j % 2, 0, n * P)
                    if dst.ndim == 3:
                        src = src.rearrange("p (c n) -> p c n", c=n)
                    nc.scalar.copy(dst, src).then_inc(tr_ready, 1)
                    tr[0] += 1

                for k in range(3):
                    project(k)
                root(1, 50)
                for k in range(3, 5):
                    project(k)
                for t in range(NT):
                    qk_out(qT[:, 4:8, t * P:t * P + P], 4)
                qk_out(kT[:, 4, 0:512], 4)
                qk_out(kT[:, 4, 512:768], 2)
                for k in range(5, 7):
                    project(k)
                for t in range(NT):
                    qk_out(qT[:, 0:4, t * P:t * P + P], 4)
                for k in range(7, 9):
                    project(k)
                for t in range(NT + 1):
                    qk_out(kT[:, 0:4, t * P:t * P + P], 4)
                for k in range(9, 11):
                    project(k)

                def dft_out1(k):
                    act.wait_ge(f1_full, layer_at(l, N_F, k + 1))
                    nc.scalar.copy(acs[:, k % 2, :, :].rearrange("p a n -> p (a n)"),
                                   PS[:, 2048:3072]).then_inc(f1_ready, 1)

                def dft_out2(k):
                    act.wait_ge(f2_full, layer_at(l, N_F, k + 1))
                    src = bank(6 + k % 2)
                    if k == 0:
                        nc.scalar.copy(fT[:, :, 0:P], src.rearrange("p (g n) -> p g n", g=4)).then_inc(f2_ready, 1)
                    else:
                        nc.scalar.copy(fT[:, k - 1, P:T], src).then_inc(f2_ready, 1)

                dft_out1(0)
                for k in range(1, 5):
                    dft_out1(k)
                    dft_out2(k - 1)
                dft_out2(4)

                def attend(t, nk):
                    base = l * N_UNIT + t * UNITS
                    base_t = l * N_T + t * TURN_GROUPS
                    w = nk * P
                    cols = slice(0, P) if nk == 1 else bass.ds(t * P, P)
                    nc.scalar.copy(qcur[:, :, :], qT[:, :, cols]).then_inc(qcur_ready, 1)

                    def exps(u):
                        act.wait_ge(mx_ready, base + u + 1)
                        if u >= 2:
                            act.wait_ge(t_full, base_t + turn_group(u - 2, 0 if u < 6 else 1) + 1)
                        s0 = 1536 * (u % 2)
                        for m in range(2):
                            last = A(prob[:, u % 2, m, 0:w], PS[:, s0 + m * 640:s0 + m * 640 + w], ACT.Exp,
                                     bias=nbias[:, u % 2, m:m + 1], scale=SCALE, accum_out=rsum[:, u % 2, m:m + 1])
                        last.then_inc(p_ready, 1)

                    def probs_out(u, m):
                        act.wait_ge(t_full, base_t + turn_group(u, m) + 1)
                        if u >= 2 and m == 0:
                            act.wait_ge(o_full, base + u - 1)
                        four, fifth = turned(u, m)
                        if nk == 1:
                            nc.scalar.copy(pT[:, u % 2, m, 0, :], four[:, 0:P]).then_inc(pT_ready, 1)
                        else:
                            nc.scalar.copy(pT[:, u % 2, m, 0:4, :].rearrange("p k n -> p (k n)"), four)
                            nc.scalar.copy(pT[:, u % 2, m, 4, :], fifth).then_inc(pT_ready, 1)

                    exps(0)
                    if nk == 5:
                        mod_rows(l * N_MOD + 8 + t * 4, l * N_COL + t + 1, PS[0:2, 1536:2560])
                    for u in range(UNITS):
                        for m in range(1 if u < 4 else 2):
                            probs_out(u, m)
                        if u + 1 < UNITS:
                            exps(u + 1)
                    act.wait_ge(o_full, base + UNITS)

                attend(0, 1)
                with act.Fori(1, NT) as t:
                    attend(t, 5)

                for w, dst in enumerate((gate1, gate2)):
                    act.wait_ge(row_full, layer_at(l, 2, w + 1))
                    nc.scalar.copy(dst[:, :, :].rearrange("p s n -> p (s n)"),
                                   PS[:, 2048 * w:2048 * w + 2048]).then_inc(row_ready, 1)
                act.wait_ge(row_ready, layer_at(l, 2, 2))
                act.dma_start(x_mix[:, :, :], x_wait[bass.ds(l, 1)].rearrange("o t p d -> p (o t) d")).then_inc(x_back, 16)
                root(2, 20)
                for t in range(NT):
                    for h in range(2):
                        j = 2 * t + h
                        act.wait_ge(br_full, layer_at(l, N_BR, j + 1))
                        nc.scalar.copy(brT[:, 4 * h:4 * h + 4, t * P:t * P + P],
                                       bank(j % 4).rearrange("p (c n) -> p c n", c=4)).then_inc(br_ready, 1)

                def slot_hi(g):
                    wait_slot(act, l, split_slot(g))
                    nc.scalar.copy(mhi[:, g % 2, :], ring[:, split_slot(g) % RING, :]).then_inc(mhi_ready, 1)

                def merged_hi(c):
                    act.wait_ge(mg_done, layer_at(l, N_MG, 16 + c + 1))
                    nc.scalar.copy(mT_hi[:, c, :], mT[:, c, :]).then_inc(mT_hi_ready, 1)

                slot_hi(0)
                slot_hi(1)
                for j in range(N_MG):
                    act.wait_ge(mg_full, layer_at(l, N_MG, j + 1))
                    if j >= 2:
                        act.wait_ge(mg_done, layer_at(l, N_MG, j - 1))
                    A(sg[:, j % 2, :].rearrange("p (h n) -> p h n", h=2), two_banks(4 * (j % 2) + 2, TH),
                      ACT.Sigmoid).then_inc(sg_ready, 1)
                    if j % 2:
                        slot_hi(j // 2 + 2)
                    if j >= 17:
                        merged_hi(j - 17)
                merged_hi(7)
                for g in (14, 15):
                    act.wait_ge(out_full, layer_at(l, N_OUT, 5 * (g - 13)))
                    slot_hi(g)

                root(3, NT)
                root(4, 1)
                act.wait_ge(mod_ready, layer_at(l, 2, 2))
                modulate(1, [0])
                root(5, NT, 1)

                for j in range(4):
                    act.wait_ge(q_full, layer_at(l, N_Q, j + 1))
                    nc.scalar.copy(qT2[:, 2 * j:2 * j + 2, 0:P],
                                   bank(4 + j, 0, 256).rearrange("p (h n) -> p h n", h=2)).then_inc(q_ready, 1)
                act.drain()

                def query_tile(t):
                    cols = slice(t * P, t * P + P) if isinstance(t, int) else bass.ds(t * P, P)
                    nc.scalar.copy(qcur2[:, :, :], qT2[:, :, cols]).then_inc(qcur2_ready, 1)

                def copy_scores(t):
                    act.wait_ge(sc_full, l * NT + t + 1)
                    nc.scalar.copy(score[:, :, :].rearrange("p s n -> p (s n)"), PS[:, 0:2048]).then_inc(score_ready, 1)

                def expand_tile(t, first=False, final=False):
                    if not final:
                        query_tile(t + 1)
                    act.wait_ge(best_ready, l * NT + t + 1)
                    A(pw[:, :, :], pv[:, :, :], ACT.Exp).then_inc(exp_ready, 1)
                    act.wait_ge(idxT_full, l * NT + t + 1)
                    nc.scalar.copy(idxT[:, :, :].rearrange("p a n -> p (a n)"), bank(4, 0, 3 * P)).then_inc(idxT_ready, 1)
                    if not final:
                        copy_scores(t + 1)
                    for half in range(2):
                        if not first:
                            act.wait_ge(g_stored[half], 16 * (l * NT + t))
                        st = stg[:, half, :, :, :].rearrange("p b j t -> p (b j) t")
                        with act.Fori(0, 4) as i:
                            for u in range(4):
                                act.wait_ge(quad_full, l * N_QUAD + t * QUADS + i * 4 + (16 * half + u + 1))
                                nc.scalar.copy(st[:, :, bass.ds(i * 16 + 4 * u, 4)],
                                               bank(4 + u).rearrange("p (t j) -> p j t", t=4)).then_inc(quad_ready, 1)
                        act.wait_ge(quad_ready, l * N_QUAD + t * QUADS + 16 * (half + 1))
                        act.dma_start(
                            gate_matrix.rearrange("b p (g n) -> p b g n", g=2 * NT)[:, :, bass.ds(t * 2 + half, 1), :]
                            .rearrange("p b g n -> p b (g n)"),
                            stg[:, half, :, :, :].rearrange("p b j t -> p b (j t)")).then_inc(g_stored[half], 16)
                    nc.scalar.copy(used, const[:, 0:1]).then_inc(tile_expanded, 1)

                wait_slot(act, l, SUB)
                query_tile(0)
                copy_scores(0)
                modulate(1, range(1, NT))
                for j in range(4, N_Q):
                    act.wait_ge(q_full, layer_at(l, N_Q, j + 1))
                    nc.scalar.copy(qT2[:, j - 4, P:T], bank(4 + j % 4)).then_inc(q_ready, 1)
                act.drain()
                expand_tile(0, first=True)
                with act.Fori(1, NT - 1) as t:
                    expand_tile(t)
                expand_tile(NT - 1, final=True)
                for half in range(2):
                    act.wait_ge(g_stored[half], layer_at(l, 16 * NT, 16 * NT))

                nc.scalar.copy(hT_hi[:, :, :], hT[:, :, :]).then_inc(hhi_ready, 1)

                def split_hi(s, n):
                    act.wait_ge(slot_full[s], 16 * (l * FILLS[s] + n + (POSITION[:PEER].count(s) + 1)))
                    nc.scalar.copy(ring_hi[:, s, :], ring[:, s, :]).then_inc(hi_ready, 1)

                def gelu(b, j, buf_wait=True):
                    act.wait_ge(h_full, l * (2 * NB) + b * 2 + (j + 1))
                    if buf_wait:
                        act.wait_ge(W_ready, l * N_W + b * 2 + (j - 1))
                    A(act_g[:, j, :].rearrange("p (h n) -> p h n", h=2), two_banks(2 * j, TH),
                      ACT.Gelu).then_inc(gelu_ready, 1)

                split_hi(0, 0)
                split_hi(1, 0)
                split_hi(2, 0)
                gelu(0, 0, False)
                gelu(0, 1, False)
                with act.Fori(0, NB // 2 - 1) as i:
                    for u in range(2):
                        gelu(i * 2 + (u + 1), 0)
                        s = (3 + 2 * u) % RING
                        split_hi(s, i + (3 + 2 * u) // RING)
                        gelu(i * 2 + (u + 1), 1)
                        s = (4 + 2 * u) % RING
                        split_hi(s, i + (4 + 2 * u) // RING)
                gelu(NB - 1, 0)
                split_hi(3, NB // 2 - 1)
                gelu(NB - 1, 1)
                root(6, NT)

        @block.vector
        def _(dve):
            tt, ts_, copy = nc.vector.tensor_tensor, nc.vector.tensor_scalar, nc.vector.tensor_copy
            stt = nc.vector.scalar_tensor_tensor
            reduce = nc.vector.tensor_reduce
            dve.wait_ge(setup, 48)
            for _ in range(2):
                nc.vector.memset(lamw[:, 10:11], 0.0).then_inc(ring_free, 1)
                dve.drain()
            copy(lamw[:, 8:10], const[:, 0:2]).then_inc(layer_free, 1)

            with dve.Fori(0, LAYERS) as l:
                def root_wait(k):
                    dve.wait_ge(std_ready, layer_at(l, N_STD, k + 1))

                def statistics(src, tiles=range(NT)):
                    for t in tiles:
                        for h in range(2):
                            nc.vector.bn_stats(stats[:, t, h, :], src[:, t, 512 * h:512 * h + 512])
                    aggregate(tiles)

                def aggregate(tiles=range(NT)):
                    a, e = tiles[0], tiles[-1] + 1
                    dve.drain()
                    for t in tiles:
                        nc.vector.bn_aggr(mv[:, t, :], stats[:, t, :, :].rearrange("p a b -> p (a b)"))
                    dve.drain()
                    ts_(var[:, a:e], mv[:, a:e, 1], EPS, None, ALU.add).then_inc(var_ready, 1)

                def inverse_root(k, tiles=range(NT)):
                    a, e = tiles[0], tiles[-1] + 1
                    root_wait(k)
                    nc.vector.reciprocal(rstd[:, a:e], std[:, a:e])
                    dve.drain()

                def h_low(t):
                    ts = slice(t * P, t * P + P)
                    dve.wait_ge(h_hi_ready, layer_at(l, NT, t + 1))
                    tt(hT_lo[:, :, ts], hT[:, :, ts], h_hi[:, :, ts].bitcast(F32), ALU.subtract).then_inc(h_lo_ready, 1)

                def normalise(t, dst):
                    return ts_(dst, x[:, t, :], mv[:, t, 0:1], rstd[:, t:t + 1], ALU.subtract, ALU.mult)

                def post_norm(src, rows_sb, tiles):
                    for t in tiles:
                        stt(x[:, t, :], src[:, t, :], mv[:, t, 0:1], rows_sb[:, 0, :], ALU.subtract, ALU.mult)
                    dve.drain()
                    for t in tiles:
                        last = stt(x[:, t, :], x[:, t, :], rstd[:, t:t + 1], rows_sb[:, 1, :], ALU.mult, ALU.add)
                    return last

                statistics(x)
                inverse_root(0)
                for t in range(2):
                    normalise(t, xn[:, t, :]).then_inc(xn_ready, 1)

                dve.wait_ge(params, layer_at(l, 16 * PARAM_DMAS, 16 * PARAM_DMAS))

                lv = row[:, 0:256].rearrange("p (a b d) -> p a b d", a=2, b=2)
                tt(lamp[:, :, :], lv[:, :, 0, :], lv[:, :, 1, :], ALU.mult)
                dve.drain()
                reduce(lamw[:, 0:2], lamp[:, :, :], AX.X, ALU.add).then_inc(lam_sum, 1)
                dve.wait_ge(lam_exp, l + 1)
                tt(lamw[:, 4:5], lamw[:, 2:3], lamw[:, 3:4], ALU.subtract)
                copy(lamw[:, 6:7], const[:, bass.ds(l * 2 + (C_LAM + 1), 1)])
                dve.drain()
                tt(lamw[:, 4:5], lamw[:, 4:5], const[:, bass.ds(l * 2 + C_LAM, 1)], ALU.add)
                dve.drain()
                ts_(lamw[:, 5:6], lamw[:, 4:5], -1.0, None, ALU.mult)

                dve.wait_ge(col_full, layer_at(l, N_COL, 2))
                cols = PS[:, 0:64].rearrange("p (q s) -> p q s", s=2)
                tt(modc[:, 0:8, :], cols[:, 0:8, :], bc[:, 0:8].unsqueeze(2).broadcast_to([P, 8, 2]), ALU.add)
                stt(modc[:, 8:16, :], cols[:, 8:16, :], 1.0, bc[:, 8:16].unsqueeze(2).broadcast_to([P, 8, 2]),
                    ALU.add, ALU.add).then_inc(mod_ready, 1)

                for t in range(2, NT):
                    dve.wait_ge(xT_full, layer_at(l, N_HT, 2 * (t - 1)))
                    normalise(t, xn[:, t % 2, :]).then_inc(xn_ready, 1)
                for t in range(NT):
                    h_low(t)

                def rotary(v, heads):
                    e = v.rearrange("p t h (f two) -> p t h f two", two=2)
                    xe, xo = e[:, :, :, :, 0], e[:, :, :, :, 1]
                    c = ropec.unsqueeze(2).broadcast_to([P, 4, heads, 32])
                    s = ropes.unsqueeze(2).broadcast_to([P, 4, heads, 32])
                    r = [rot[:, n, 0:4 * heads * 32].rearrange("p (t h f) -> p t h f", t=4, h=heads) for n in range(4)]
                    tt(r[0], xe, c, ALU.mult)
                    tt(r[1], xo, s, ALU.mult)
                    tt(r[2], xe, s, ALU.mult)
                    tt(r[3], xo, c, ALU.mult)
                    dve.drain()
                    tt(xe, r[0], r[1], ALU.subtract)
                    return tt(xo, r[2], r[3], ALU.add)

                gq = z[:, 0, :, :].rearrange("p t (h d) -> p (t h) d", d=64)
                gk = zk[:, :, :].rearrange("p t (h d) -> p (t h) d", d=64)
                dve.wait_ge(z_ready, layer_at(l, N_Z, 15))
                for v, n0, n in ((gq, 0, 40), (gk, 40, 10)):
                    tmp = sq[:, 0:64 * n].rearrange("p (n d) -> p n d", d=64)
                    tt(tmp, v, v, ALU.mult)
                    dve.drain()
                    reduce(var[:, n0:n0 + n], tmp, AX.X, ALU.add)
                    dve.drain()
                ts_(var[:, 0:50], var[:, 0:50], 1.0 / 64, EPS, ALU.mult, ALU.add).then_inc(var_ready, 1)
                root_wait(1)
                nc.vector.reciprocal(rstd[:, 0:50], std[:, 0:50])
                dve.drain()
                for v, n0, n, g0 in ((gq, 0, 40, 256), (gk, 40, 10, 320)):
                    tt(v, v, rstd[:, n0:n0 + n].unsqueeze(2).broadcast_to([P, n, 64]), ALU.mult)
                    dve.drain()
                    tt(v, v, row[:, g0:g0 + 64].unsqueeze(1).broadcast_to([P, n, 64]), ALU.mult)
                    dve.drain()
                rotary(z[:, 0, 1:NT, :].rearrange("p t (h d) -> p t h d", d=64), 8).then_inc(blk_ready, 1)
                dve.drain()
                rotary(zk[:, 1:NT, :].rearrange("p t (h d) -> p t h d", d=64), 2).then_inc(blk_ready, 1)
                for buf, done in ((1, 25), (0, 35)):
                    dve.drain()
                    dve.wait_ge(z_ready, layer_at(l, N_Z, done))
                    rotary(z[:, buf, 1:NT, :].rearrange("p t (h d) -> p t h d", d=64), 8).then_inc(blk_ready, 1)

                dve.wait_ge(kv_stored, 64 * (l + 1))
                dve.wait_ge(f2_full, layer_at(l, N_F, N_F))

                def attend(t, nk):
                    base = l * N_UNIT + t * UNITS
                    base_t = l * N_T + t * TURN_GROUPS
                    w = nk * P
                    tile_rows = oall[:, 0, :] if nk == 1 else oall[:, bass.ds(t, 1), :].rearrange("p o d -> p (o d)")

                    def maxima(u):
                        dve.wait_ge(s_full, base + u + 1)
                        s0 = 1536 * (u % 2)
                        s = PS[:, s0:s0 + 1280].rearrange("p (m n) -> p m n", m=2)[:, :, 0:w]
                        reduce(smx[:, u % 2, :], s, AX.X, ALU.max)
                        dve.drain()
                        ts_(nbias[:, u % 2, :], smx[:, u % 2, :], -SCALE, None, ALU.mult).then_inc(mx_ready, 1)

                    def weights_of(u):
                        b = u % 2
                        dve.wait_ge(p_ready, base + u + 1)
                        if u >= 4:
                            nc.vector.reciprocal(rinv[:, u % 4, :], rsum[:, b, :]).then_inc(w_ready, 1)
                            return
                        nc.vector.reciprocal(rinv[:, u % 4, :], rsum[:, b, :])
                        dve.drain()
                        tt(rneg[:, b:b + 1], rinv[:, u % 4, 1:2], lamw[:, 5:6], ALU.mult)
                        dve.drain()
                        ts_(prob[:, b, 1, 0:w], prob[:, b, 1, 0:w], rneg[:, b:b + 1], None, ALU.mult)
                        dve.drain()
                        if u >= 2:
                            dve.wait_ge(t_full, base_t + u - 1)
                        stt(wd[:, b, 0:w], prob[:, b, 0, 0:w], rinv[:, u % 4, 0:1], prob[:, b, 1, 0:w],
                            ALU.mult, ALU.add).then_inc(w_ready, 1)

                    def outputs(u):
                        dve.wait_ge(o_full, base + u + 1)
                        if u < 4:
                            last = copy(tile_rows[:, u * P:u * P + P], bank(7, P, 2 * P))
                        else:
                            for m in range(2):
                                c = 512 + (4 * m + u - 4) * 64
                                last = ts_(tile_rows[:, c:c + 64], bank(7, P + 64 * m, P + 64 * m + 64),
                                           rinv[:, u % 4, m:m + 1], None, ALU.mult)
                        last.then_inc(o_ready, 1)

                    maxima(0)
                    if nk == 5:
                        dve.wait_ge(col_full, l * N_COL + t + 2)
                        tt(modc[:, bass.ds(t * 8 + 8, 8), :], bank(6, 0, 16).rearrange("p (q s) -> p q s", s=2),
                           bc[:, bass.ds(t * 8 + 8, 8)].unsqueeze(2).broadcast_to([P, 8, 2]), ALU.add)
                    for u in range(UNITS):
                        weights_of(u)
                        if u + 1 < UNITS:
                            maxima(u + 1)
                        if u >= 1:
                            outputs(u - 1)
                    outputs(UNITS - 1)
                    dve.drain()

                attend(0, 1)
                with dve.Fori(1, NT) as t:
                    attend(t, 5)

                for w, q in ((0, 16), (1, 40)):
                    for s in range(2):
                        last = tt(diag[:, w, s, :, :], ident.unsqueeze(1).broadcast_to([P, KC, P]),
                                  modc[:, q:q + 8, s:s + 1].broadcast_to([P, KC, P]), ALU.mult)
                    last.then_inc(diag_ready, 1)
                ts_(modc[:, 32:40, :], modc[:, 32:40, :], 1.0, None, ALU.add).then_inc(mod_ready, 1)

                dv4 = oall[:, :, 0:512].rearrange("p t (h d) -> p t h d", d=P)
                s4 = sq[:, :].rearrange("p (t h d) -> p t h d", t=NT, h=4)
                tt(s4, dv4, dv4, ALU.mult)
                dve.drain()
                reduce(var[:, 0:20], sq[:, :].rearrange("p (n d) -> p n d", d=P), AX.X, ALU.add)
                dve.drain()
                ts_(var[:, 0:20], var[:, 0:20], 1.0 / P, EPS, ALU.mult, ALU.add).then_inc(var_ready, 1)
                root_wait(2)
                nc.vector.reciprocal(rstd[:, 0:20], std[:, 0:20])
                dve.drain()
                ts_(rstd[:, 0:20], rstd[:, 0:20], lamw[:, 6:7], None, ALU.mult)
                dve.drain()
                tt(dv4, dv4, rstd[:, 0:20].rearrange("p (t h) -> p t h", t=NT).unsqueeze(3).broadcast_to([P, NT, 4, P]),
                   ALU.mult)
                dve.drain()
                tt(dv4, dv4, row[:, 384:512].unsqueeze(1).unsqueeze(1).broadcast_to([P, NT, 4, P]),
                   ALU.mult).then_inc(dn_ready, 1)

                def slot_lo(g):
                    p = split_slot(g) % RING
                    dve.wait_ge(mhi_ready, layer_at(l, N_MSPLIT, g + 1))
                    tt(ring_lo[:, p, :], ring[:, p, :], mhi[:, g % 2, :].bitcast(F32), ALU.subtract).then_inc(mlo_ready, 1)

                def merged_lo(c):
                    dve.wait_ge(mT_hi_ready, layer_at(l, KC, c + 1))
                    tt(mT_lo[:, c, :], mT[:, c, :], mT_hi[:, c, :].bitcast(F32), ALU.subtract).then_inc(mT_lo_ready, 1)

                slot_lo(0)
                slot_lo(1)
                for j in range(N_MG):
                    n, dc = j // 8, j % 8
                    b = 4 * (j % 2)
                    dve.wait_ge(sg_ready, layer_at(l, N_MG, j + 1))
                    s = sg[:, j % 2, :].rearrange("p (h n) -> p h n", h=2)
                    m = mT[:, dc, :].rearrange("p (h n) -> p h n", h=2)
                    tm = mtmp[:, :].rearrange("p (h n) -> p h n", h=2)
                    if n == 0:
                        tt(m, two_banks(b, TH), s, ALU.mult).then_inc(mg_done, 1)
                    else:
                        tt(tm, two_banks(b, TH), s, ALU.mult)
                        dve.drain()
                        tt(m, m, tm, ALU.add).then_inc(mg_done, 1)
                        dve.drain()
                    if j % 2:
                        slot_lo(j // 2 + 2)
                    if j >= 18:
                        merged_lo(j - 18)
                merged_lo(6)
                merged_lo(7)

                dve.wait_ge(x_back, 16 * (l + 1))
                for j in range(N_OUT):
                    k, t = j // 5, j % 5
                    s = 0 if t == 0 else 1
                    cols = slice(256 * k, 256 * k + 256)
                    dve.wait_ge(out_full, layer_at(l, N_OUT, j + 1))
                    tt(otmp[:, j % 2, :], bank(j % 4, 0, 256), gate1[:, s, cols], ALU.mult)
                    dve.drain()
                    stt(x_mix[:, t, cols], x_mix[:, t, cols], ALPHA, otmp[:, j % 2, :], ALU.mult, ALU.add).then_inc(out_done, 1)
                    if j in (4, 9):
                        slot_lo(13 + (j + 1) // 5)
                dve.drain()
                dve.wait_ge(ln1_rows, 16 * (l + 1))
                statistics(x_mix)
                inverse_root(3)
                post_norm(x_mix, lnr, [0])
                dve.drain()
                statistics(x, [0])
                post_norm(x_mix, lnr, [1])
                inverse_root(4, [0])
                normalise(0, xn2[:, 0, :]).then_inc(xn_ready, 1)
                post_norm(x_mix, lnr, [2, 3, 4])
                dve.drain()
                others = range(1, NT)
                statistics(x, others)
                inverse_root(5, others)
                for t in others:
                    normalise(t, xn2[:, t, :]).then_inc(xn_ready, 1)

                scores = score
                with dve.Fori(0, NT) as t:
                    dve.wait_ge(score_ready, l * NT + t + 1)
                    nc.vector.memset(pm[:, :], 0.0)
                    for s in range(16):
                        nc.vector.max(sv[:, s, 0:8], scores[:, s, :])
                    dve.drain()
                    dve.wait_ge(tile_expanded, l * NT + t + 1)
                    nc.vector.memset(pm[:, :], 0.0)
                    for s in range(16):
                        nc.vector.match_replace(work[:, s, :], sv[:, s, 0:8], scores[:, s, :], LOWEST)
                        nc.vector.max_index(si[:, s, 0:8], sv[:, s, 0:8], scores[:, s, :])
                    dve.drain()
                    for s in range(16):
                        nc.vector.max(sv[:, s, 8:16], work[:, s, :])
                    dve.drain()
                    for s in range(16):
                        nc.vector.max_index(si[:, s, 8:16], sv[:, s, 8:16], work[:, s, :])
                    c4 = cand[:, :, :].rearrange("p h (i j) -> p h i j", i=TOPK)
                    tt(c4, sv[:, 0:8, :].unsqueeze(3).broadcast_to([P, 8, TOPK, TOPK]),
                       sv[:, 8:16, :].unsqueeze(2).broadcast_to([P, 8, TOPK, TOPK]), ALU.add)
                    dve.drain()
                    copy(sif[:, :, :], si[:, :, :])
                    c2 = work[:, :, :].rearrange("p s n -> p (s n)").rearrange("p (h n) -> p h n", h=8)
                    for h in range(HEADS):
                        nc.vector.max(pv[:, h, 0:8], cand[:, h, :])
                    dve.drain()
                    for h in range(HEADS):
                        nc.vector.match_replace(c2[:, h, :], pv[:, h, 0:8], cand[:, h, :], LOWEST)
                        nc.vector.max_index(pi[:, h, 0:8], pv[:, h, 0:8], cand[:, h, :])
                    dve.drain()
                    for h in range(HEADS):
                        nc.vector.max(pv[:, h, 8:16], c2[:, h, :])
                    dve.drain()
                    for h in range(HEADS):
                        nc.vector.max_index(pi[:, h, 8:16], pv[:, h, 8:16], c2[:, h, :])
                    copy(pm[:, 8:16], pv[:, :, 0])
                    dve.drain()
                    tt(pv[:, :, :], pv[:, :, :], pm[:, 8:16].unsqueeze(2).broadcast_to([P, 8, TOPK]),
                       ALU.subtract).then_inc(best_ready, 1)
                    flat = pi[:, :, :].rearrange("p h k -> p (h k)")
                    ts_(pii[:, 0, :], flat, 4, None, ALU.logical_shift_right)
                    ts_(pii[:, 1, :], flat, 15, None, ALU.bitwise_and)
                    dve.drain()
                    copy(pif[:, :, :], pii[:, :, :])
                    dve.drain()
                    eq = cand[:, :, :].rearrange("p h (k m) -> p h k m", k=TOPK)
                    for p in range(2):
                        place = pif[:, p, :].unsqueeze(2).broadcast_to([P, P, TOPK])
                        tt(cand[:, :, :].rearrange("p h (k m) -> p (h k) m", k=TOPK),
                           iota[:, 0:TOPK].unsqueeze(1).broadcast_to([P, P, TOPK]), place, ALU.is_equal)
                        dve.drain()
                        tt(eq, eq, sif[:, 8 * p:8 * p + 8, :].unsqueeze(2).broadcast_to([P, 8, TOPK, TOPK]), ALU.mult)
                        dve.drain()
                        reduce(idx[:, p, :], cand[:, :, :].rearrange("p h (k m) -> p (h k) m", k=TOPK), AX.X, ALU.add)
                        dve.drain()
                    dve.wait_ge(exp_ready, l * NT + t + 1)
                    reduce(pm[:, 0:8], pw[:, :, :], AX.X, ALU.add)
                    dve.drain()
                    nc.vector.reciprocal(pm[:, 8:16], pm[:, 0:8])
                    dve.drain()
                    tt(idx[:, 2, :].rearrange("p (h k) -> p h k", h=8), pw[:, :, :],
                       pm[:, 8:16].unsqueeze(2).broadcast_to([P, 8, TOPK]), ALU.mult).then_inc(idx_ready, 1)
                    dve.wait_ge(idxT_ready, l * NT + t + 1)

                    def onehots(i, u):
                        for n, oh in enumerate((ohA[:, u, :, :], ohE[:, u % 2, :, :])):
                            key = idxT[:, n, bass.ds(i * 16 + 4 * u, 4)].unsqueeze(2).broadcast_to([P, 4, P])
                            last = tt(oh, iota.unsqueeze(1).broadcast_to([P, 4, P]), key, ALU.is_equal)
                        last.then_inc(eq_ready, 1)

                    for u in range(4):
                        if u >= 2:
                            dve.wait_ge(oh_ready, l * N_QUAD + t * QUADS + (u - 1))
                        onehots(0, u)
                    with dve.Fori(1, P // 16) as i:
                        for u in range(4):
                            dve.wait_ge(quad_ready, l * N_QUAD + t * QUADS + i * 4 + (u - 3))
                            dve.wait_ge(oh_ready, l * N_QUAD + t * QUADS + i * 4 + (u - 1))
                            onehots(i, u)
                dve.wait_ge(quad_ready, layer_at(l, N_QUAD, N_QUAD))

                dve.wait_ge(hhi_ready, l + 1)
                nc.vector.memset(acc[:, :, :], 0.0)
                dve.drain()
                tt(hT_lo[:, :, :], hT[:, :, :], hT_hi[:, :, :].bitcast(F32), ALU.subtract).then_inc(hlo_ready, 1)

                def split_lo(s, n):
                    dve.wait_ge(hi_ready, l * N_SPLIT + n + 1)
                    tt(ring_lo[:, s, :], ring[:, s, :], ring_hi[:, s, :].bitcast(F32), ALU.subtract).then_inc(split_ready, 1)

                def weigh(b, j, u, gcount):
                    if j == 0:
                        dve.wait_ge(g_loaded[u], 16 * (l * (NB // 2) + gcount + 1))
                    dve.wait_ge(gelu_ready, l * (2 * NB) + b * 2 + (j + 1))
                    tt(wtmp[:, :].rearrange("p (g t) -> p g t", t=64),
                       act_g[:, j, :].rearrange("p (g t) -> p g t", t=64), G[:, u, :, j, :], ALU.mult)
                    dve.drain()
                    copy(W_hi[:, u, j, :], wtmp[:, :])
                    dve.drain()
                    tt(W_lo[:, u, j, :], wtmp[:, :], W_hi[:, u, j, :].bitcast(F32), ALU.subtract).then_inc(W_ready, 1)
                    dve.drain()

                def add_up(b, n0, n1, par):
                    for n in range(n0, n1):
                        t, dh = n // 2, n % 2
                        dve.wait_ge(v_full, l * N_V + b * 10 + (n + 1))
                        a = acc[:, t, 512 * dh:512 * dh + 512]
                        tt(a, a, bank(4 + (10 * par + n) % 4), ALU.add).then_inc(v_done, 1)

                for n in range(3):
                    split_lo(n, n)
                weigh(0, 0, 0, 0)
                weigh(0, 1, 0, 0)
                with dve.Fori(0, NB // 2 - 1) as i:
                    for u in range(2):
                        v = 1 - u
                        gc = i + u
                        weigh(i * 2 + (u + 1), 0, v, gc)
                        split_lo((3 + 2 * u) % RING, i * 4 + (3 + 2 * u))
                        weigh(i * 2 + (u + 1), 1, v, gc)
                        add_up(i * 2 + u, 0, 5, u)
                        split_lo((4 + 2 * u) % RING, i * 4 + (4 + 2 * u))
                        add_up(i * 2 + u, 5, 10, u)
                weigh(NB - 1, 0, 1, NB // 2 - 1)
                split_lo(3, 2 * NB - 1)
                weigh(NB - 1, 1, 1, NB // 2 - 1)
                add_up(NB - 2, 0, 10, 0)
                nc.vector.memset(lamw[:, 10:11], 0.0).then_inc(ring_free, 1)
                for t in range(NT):
                    add_up(NB - 1, 2 * t, 2 * t + 2, 1)
                    dve.drain()
                    if t == NT - 1:
                        nc.vector.memset(lamw[:, 10:11], 0.0).then_inc(ring_free, 1)
                    tt(acc[:, t, :], acc[:, t, :], gate2[:, 0 if t == 0 else 1, :], ALU.mult)
                    dve.drain()
                    stt(x[:, t, :], x[:, t, :], ALPHA, acc[:, t, :], ALU.mult, ALU.add)
                    dve.drain()
                    for h in range(2):
                        nc.vector.bn_stats(stats[:, t, h, :], x[:, t, 512 * h:512 * h + 512])
                aggregate()
                inverse_root(6)
                dve.wait_ge(ln2_rows, 16 * (l + 1))
                post_norm(x, lnr2, range(NT)).then_inc(layer_done, 1)
                dve.drain()
                copy(lamw[:, 8:10], const[:, 0:2]).then_inc(layer_free, 1)


def constants(np):
    f = np.float64
    n = np.arange(P)
    ang = 2 * np.pi * ((n[:, None] * n[None, :]) % P) / P
    cos, sin = np.cos(ang) / np.sqrt(f(P)), np.sin(ang) / np.sqrt(f(P))
    tok = np.arange(4 * P)
    freq = np.float32(10000.0) ** (-np.arange(16, dtype=np.float32) / np.float32(16))
    pos = np.concatenate([(tok // 64)[:, None] * freq, (tok % 64)[:, None] * freq], -1).astype(np.float32)
    rc = np.cos(pos.astype(f)).reshape(4, P, 32).transpose(1, 0, 2).reshape(P, P)
    rs = np.sin(pos.astype(f)).reshape(4, P, 32).transpose(1, 0, 2).reshape(P, P)
    lam = []
    for layer in range(LAYERS):
        init = 0.8 - 0.6 * np.exp(-0.3 * layer)
        lam += [init, 1.0 - init]
    parts = [np.eye(P), np.tile(n, (P, 1)), cos, sin, -sin, rc, rs, np.ones((P, P)), np.tile(lam, (P, 1))]
    table = np.concatenate(parts, 1).astype(np.float32)
    assert table.shape[1] == NCONST
    m = np.arange(4 * P)
    ang = 2 * np.pi * ((m[:, None] * m[None, :]) % (4 * P)) / (4 * P)
    dft = [(g(ang) / np.sqrt(f(4 * P))).astype(np.float32).reshape(4, P, 4 * P).transpose(1, 0, 2).reshape(P, SLOT)
           for g in (np.cos, np.sin)]
    return table, dft


def weight_stream(np, w_mod, w_in, w_branch, w_out, peer_wq, peer_subkeys, peer_u, peer_v, dft):
    out = np.zeros((LAYERS, PER_LAYER, P, SLOT), np.float32)

    def columns(w, c0, width=256):
        return w[:, c0:c0 + width].reshape(-1, P, width).transpose(1, 0, 2).reshape(P, -1)

    for l in range(LAYERS):
        s = out[l]
        for k in range(24):
            s[MOD1 + k if k < 8 else MOD2 + k - 8] = columns(w_mod[l], 256 * k)
        starts = [1536, 1792, 2048, 0, 256, 512, 768, 1024, 1280, 2304, 2560]
        for k, c0 in enumerate(starts):
            s[GQ + k] = columns(w_in[l], c0)
        s[DFT], s[DFT + 1] = dft
        for n in range(3):
            for half in range(2):
                slot = MERGE + 6 * n + 3 * half
                s[slot + 1] = columns(w_branch[l, n], 512 * half, 512)
                for g in range(2):
                    s[slot + 2 * g] = columns(w_in[l], 2816 + n * D + 512 * half + 256 * g)
        for k in range(4):
            s[OUT + k] = columns(w_out[l], 256 * k)
            s[WQA + k] = s[WQB + k] = columns(peer_wq[l], 256 * k)
        s[SUB, :, 0:1024] = peer_subkeys[l].transpose(1, 3, 0, 2).reshape(P, 1024)
        u = peer_u[l].reshape(P, NB, 2, KC, P).transpose(1, 4, 3, 2, 0).reshape(NB, P, SLOT)
        v = peer_v[l].reshape(P, NB, 2, D).transpose(1, 0, 2, 3).reshape(NB, P, SLOT)
        s[PEER] = u[0]
        s[PEER + 1:PER_LAYER - 1:2] = u[1:]
        s[PEER + 2:PER_LAYER:2] = v[:-1]
        s[PER_LAYER - 1] = v[-1]
    return out.reshape(LAYERS * PER_LAYER, P, SLOT)


def build(nc):
    def dram(name, shape, kind):
        return nc.dram_tensor(name, shape, F32, kind=kind).ap()

    ins = {n: dram(n, s, "ExternalInput") for n, s in (
        ("weights", (LAYERS * PER_LAYER, P, SLOT)), ("consts", (P, NCONST)), ("x_in", (NT, P, D)),
        ("cond", (P, 2 * KC)), ("bcol", (LAYERS, P, 48)), ("rows", (LAYERS, 512)),
        ("lnrows", (LAYERS * 2, 2, D)), ("cache_k", (LAYERS, P, 640)), ("cache_v", (LAYERS, P, 640)))}
    outs = {n: dram(n, s, "ExternalOutput") for n, s in (
        ("y", (NT, P, D)), ("new_dk", (LAYERS, P, 512)), ("new_dv", (LAYERS, P, 512)),
        ("new_gk", (LAYERS, P, P)), ("new_gv", (LAYERS, P, P)))}
    gate_matrix = dram("gate_matrix", (NB, P, 2 * T), "Internal")
    x_wait = dram("x_wait", (LAYERS, NT, P, D), "Internal")
    trunk(nc, **ins, **outs, gate_matrix=gate_matrix, x_wait=x_wait)


def layouts(np, i):
    c = np.ascontiguousarray
    table, dft = constants(np)
    rows = np.concatenate([i["diff_lam"].reshape(LAYERS, 256), i["q_norm_g"], i["k_norm_g"], i["diff_norm_g"]], 1)
    b = i["b_mod"]
    return {
        "weights": weight_stream(np, i["w_mod"], i["w_in"], i["w_branch"], i["w_out"], i["peer_wq"],
                                 i["peer_subkeys"], i["peer_u"], i["peer_v"], dft),
        "consts": table,
        "x_in": np.concatenate([i["x_prompt"].reshape(1, P, D), i["x_sample"].reshape(4, P, D)], 0),
        "cond": c(np.stack([i["c_ctx"], i["c"][0]], -1).reshape(KC, P, 2).transpose(1, 0, 2).reshape(P, 2 * KC)),
        "bcol": c(b.reshape(LAYERS, 48, P).transpose(0, 2, 1)),
        "rows": rows,
        "lnrows": c(np.stack([i["ln_g"], i["ln_b"]], 2).reshape(LAYERS * 2, 2, D)),
        "cache_k": np.concatenate([i["cache_diff_k"][0].reshape(LAYERS, P, 512),
                                   i["cache_gqa_k"][0].reshape(LAYERS, P, P)], -1),
        "cache_v": np.concatenate([i["cache_diff_v"][0].reshape(LAYERS, P, 512),
                                   i["cache_gqa_v"][0].reshape(LAYERS, P, P)], -1),
    }


def kernel(**inputs):
    import numpy as np
    import concourse.bacc as bacc
    from concourse.bass_utils import run_bass_kernel_spmd

    arrays = layouts(np, {k: np.asarray(v) for k, v in inputs.items()})
    nc = bacc.Bacc("TRN2", target_bir_lowering=False, num_devices=1)
    build(nc)
    r = run_bass_kernel_spmd(nc, [arrays], core_ids=[0]).results[0]
    y = r["y"]
    return (y[0:1], y[1:].reshape(1, 512, D),
            r["new_dk"].reshape(1, LAYERS, P, 4, P), r["new_dv"].reshape(1, LAYERS, P, 4, P),
            r["new_gk"].reshape(1, LAYERS, P, 2, 64), r["new_gv"].reshape(1, LAYERS, P, 2, 64))
```
